# Optimizing a Trainium2 kernel written in Bass

```python
import jax, jax.numpy as jnp
from jax import lax
import numpy as np

D_MODEL = 1024
BATCH = 1
SEQ = 512
DEPTH = 2

HEAD_DIM = 64
N_GROUP_HEADS = 4
GROUP_WIDTH = N_GROUP_HEADS * HEAD_DIM
MIX_WIDTH = 4 * GROUP_WIDTH
MLA_Q_RANK = 256
MLA_KV_RANK = 128
MLA_NOPE = 64
MLA_ROPE = 32
MLA_V = 64
SWA_KV_HEADS = 2
SWA_WINDOW = 128
IDX_HEADS = 8
IDX_DIM = 32
DSA_TOPK = 256
FOX_HEADS = 4
D_FF = 4 * D_MODEL
ROPE_THETA = 10000.0
Q_BLOCK = 128
EPS = 1e-6

IN_SPLITS = (
    MLA_Q_RANK, MLA_KV_RANK, MLA_ROPE,
    GROUP_WIDTH, SWA_KV_HEADS * HEAD_DIM, SWA_KV_HEADS * HEAD_DIM,
    GROUP_WIDTH, GROUP_WIDTH, GROUP_WIDTH, IDX_HEADS * IDX_DIM, IDX_DIM, IDX_HEADS,
    GROUP_WIDTH, GROUP_WIDTH, GROUP_WIDTH, FOX_HEADS,
)
IN_WIDTH = sum(IN_SPLITS)


def rms_norm(x, g):
    xf = x.astype(jnp.float32)
    y = xf * lax.rsqrt(jnp.mean(xf * xf, axis=-1, keepdims=True) + EPS)
    return (y * g.astype(jnp.float32)).astype(x.dtype)

def rope(x, pos):
    d = x.shape[-1]
    half = d // 2
    inv_freq = 1.0 / (ROPE_THETA ** (jnp.arange(0, half, dtype=jnp.float32) * 2.0 / d))
    ang = pos[:, None] * inv_freq[None, :]
    cos = jnp.cos(ang)[:, None, :]
    sin = jnp.sin(ang)[:, None, :]
    xf = x.astype(jnp.float32)
    x1, x2 = xf[..., :half], xf[..., half:]
    out = jnp.concatenate([x1 * cos - x2 * sin, x2 * cos + x1 * sin], axis=-1)
    return out.astype(x.dtype)

def split_cols(proj):
    offs, acc = [], 0
    for n in IN_SPLITS[:-1]:
        acc += n
        offs.append(acc)
    return jnp.split(proj, offs, axis=-1)

def causal_block_attention(q, k, v, scale, log_f_cum=None):
    B, S, H, dk = q.shape
    dv = v.shape[-1]
    nb = S // Q_BLOCK
    q_blocks = q.reshape(B, nb, Q_BLOCK, H, dk).swapaxes(0, 1)
    starts = jnp.arange(nb, dtype=jnp.int32) * Q_BLOCK
    key_pos = jnp.arange(S, dtype=jnp.int32)
    if log_f_cum is None:
        xs = (q_blocks, starts)
    else:
        cum_blocks = log_f_cum.reshape(B, nb, Q_BLOCK, H).swapaxes(0, 1)
        cum_keys = log_f_cum.transpose(0, 2, 1)[:, :, None, :]
        xs = (q_blocks, starts, cum_blocks)

    def block(args):
        q_blk, start = args[0], args[1]
        s = jnp.einsum('bqhd,bkhd->bhqk', q_blk, k).astype(jnp.float32) * scale
        if log_f_cum is not None:
            s = s + (args[2].transpose(0, 2, 1)[..., None] - cum_keys)
        qpos = start + jnp.arange(Q_BLOCK, dtype=jnp.int32)
        causal = key_pos[None, :] <= qpos[:, None]
        s = jnp.where(causal, s, -jnp.inf)
        p = jax.nn.softmax(s, axis=-1).astype(v.dtype)
        return jnp.einsum('bhqk,bkhd->bqhd', p, v)

    out = lax.map(block, xs)
    return out.swapaxes(0, 1).reshape(B, S, H, dv)

def sliding_window_attention(q, k, v, sinks, scale):
    B, S, H, d = q.shape
    Hk = k.shape[2]
    G = H // Hk
    W = SWA_WINDOW
    nb = S // W
    qb = q.reshape(B, nb, W, Hk, G, d)

    def with_prev(t):
        tb = t.reshape(B, nb, W, Hk, d)
        prev = jnp.concatenate([jnp.zeros_like(tb[:, :1]), tb[:, :-1]], axis=1)
        return jnp.concatenate([prev, tb], axis=2)

    kb, vb = with_prev(k), with_prev(v)
    s = jnp.einsum('bnqkgd,bnjkd->bnkgqj', qb, kb).astype(jnp.float32) * scale
    blk = jnp.arange(nb, dtype=jnp.int32)[:, None, None]
    qi = jnp.arange(W, dtype=jnp.int32)[None, :, None]
    kj = jnp.arange(2 * W, dtype=jnp.int32)[None, None, :]
    qpos = blk * W + qi
    kpos = blk * W - W + kj
    mask = (kpos >= 0) & (kpos <= qpos) & (qpos - kpos < SWA_WINDOW)
    s = jnp.where(mask[None, :, None, None], s, -jnp.inf)
    sink = jnp.broadcast_to(sinks.astype(jnp.float32).reshape(1, 1, Hk, G, 1, 1),
                            s.shape[:-1] + (1,))
    p = jax.nn.softmax(jnp.concatenate([s, sink], axis=-1), axis=-1)[..., :-1]
    o = jnp.einsum('bnkgqj,bnjkd->bnqkgd', p.astype(v.dtype), vb)
    return o.reshape(B, S, H, d)

def dsa_attention(q, k, v, q_idx, k_idx, w_idx, top_k, scale):
    B, S, H, d = q.shape
    nb = S // Q_BLOCK

    def blocks(t):
        return t.reshape((B, nb, Q_BLOCK) + t.shape[2:]).swapaxes(0, 1)

    starts = jnp.arange(nb, dtype=jnp.int32) * Q_BLOCK
    key_pos = jnp.arange(S, dtype=jnp.int32)

    def block(args):
        q_blk, qi_blk, w_blk, start = args
        qpos = start + jnp.arange(Q_BLOCK, dtype=jnp.int32)
        rel = jax.nn.relu(jnp.einsum('bqhd,bkd->bqhk', qi_blk, k_idx).astype(jnp.float32))
        score = jnp.einsum('bqhk,bqh->bqk', rel, w_blk.astype(jnp.float32))
        score = jnp.where(key_pos[None, None, :] <= qpos[None, :, None], score, -jnp.inf)
        _, idx = lax.top_k(score, top_k)
        k_sel = jax.vmap(lambda kb, ib: kb[ib])(k, idx)
        v_sel = jax.vmap(lambda vb, ib: vb[ib])(v, idx)
        s = jnp.einsum('bqhd,bqkhd->bqhk', q_blk, k_sel).astype(jnp.float32) * scale
        valid = (idx <= qpos[None, :, None])[:, :, None, :]
        s = jnp.where(valid, s, -jnp.inf)
        p = jax.nn.softmax(s, axis=-1).astype(v.dtype)
        return jnp.einsum('bqhk,bqkhd->bqhd', p, v_sel)

    out = lax.map(block, (blocks(q), blocks(q_idx), blocks(w_idx), starts))
    return out.swapaxes(0, 1).reshape(B, S, H, d)

def first_inputs(seed: int = 0) -> dict:
    key = jax.random.key(seed)
    ks = jax.random.split(key, 16)
    H = N_GROUP_HEADS
    f32 = jnp.float32

    def nrm(k, shape, fan_in):
        return jax.random.normal(k, shape, f32) * (fan_in ** -0.5)

    def gain(k, shape):
        return 1.0 + 0.05 * jax.random.normal(k, shape, f32)

    return {
        "x": jax.random.normal(ks[0], (BATCH, SEQ, D_MODEL), f32),
        "norm1": gain(ks[1], (DEPTH, D_MODEL)),
        "w_in": nrm(ks[2], (DEPTH, D_MODEL, IN_WIDTH), D_MODEL),
        "mla_q_norm": gain(ks[3], (DEPTH, MLA_Q_RANK)),
        "mla_kv_norm": gain(ks[4], (DEPTH, MLA_KV_RANK)),
        "mla_w_uq": nrm(ks[5], (DEPTH, MLA_Q_RANK, H * (MLA_NOPE + MLA_ROPE)), MLA_Q_RANK),
        "mla_w_ukv": nrm(ks[6], (DEPTH, MLA_KV_RANK, H * (MLA_NOPE + MLA_V)), MLA_KV_RANK),
        "swa_sinks": 0.5 * jax.random.normal(ks[7], (DEPTH, H), f32),
        "fox_b_f": 0.1 * jax.random.normal(ks[8], (DEPTH, FOX_HEADS), f32),
        "w_out": nrm(ks[9], (DEPTH, MIX_WIDTH, D_MODEL), MIX_WIDTH),
        "norm2": gain(ks[10], (DEPTH, D_MODEL)),
        "w_up": nrm(ks[11], (DEPTH, D_MODEL, D_FF), D_MODEL),
        "w_down": nrm(ks[12], (DEPTH, D_FF, D_MODEL), D_FF),
        "final_norm": gain(ks[13], (D_MODEL,)),
    }

def first_block(x, norm1, w_in, mla_q_norm, mla_kv_norm, mla_w_uq, mla_w_ukv, swa_sinks,
              fox_b_f, w_out, norm2, w_up, w_down, final_norm):
    B, S, _ = x.shape
    H = N_GROUP_HEADS
    Dh = HEAD_DIM
    pos = jnp.arange(S, dtype=jnp.float32)
    top_k = min(DSA_TOPK, S // 4)
    for l in range(DEPTH):
        h = rms_norm(x, norm1[l])
        proj = h @ w_in[l]
        (a_cq, a_ckv, a_kr, b_q, b_k, b_v, c_q, c_k, c_v, c_qi, c_ki, c_w,
         d_q, d_k, d_v, d_f) = split_cols(proj)

        qa = (rms_norm(a_cq, mla_q_norm[l]) @ mla_w_uq[l]).reshape(B, S, H, MLA_NOPE + MLA_ROPE)
        q_a = jnp.concatenate([qa[..., :MLA_NOPE], rope(qa[..., MLA_NOPE:], pos)], axis=-1)
        kv = (rms_norm(a_ckv, mla_kv_norm[l]) @ mla_w_ukv[l]).reshape(B, S, H, MLA_NOPE + MLA_V)
        k_rope = rope(a_kr.reshape(B, S, 1, MLA_ROPE), pos)
        k_a = jnp.concatenate([kv[..., :MLA_NOPE],
                               jnp.broadcast_to(k_rope, (B, S, H, MLA_ROPE))], axis=-1)
        o_a = causal_block_attention(q_a, k_a, kv[..., MLA_NOPE:],
                                     (MLA_NOPE + MLA_ROPE) ** -0.5)

        q_b = rope(b_q.reshape(B, S, H, Dh), pos)
        k_b = rope(b_k.reshape(B, S, SWA_KV_HEADS, Dh), pos)
        v_b = b_v.reshape(B, S, SWA_KV_HEADS, Dh)
        o_b = sliding_window_attention(q_b, k_b, v_b, swa_sinks[l], Dh ** -0.5)

        q_c = rope(c_q.reshape(B, S, H, Dh), pos)
        k_c = rope(c_k.reshape(B, S, H, Dh), pos)
        v_c = c_v.reshape(B, S, H, Dh)
        qi = rope(c_qi.reshape(B, S, IDX_HEADS, IDX_DIM), pos)
        ki = rope(c_ki.reshape(B, S, 1, IDX_DIM), pos)[:, :, 0, :]
        o_c = dsa_attention(q_c, k_c, v_c, qi, ki, c_w, top_k, Dh ** -0.5)

        log_f = jax.nn.log_sigmoid((d_f + fox_b_f[l]).astype(jnp.float32))
        cum = lax.cumsum(log_f, axis=1)
        o_d = causal_block_attention(d_q.reshape(B, S, FOX_HEADS, Dh),
                                     d_k.reshape(B, S, FOX_HEADS, Dh),
                                     d_v.reshape(B, S, FOX_HEADS, Dh),
                                     Dh ** -0.5, log_f_cum=cum)

        mixed = jnp.concatenate([o_a.reshape(B, S, GROUP_WIDTH), o_b.reshape(B, S, GROUP_WIDTH),
                                 o_c.reshape(B, S, GROUP_WIDTH), o_d.reshape(B, S, GROUP_WIDTH)],
                                axis=-1)
        x = x + mixed @ w_out[l]

        h2 = rms_norm(x, norm2[l])
        x = x + jnp.square(jax.nn.relu(h2 @ w_up[l])) @ w_down[l]
    return rms_norm(x, final_norm)


DEPTH_2 = 1

DN_HEADS = 8
DN_DK = 128
DN_DV = 128
DN_QK_WIDTH = DN_HEADS * DN_DK
DN_WIDTH = DN_HEADS * DN_DV
CONV_K = 4
CHUNK = 64
DIL_CONFIGS = ((128, 1), (512, 4), (2048, 16))
HEADS_PER_GROUP = 4
ATTN_HEADS = HEADS_PER_GROUP * len(DIL_CONFIGS)
ATTN_HEAD_DIM = 64
ATTN_WIDTH = ATTN_HEADS * ATTN_HEAD_DIM
ATTN_BLOCK = 128
IN_SPLITS_2 = (DN_QK_WIDTH, DN_QK_WIDTH, DN_WIDTH, DN_WIDTH, DN_HEADS, DN_HEADS,
             ATTN_WIDTH, ATTN_WIDTH, ATTN_WIDTH, ATTN_WIDTH, D_MODEL, D_MODEL)
N_IN = sum(IN_SPLITS_2)


def rms_norm_2(x, w):
    xf = x.astype(jnp.float32)
    y = xf * lax.rsqrt(jnp.mean(xf * xf, axis=-1, keepdims=True) + EPS)
    return (y * w.astype(jnp.float32)).astype(x.dtype)

def l2_normalize(x):
    xf = x.astype(jnp.float32)
    return xf * lax.rsqrt(jnp.sum(xf * xf, axis=-1, keepdims=True) + EPS)

def causal_dwconv_silu(x, w):
    k_w = w.shape[0]
    s = x.shape[1]
    xp = jnp.pad(x, ((0, 0), (k_w - 1, 0), (0, 0)))
    y = sum(xp[:, j:j + s] * w[j] for j in range(k_w))
    return jax.nn.silu(y)

def gated_delta_rule(q, k, v, g, beta):
    b, s, h, dk = q.shape
    n = s // CHUNK

    def to_chunks(t):
        return jnp.moveaxis(t.reshape((b, n, CHUNK) + t.shape[2:]), 3, 2)

    q, k, v, g, beta = map(to_chunks, (q * dk ** -0.5, k, v, g, beta))
    gc = jnp.cumsum(g, axis=-1)
    causal = jnp.tril(jnp.ones((CHUNK, CHUNK), dtype=bool))
    strict = jnp.tril(jnp.ones((CHUNK, CHUNK), dtype=bool), -1)
    decay = jnp.exp(jnp.where(causal, gc[..., :, None] - gc[..., None, :], -jnp.inf))
    k_beta = k * beta[..., None]
    v_beta = v * beta[..., None]
    lmat = jnp.where(strict, jnp.einsum('bnhcd,bnhed->bnhce', k_beta, k) * decay, 0.0)
    eye = jnp.eye(CHUNK, dtype=jnp.float32)
    t_inv = lax.linalg.triangular_solve(eye + lmat, jnp.broadcast_to(eye, lmat.shape),
                                        left_side=True, lower=True, unit_diagonal=True)
    u = jnp.einsum('bnhce,bnhed->bnhcd', t_inv, v_beta)
    w = jnp.einsum('bnhce,bnhed->bnhcd', t_inv, k_beta * jnp.exp(gc)[..., None])
    a_qk = jnp.einsum('bnhcd,bnhed->bnhce', q, k) * decay
    q_dec = q * jnp.exp(gc)[..., None]
    k_dec = k * jnp.exp(gc[..., -1:] - gc)[..., None]
    g_last = jnp.exp(gc[..., -1])

    def step(state, xs):
        q_c, k_c, u_c, w_c, a_c, gl = xs
        v_new = u_c - jnp.einsum('bhcd,bhde->bhce', w_c, state)
        o_c = jnp.einsum('bhcd,bhde->bhce', q_c, state) + jnp.einsum('bhce,bhed->bhcd', a_c, v_new)
        state = state * gl[..., None, None] + jnp.einsum('bhcd,bhce->bhde', k_c, v_new)
        return state, o_c

    xs = tuple(jnp.moveaxis(t, 1, 0) for t in (q_dec, k_dec, u, w, a_qk, g_last))
    state0 = jnp.zeros((b, h, dk, v.shape[-1]), jnp.float32)
    _, o = lax.scan(step, state0, xs)
    o = jnp.moveaxis(jnp.moveaxis(o, 0, 1), 2, 3)
    return o.reshape(b, s, h, -1)

def dilated_window_attention(q, k, v, window, dilation):
    b, s, h, dh = q.shape
    n_back = window // dilation
    sub_len = s // dilation
    nb = -(-sub_len // ATTN_BLOCK)
    lp = nb * ATTN_BLOCK
    bb = b * dilation

    def to_sub(t):
        t = t.reshape(b, sub_len, dilation, h, dh).transpose(0, 2, 1, 3, 4).reshape(bb, sub_len, h, dh)
        return jnp.pad(t, ((0, 0), (0, lp - sub_len), (0, 0), (0, 0)))

    def band(t):
        tp = jnp.pad(t, ((0, 0), (ATTN_BLOCK, 0), (0, 0), (0, 0))).reshape(bb, nb + 1, ATTN_BLOCK, h, dh)
        return jnp.concatenate([tp[:, :-1], tp[:, 1:]], axis=2)

    qb = to_sub(q).reshape(bb, nb, ATTN_BLOCK, h, dh)
    kb = band(to_sub(k))
    vb = band(to_sub(v))
    scores = jnp.einsum('bnqhd,bnkhd->bnhqk', qb, kb,
                        preferred_element_type=jnp.float32) * (dh ** -0.5)
    blk = jnp.arange(nb)[:, None, None]
    qpos = blk * ATTN_BLOCK + jnp.arange(ATTN_BLOCK)[None, :, None]
    kpos = (blk - 1) * ATTN_BLOCK + jnp.arange(2 * ATTN_BLOCK)[None, None, :]
    dist = qpos - kpos
    mask = (dist >= 0) & (dist <= n_back) & (kpos >= 0)
    scores = jnp.where(mask[None, :, None], scores, -jnp.inf)
    m = jnp.max(scores, axis=-1, keepdims=True)
    p = jnp.exp(scores - m)
    denom = jnp.sum(p, axis=-1, keepdims=True)
    o = jnp.einsum('bnhqk,bnkhd->bnqhd', (p / denom).astype(v.dtype), vb)
    lse = (m + jnp.log(denom))[..., 0]
    o = o.reshape(bb, lp, h, dh)[:, :sub_len]
    o = o.reshape(b, dilation, sub_len, h, dh).transpose(0, 2, 1, 3, 4).reshape(b, s, h, dh)
    lse = lse.transpose(0, 1, 3, 2).reshape(bb, lp, h)[:, :sub_len]
    lse = lse.reshape(b, dilation, sub_len, h).transpose(0, 2, 1, 3).reshape(b, s, h)
    return o, lse

def second_inputs(seed: int = 0) -> dict:
    key = jax.random.key(seed)
    ks = jax.random.split(key, 16)
    f32 = jnp.float32
    d = D_MODEL
    x = jax.random.normal(ks[0], (BATCH, SEQ, d), f32)
    c = jax.random.normal(ks[1], (BATCH, d), f32)
    norm_w = 1.0 + 0.02 * jax.random.normal(ks[2], (DEPTH_2, d), f32)
    ada_w = jax.random.normal(ks[3], (DEPTH_2, d, 3 * d), f32) * d ** -0.5
    ada_b = 0.01 * jax.random.normal(ks[4], (DEPTH_2, 3 * d), f32)
    w_in = jax.random.normal(ks[5], (DEPTH_2, d, N_IN), f32) * d ** -0.5
    conv_w = jax.random.normal(ks[6], (DEPTH_2, CONV_K, 2 * DN_QK_WIDTH + DN_WIDTH), f32) * CONV_K ** -0.5
    a_log = jnp.log(jax.random.uniform(ks[7], (DEPTH_2, DN_HEADS), f32, 1.0, 16.0))
    dt = jnp.exp(jax.random.uniform(ks[8], (DEPTH_2, DN_HEADS), f32, np.log(1e-3), np.log(1e-1)))
    dt_bias = dt + jnp.log(-jnp.expm1(-dt))
    dn_norm_w = 1.0 + 0.02 * jax.random.normal(ks[9], (DEPTH_2, DN_DV), f32)
    w_proj_a = jax.random.normal(ks[10], (DEPTH_2, DN_WIDTH, d), f32) * DN_WIDTH ** -0.5
    w_proj_b = jax.random.normal(ks[11], (DEPTH_2, ATTN_WIDTH, d), f32) * ATTN_WIDTH ** -0.5
    w_out = jax.random.normal(ks[12], (DEPTH_2, d, d), f32) * d ** -0.5
    final_norm_w = 1.0 + 0.02 * jax.random.normal(ks[13], (d,), f32)
    return {"x": x, "c": c, "norm_w": norm_w, "ada_w": ada_w, "ada_b": ada_b, "w_in": w_in,
            "conv_w": conv_w, "a_log": a_log, "dt_bias": dt_bias, "dn_norm_w": dn_norm_w,
            "w_proj_a": w_proj_a, "w_proj_b": w_proj_b, "w_out": w_out, "final_norm_w": final_norm_w}

def second_block(x, c, norm_w, ada_w, ada_b, w_in, conv_w, a_log, dt_bias, dn_norm_w,
              w_proj_a, w_proj_b, w_out, final_norm_w):
    b, s, _ = x.shape
    split_points = [int(p) for p in np.cumsum(IN_SPLITS_2)[:-1]]
    for l in range(DEPTH_2):
        mod = jax.nn.silu(c) @ ada_w[l] + ada_b[l]
        shift, scale, gate = jnp.split(mod, 3, axis=-1)
        h = rms_norm_2(x, norm_w[l]) * (1.0 + scale[:, None]) + shift[:, None]
        proj = h @ w_in[l]
        (qa, ka, va, za, beta_in, a_in, qb, kb, vb, zb, ga, gb) = jnp.split(proj, split_points, axis=-1)

        qkv = causal_dwconv_silu(jnp.concatenate([qa, ka, va], axis=-1), conv_w[l])
        qa, ka, va = jnp.split(qkv, [DN_QK_WIDTH, 2 * DN_QK_WIDTH], axis=-1)
        q_dn = l2_normalize(qa.reshape(b, s, DN_HEADS, DN_DK))
        k_dn = l2_normalize(ka.reshape(b, s, DN_HEADS, DN_DK))
        v_dn = va.reshape(b, s, DN_HEADS, DN_DV).astype(jnp.float32)
        beta = jax.nn.sigmoid(beta_in.astype(jnp.float32))
        g = -jnp.exp(a_log[l].astype(jnp.float32)) * jax.nn.softplus(
            a_in.astype(jnp.float32) + dt_bias[l].astype(jnp.float32))
        o_a = gated_delta_rule(q_dn, k_dn, v_dn, g, beta).astype(x.dtype)
        y_a = rms_norm_2(o_a, dn_norm_w[l]).reshape(b, s, DN_WIDTH) * jax.nn.silu(za)
        y_a = y_a @ w_proj_a[l]

        qb = qb.reshape(b, s, ATTN_HEADS, ATTN_HEAD_DIM)
        kb = kb.reshape(b, s, ATTN_HEADS, ATTN_HEAD_DIM)
        vb = vb.reshape(b, s, ATTN_HEADS, ATTN_HEAD_DIM)
        outs, lses = [], []
        for gi, (win, dil) in enumerate(DIL_CONFIGS):
            hs = slice(gi * HEADS_PER_GROUP, (gi + 1) * HEADS_PER_GROUP)
            o_g, lse_g = dilated_window_attention(qb[:, :, hs], kb[:, :, hs], vb[:, :, hs], win, dil)
            outs.append(o_g)
            lses.append(lse_g)
        o_b = jnp.stack(outs, axis=2)
        w_g = jax.nn.softmax(jnp.stack(lses, axis=2), axis=2)
        y_b = (o_b * w_g[..., None].astype(o_b.dtype)).reshape(b, s, ATTN_WIDTH) * jax.nn.silu(zb)
        y_b = y_b @ w_proj_b[l]

        merged = jax.nn.sigmoid(ga) * y_a + jax.nn.sigmoid(gb) * y_b
        x = x + gate[:, None] * (merged @ w_out[l])
    return rms_norm_2(x, final_norm_w)


def setup_inputs(seed=0):
    out = dict(first_inputs(seed))
    for name, value in second_inputs(seed + 1).items():
        if name != "x":
            out[name + "_2"] = value
    return out


def reference(
    x, norm1, w_in, mla_q_norm, mla_kv_norm, mla_w_uq, mla_w_ukv, swa_sinks, fox_b_f, w_out,
    norm2, w_up, w_down, final_norm, c_2, norm_w_2, ada_w_2, ada_b_2, w_in_2, conv_w_2, a_log_2,
    dt_bias_2, dn_norm_w_2, w_proj_a_2, w_proj_b_2, w_out_2, final_norm_w_2,
):
    x = first_block(
        x, norm1, w_in, mla_q_norm, mla_kv_norm, mla_w_uq, mla_w_ukv, swa_sinks, fox_b_f, w_out,
        norm2, w_up, w_down, final_norm,
    )
    return second_block(
        x, c_2, norm_w_2, ada_w_2, ada_b_2, w_in_2, conv_w_2, a_log_2, dt_bias_2, dn_norm_w_2,
        w_proj_a_2, w_proj_b_2, w_out_2, final_norm_w_2,
    )


_drawn_inputs = setup_inputs


def setup_inputs(seed=0):
    import zlib

    import numpy as np

    out = dict(_drawn_inputs(seed))
    spreads = {}
    factors = {'mla_q_norm': 8.0,
     'mla_kv_norm': 5.834,
     'swa_sinks': 8.0,
     'fox_b_f': 2.816,
     'norm_w_2': 6.739,
     'ada_b_2': 7.878,
     'a_log_2': 2.984,
     'dn_norm_w_2': 8.0,
     'final_norm_w_2': 2.79}
    for name, (base, spread) in spreads.items():
        noise = np.random.default_rng([zlib.crc32(name.encode()), seed]).standard_normal(out[name].shape)
        drawn = base * np.exp(spread * noise) if base else spread * noise
        out[name] = __import__('jax').numpy.asarray(drawn.astype(out[name].dtype))
    for name, factor in factors.items():
        out[name] = (out[name] * factor).astype(out[name].dtype)
    return out
```

```python
from contextlib import ExitStack, contextmanager

import numpy as np

import concourse.bass as bass
from concourse import mybir

F32 = mybir.dt.float32
ACT = mybir.ActivationFunctionType
ALU = mybir.AluOpType
AX_X = mybir.AxisListType.X

P = 128
S = 512
D = 1024
T = S // P
KD = D // P
DEPTH = 2
EPS = 1e-6
MASKED = -1e30
TAKEN = -3e38
ROPE_THETA = 10000.0

SPLITS = dict(cq=256, ckv=128, kr=32, bq=256, bk=128, bv=128, cq_=256, ck_=256, cv=256, qi=256, ki=32,
              w=8, dq=256, dk=256, dv=256, f=4)
COL = {}
_n = 0
for _k, _w in SPLITS.items():
    COL[_k] = _n
    _n += _w
IN_WIDTH = _n
GAP = COL["dv"] - COL["dq"]
TOK_W = IN_WIDTH - GAP


def tok(name):
    return COL[name] - (GAP if COL[name] > COL["dq"] else 0)


QR, KR, BQ, BK, CQ, CK, QI, KI, QN, KN, DQ, DK = 0, 1, 2, 4, 6, 8, 10, 12, 13, 15, 17, 19
N_TURNED = 21
N_ROPED = 13

RING = 5
SLOT = 2080


class Chain:

    def __init__(self, eng, sem):
        self.eng, self.sem, self.n = eng, sem, 0

    def __call__(self, instruction):
        self.n += 1
        instruction.then_inc(self.sem, 1)
        self.eng.wait_ge(self.sem, self.n)


class WeightRing:

    def __init__(self, nc, ctx):
        self.buf = ctx.enter_context(nc.sbuf_tensor("weight_ring", [P, RING, SLOT], F32))
        self.landed = [ctx.enter_context(nc.semaphore(f"weights_landed_{i}")) for i in range(RING)]
        self.items_done = ctx.enter_context(nc.semaphore("items_done"))
        self.restart([])

    def restart(self, items):
        self.items, self.sent, self.taken = items, 0, 0

    def view(self, i):
        rows, cols = self.items[i].shape[1:]
        return self.buf[:, i % RING, 0:rows * cols].rearrange("p (k c) -> p k c", k=rows)

    def send(self, sp, end):
        while self.sent < min(len(self.items), end + RING):
            i = self.sent
            if i >= RING:
                sp.wait_ge(self.items_done, i - RING + 1)
            sp.dma_start(self.view(i), self.items[i]).then_inc(self.landed[i % RING], 16)
            self.sent += 1

    def take(self, pe):
        i = self.taken
        self.taken += 1
        pe.wait_ge(self.landed[i % RING], 16 * (i // RING + 1))
        return self.view(i)

    def used(self, last_matmul):
        last_matmul.then_inc(self.items_done, 1)

    def sems(self):
        return self.landed + [self.items_done]


@contextmanager
def stage(nc, names):
    with ExitStack() as ctx:
        sems = [ctx.enter_context(nc.semaphore(n)) for n in names.split()]
        yield sems
        clear(nc, sems)


def clear(nc, sems):
    nums = sorted(s.num for s in sems)
    starts = [n for n in nums if n - 1 not in nums]
    for start in starts:
        end = start
        while end in nums:
            end += 1
        nc.all_engine_barrier(sems_to_clear=range(start, end))


def spread(ap, axis, n):
    ap = ap.unsqueeze(axis)
    shape = list(ap.shape)
    shape[axis] = n
    return ap.broadcast_to(shape)


def rope_tables():
    half = 32
    freq = (1.0 / (ROPE_THETA ** (np.arange(half, dtype=np.float32) * np.float32(2.0) / 64))).astype(np.float32)
    ang = np.arange(S, dtype=np.float32)[:, None] * freq[None, :]
    both = np.stack([np.cos(ang), np.sin(ang)], 0).astype(np.float32)
    return np.ascontiguousarray(both.reshape(2, T, P, half).transpose(2, 0, 1, 3))



def constants(nc, sb, psum):
    ident = sb("ident", [P, P])
    ones = sb("ones", [P, P])
    causal = sb("causal", [P, S])
    window = sb("window", [P, 2 * P])
    onehot = sb("onehot", [16, 16, P])
    with stage(nc, "filled masked") as (filled, masked), nc.Block() as block:
        @block.vector
        def _(dve):
            dve.memset(ident[:], 0.0).then_inc(filled, 1)
            dve.memset(ones[:], 1.0).then_inc(filled, 1)
            dve.memset(causal[:], 0.0).then_inc(filled, 1)
            dve.memset(window[:], 0.0).then_inc(filled, 1)
            dve.memset(onehot[:], 0.0).then_inc(filled, 1)

        @block.gpsimd
        def _(pool):
            pool.wait_ge(filled, 5)
            own = Chain(pool, masked)
            own(pool.affine_select(out=ident[:], in_=ident[:], compare_op=ALU.not_equal, fill=1.0, base=0,
                                   pattern=[[-1, P]], channel_multiplier=1))
            own(pool.affine_select(out=causal[:], in_=causal[:], compare_op=ALU.is_ge, fill=MASKED, base=S - P,
                                   pattern=[[-1, S]], channel_multiplier=1))
            own(pool.affine_select(out=window[:], in_=window[:], compare_op=ALU.is_ge, fill=MASKED, base=P,
                                   pattern=[[-1, 2 * P]], channel_multiplier=1))
            own(pool.affine_select(out=window[:], in_=window[:], compare_op=ALU.is_gt, fill=MASKED, base=0,
                                   pattern=[[1, 2 * P]], channel_multiplier=-1))
            own(pool.affine_select(out=onehot[:], in_=onehot[:], compare_op=ALU.not_equal, fill=1.0, base=0,
                                   pattern=[[-1, 16], [0, P]], channel_multiplier=1))
    return ident, ones, causal, window, onehot



def norm_and_turn(nc, psum, x, xn, gains, turned_x, ident, small, bias=None):
    ss, ms, root, rstd = (small[:, 4 * i:4 * i + 4] for i in range(4))
    with stage(nc, "squared mean_ready root_ready dve_own scaled turned stored_act stored_dve") as (
            squared, mean_ready, root_ready, dve_own, scaled, turned, stored_act, stored_dve), nc.Block() as block:
        @block.scalar
        def _(act):
            for t in range(T):
                act.activation(xn[:, t, :], x[:, t, :], ACT.Square, accum_out=ss[:, t:t + 1]).then_inc(squared, 1)
            act.wait_ge(mean_ready, 1)
            act.activation(root, ms, ACT.Sqrt).then_inc(root_ready, 1)
            for k in range(0, KD, 2):
                act.wait_ge(turned, k + 1)
                if bias is None:
                    act.activation(turned_x[:, k, :], psum[:, k, :], ACT.Copy,
                                   scale=gains[:, k:k + 1]).then_inc(stored_act, 1)
                else:
                    act.activation(turned_x[:, k, :], psum[:, k, :], ACT.Identity, scale=gains[:, k:k + 1],
                                   bias=bias[:, k:k + 1]).then_inc(stored_act, 1)

        @block.vector
        def _(dve):
            own = Chain(dve, dve_own)
            dve.wait_ge(squared, T)
            dve.tensor_scalar(ms, ss, 1.0 / D, EPS, ALU.mult, ALU.add).then_inc(mean_ready, 1)
            dve.wait_ge(root_ready, 1)
            own(dve.reciprocal(rstd, root))
            for t in range(T):
                dve.tensor_scalar(xn[:, t, :], x[:, t, :], rstd[:, t:t + 1], None, ALU.mult).then_inc(scaled, 1)
            for k in range(1, KD, 2):
                dve.wait_ge(turned, k + 1)
                if bias is None:
                    dve.tensor_scalar(turned_x[:, k, :], psum[:, k, :], gains[:, k:k + 1], None,
                                      ALU.mult).then_inc(stored_dve, 1)
                else:
                    dve.tensor_scalar(turned_x[:, k, :], psum[:, k, :], gains[:, k:k + 1], bias[:, k:k + 1],
                                      ALU.mult, ALU.add).then_inc(stored_dve, 1)

        @block.tensor
        def _(pe):
            pe.wait_ge(scaled, T)
            for k in range(KD):
                for t in range(T):
                    mm = pe.transpose(psum[:, k, t * P:(t + 1) * P], xn[:, t, k * P:(k + 1) * P], ident[:])
                mm.then_inc(turned, 1)



class Job:

    def __init__(self, scores, width, mask, scale, values, row, col, sink=None):
        self.scores, self.width, self.mask, self.scale = scores, width, mask, scale
        self.values, self.row, self.col, self.sink = values, row, col, sink


def attention(nc, psum, jobs, stores, ident, masked_s, probs, probs_t, stats, sems, extra_sync=None):
    (scored, added, shifted, powered, normed, turned, copied, valued, stored, dve_own, act_own) = sems
    RUN = 8
    n = len(jobs)
    B = 3
    with nc.Block() as block:
        if extra_sync is not None:
            block.sync(extra_sync)

        @block.tensor
        def _(pe):
            def scores(j):
                if j >= B:
                    pe.wait_ge(added, j - B + 1)
                job = jobs[j]
                for i, (lhs, rhs) in enumerate(job.scores):
                    mm = pe.matmul(psum[:, j % B, 0:job.width], lhs, rhs, start=(i == 0),
                                   stop=(i == len(job.scores) - 1))
                mm.then_inc(scored, 1)

            def turn(j):
                pe.wait_ge(normed, j + 1)
                if j >= B:
                    pe.wait_ge(copied, j - B + 1)
                for b in range(jobs[j].width // P):
                    mm = pe.transpose(psum[:, B + j % B, b * P:(b + 1) * P],
                                      probs[:, j % B, b * P:(b + 1) * P], ident[:])
                mm.then_inc(turned, 1)

            def values(j):
                job = jobs[j]
                run = j // RUN
                pe.wait_ge(copied, j + 1)
                if run >= 2 and j % RUN == 0:
                    pe.wait_ge(stored, run - 1)
                nb = len(job.values)
                for b, v in enumerate(job.values):
                    mm = pe.matmul(psum[job.row:job.row + 64, 2 * B + run % 2, job.col:job.col + P], v,
                                   probs_t[:, j % B, b * P:(b + 1) * P], start=(b == 0), stop=(b == nb - 1))
                mm.then_inc(valued, 1)

            for j in range(n + 2):
                if j < n:
                    scores(j)
                if 1 <= j <= n:
                    turn(j - 1)
                if j >= 2:
                    values(j - 2)

        @block.vector
        def _(dve):
            own = Chain(dve, dve_own)

            def add_mask(j):
                job = jobs[j]
                w = job.width
                dve.wait_ge(scored, j + 1)
                if j >= B:
                    dve.wait_ge(powered, j - B + 1)
                dve.scalar_tensor_tensor(out=masked_s[:, j % B, 0:w], in0=psum[:, j % B, 0:w], scalar=job.scale,
                                         in1=job.mask, op0=ALU.mult, op1=ALU.add).then_inc(added, 1)
                dve.wait_ge(added, j + 1)
                if job.sink is None:
                    dve.tensor_reduce(stats[:, 0, j:j + 1], masked_s[:, j % B, 0:w], AX_X, ALU.max,
                                      negate=True).then_inc(shifted, 1)
                else:
                    own(dve.tensor_reduce(stats[:, 4, j:j + 1], masked_s[:, j % B, 0:w], AX_X, ALU.max))
                    dve.tensor_scalar(stats[:, 0, j:j + 1], stats[:, 4, j:j + 1], job.sink, -1.0, ALU.max,
                                      ALU.mult).then_inc(shifted, 1)

            def norm(j):
                job = jobs[j]
                dve.wait_ge(powered, j + 1)
                total = stats[:, 1, j:j + 1]
                if job.sink is not None:
                    own(dve.tensor_scalar(stats[:, 2, j:j + 1], total, stats[:, 3, j:j + 1], None, ALU.add))
                    total = stats[:, 2, j:j + 1]
                own(dve.reciprocal(stats[:, 4, j:j + 1], total))
                dve.tensor_scalar(probs[:, j % B, 0:job.width], probs[:, j % B, 0:job.width],
                                  stats[:, 4, j:j + 1], None, ALU.mult).then_inc(normed, 1)

            for j in range(n + 1):
                if j < n:
                    add_mask(j)
                if j >= 1:
                    norm(j - 1)

        @block.scalar
        def _(act):
            def power(j):
                job = jobs[j]
                act.wait_ge(shifted, j + 1)
                if job.sink is not None:
                    own = Chain(act, act_own)
                    own.n = sum(1 for k in jobs[:j] if k.sink is not None)
                    own(act.activation(stats[:, 3, j:j + 1], job.sink, ACT.Exp, bias=stats[:, 0, j:j + 1]))
                if j >= B:
                    act.wait_ge(turned, j - B + 1)
                act.activation(probs[:, j % B, 0:job.width], masked_s[:, j % B, 0:job.width], ACT.Exp,
                               bias=stats[:, 0, j:j + 1], accum_out=stats[:, 1, j:j + 1]).then_inc(powered, 1)

            def copy(j):
                act.wait_ge(turned, j + 1)
                if j >= B:
                    act.wait_ge(valued, j - B + 1)
                w = jobs[j].width
                act.activation(probs_t[:, j % B, 0:w], psum[:, B + j % B, 0:w], ACT.Copy).then_inc(copied, 1)

            def store(run):
                act.wait_ge(valued, RUN * (run + 1))
                out, bank_view = stores[run]
                act.activation(out, bank_view(psum[:, 2 * B + run % 2, :]), ACT.Copy).then_inc(stored, 1)

            done = 0
            for j in range(n + 1):
                if j < n:
                    power(j)
                if j >= 1:
                    copy(j - 1)
                if j >= 3 and (j - 2) % RUN == 0:
                    store(done)
                    done += 1
            while done < n // RUN:
                store(done)
                done += 1


ATTENTION_SEMS = "scored added shifted powered normed turned copied valued stored dve_own act_own"



def product_by_tokens(pe, psum, bank, weights, lhs, n_items, chunks):
    k = 0
    for i in range(n_items):
        w = weights.take(pe)
        for kk in range(w.shape[1]):
            for t in range(T):
                mm = pe.matmul(psum[:, bank + t, 0:w.shape[2]], lhs[:, k, t * P:(t + 1) * P], w[:, kk, :],
                               start=(k == 0), stop=(k == chunks - 1))
            k += 1
        weights.used(mm)
    assert k == chunks


def product_by_channels(pe, bank, w, first, turned_x, chunks):
    for k in range(chunks):
        mm = pe.matmul(bank, w[:, k, first:first + P], turned_x[:, k, :], start=(k == 0), stop=(k == chunks - 1))
    return mm


def rows(w, k0, kk, c0, c1):
    return w[k0 * P:(k0 + kk) * P, c0:c1].rearrange("(k p) c -> p k c", p=P)


def output_products(nc, psum, x, weights, lhs, chunks, per_half, end, gate=None):
    with stage(nc, "summed gated") as (summed, gated), nc.Block() as block:
        start = weights.taken

        @block.sync
        def _(sp):
            weights.send(sp, end)

        @block.tensor
        def _(pe):
            for c in range(2):
                product_by_tokens(pe, psum, 4 * c, weights, lhs, per_half, chunks)

        @block.vector
        def _(dve):
            for c in range(2):
                dve.wait_ge(weights.items_done, start + (c + 1) * per_half)
                for t in range(T):
                    cols = slice(c * 512, (c + 1) * 512)
                    prod = psum[:, 4 * c + t, :]
                    if gate is not None:
                        dve.tensor_tensor(gate[1][:, t % 2, :], prod, gate[0][:, cols], ALU.mult).then_inc(gated, 1)
                        dve.wait_ge(gated, 4 * c + t + 1)
                        prod = gate[1][:, t % 2, :]
                    dve.tensor_tensor(x[:, t, cols], prod, x[:, t, cols], ALU.add).then_inc(summed, 1)


def layers(nc, psum, x, weights, consts, norm1, w_in, mla_q_norm, mla_kv_norm, mla_w_uq, mla_w_ukv,
           swa_sinks, fox_b_f, w_out, norm2, w_up, w_down):
    ident, ones, causal, window, onehot = consts
    F = w_up.shape[2]
    KF = F // P
    chunks = [(0, 512), (512, 1024), (1024, 1536), (1536, COL["dq"]), (COL["dv"], IN_WIDTH)]
    chunk_at = [0, 512, 1024, 1536, COL["dq"]]

    rope_table = nc.inline_tensor(rope_tables(), name="rope_table")
    with nc.Fori(0, DEPTH) as l, ExitStack() as lay:
        def sb(name, shape, ctx=lay):
            return ctx.enter_context(nc.sbuf_tensor(name, shape, F32))

        def one(a):
            return a[bass.ds(l, 1)].rearrange("o a b -> (o a) b")

        win, wuq, wukv, wout, wup, wdown = (one(a) for a in (w_in, mla_w_uq, mla_w_ukv, w_out, w_up, w_down))
        items = []
        for c0, c1 in chunks:
            per = 4 if KD * (c1 - c0) > SLOT else KD
            items += [rows(win, k, per, c0, c1) for k in range(0, KD, per)]
        n_tok = len(items)
        items += [rows(win, 0, KD, COL["dq"] + 256 * i, COL["dq"] + 256 * (i + 1)) for i in range(2)]
        n_proj = len(items)
        items += [rows(wuq, 0, 2, 0, 384), rows(wukv, 0, 1, 0, 512)]
        n_latent = len(items)
        items += [rows(wout, k, 4, c, c + 512) for c in (0, 512) for k in (0, 4)]
        n_out = len(items)
        items += [rows(wup, 0, KD, c, c + 256) for c in range(0, F, 256)]
        n_up = len(items)
        items += [rows(wdown, k, 4, c, c + 512) for c in (0, 512) for k in range(0, KF, 4)]
        n_down = len(items)
        weights.restart(items)

        gains = sb("gains", [P, 32])
        sinks = sb("sinks", [P, 4])
        rope = sb("rope", [P, 2, T, 32])
        forget_bias = sb("forget_bias", [4, 1])
        small = sb("small", [P, 32])
        turned_x = sb("turned_x", [P, KD, S])
        with ExitStack() as ctx:
            vec_rows = sb("vec_rows", [32, P], ctx)
            with stage(nc, "vectors_landed cleared vectors_turned vectors_stored") as (
                    vectors_landed, cleared, vectors_turned, vectors_stored), nc.Block() as block:
                @block.sync
                def _(sp):
                    sp.wait_ge(cleared, 1)
                    for r, v in ((0, norm1), (8, norm2), (16, mla_q_norm), (18, mla_kv_norm)):
                        n = v.shape[1] // P
                        sp.dma_start(vec_rows[r:r + n, :],
                                     v[bass.ds(l, 1), :].rearrange("o (r c) -> (o r) c", c=P)).then_inc(vectors_landed, 16)
                    sp.dma_start(sinks[:], swa_sinks[bass.ds(l, 1), :].to_broadcast([P, 4])).then_inc(vectors_landed, 16)
                    sp.dma_start(forget_bias[:], fox_b_f[bass.ds(l, 1), :].rearrange("o (h u) -> (o h) u", u=1)
                                 ).then_inc(vectors_landed, 16)
                    sp.dma_start(rope[:], rope_table[:]).then_inc(vectors_landed, 16)
                    weights.send(sp, 0)
                    sp.wait_ge(vectors_landed, 112)

                @block.vector
                def _(dve):
                    dve.memset(vec_rows[:], 0.0).then_inc(cleared, 1)
                    dve.wait_ge(vectors_turned, 1)
                    dve.tensor_copy(gains[:], psum[:, 0, 0:32]).then_inc(vectors_stored, 1)

                @block.tensor
                def _(pe):
                    pe.wait_ge(vectors_landed, 112)
                    pe.transpose(psum[:, 0, 0:32], vec_rows[:], ident[0:32, 0:32]).then_inc(vectors_turned, 1)

        with ExitStack() as mix:
            proj = sb("proj", [P, T, TOK_W], mix)
            turned = sb("turned_qk", [P, N_TURNED, S], mix)
            v_mla = sb("v_mla", [P, T, 256], mix)
            gates = sb("gates", [4, 2, S], mix)
            rows_x = proj[:].rearrange("p t c -> p (t c)")[:, 0:T * D].rearrange("p (t c) -> p t c", t=T)
            norm_and_turn(nc, psum, x, rows_x, gains[:, 0:8], turned_x, ident, small)
            in_projection(nc, psum, weights, turned_x, proj, turned, chunks, chunk_at, n_tok, n_proj)
            with ExitStack() as ctx:
                qa = sb("qa", [P, T, 384], ctx)
                k_nope = sb("k_nope", [P, T, 256], ctx)
                with ExitStack() as c2:
                    latents(nc, psum, weights, proj, qa, k_nope, v_mla, gates, gains, forget_bias, small, ident,
                            sb("latent", [P, T, 384], c2), sb("latent_t", [P, 3, S], c2),
                            sb("gate_work", [4, 3, S], c2), n_latent)
                rotate_and_turn(nc, psum, proj, qa, k_nope, turned, rope, ident,
                                sb("rotated", [P, 2, N_ROPED * P], ctx), sb("shared", [P, 2, 192], ctx),
                                sb("sines", [P, 512], ctx))
            chosen = sb("chosen", [P, T, S], mix)
            with ExitStack() as ctx:
                select_keys(nc, psum, proj, turned, chosen, causal, sb("relu", [P, 3, S], ctx),
                            sb("index_score", [P, T, S], ctx), sb("best", [P, 8], ctx))
            with ExitStack() as ctx:
                jobs = layer_jobs(turned, proj, v_mla, gates, chosen, causal, window, onehot, sinks)
                stores = [(turned_x[:, r, :], lambda bank: bank) for r in range(8)]
                with stage(nc, ATTENTION_SEMS) as sems:
                    attention(nc, psum, jobs, stores, ident, sb("masked_s", [P, 3, S], ctx), sb("probs", [P, 3, S], ctx),
                              sb("probs_t", [P, 3, S], ctx), sb("stats", [P, 5, len(jobs)], ctx), sems)
            output_products(nc, psum, x, weights, turned_x, KD, 2, n_out)

        with ExitStack() as ctx:
            hidden = sb("hidden", [P, KF, S], ctx)
            rows_x = hidden[:].rearrange("p k s -> p (k s)")[:, 0:T * D].rearrange("p (t c) -> p t c", t=T)
            norm_and_turn(nc, psum, x, rows_x, gains[:, 8:16], turned_x, ident, small)
            with stage(nc, "computed rectified squared") as (computed, rectified, squared), nc.Block() as block:
                @block.sync
                def _(sp):
                    weights.send(sp, n_up)

                @block.tensor
                def _(pe):
                    for f in range(KF):
                        if f % 2 == 0:
                            w = weights.take(pe)
                        if f >= 8:
                            pe.wait_ge(rectified, f - 7)
                        mm = product_by_channels(pe, psum[:, f % 8, :], w, P * (f % 2), turned_x, KD)
                        if f % 2 == 0:
                            mm.then_inc(computed, 1)
                        else:
                            weights.used(mm)

                @block.scalar
                def _(act):
                    for f in range(KF):
                        if f % 2 == 0:
                            act.wait_ge(computed, f // 2 + 1)
                        else:
                            act.wait_ge(weights.items_done, n_out + f // 2 + 1)
                        act.activation(hidden[:, f, :], psum[:, f % 8, :], ACT.Relu).then_inc(rectified, 1)

                @block.vector
                def _(dve):
                    for f in range(KF):
                        dve.wait_ge(rectified, f + 1)
                        dve.tensor_tensor(hidden[:, f, :], hidden[:, f, :], hidden[:, f, :], ALU.mult).then_inc(squared, 1)
            output_products(nc, psum, x, weights, hidden, KF, KF // 4, n_down)
        clear(nc, weights.sems())


def in_projection(nc, psum, weights, turned_x, proj, turned, chunks, chunk_at, n_tok, n_proj):
    ends = []
    n = 0
    for c0, c1 in chunks:
        n += 2 if KD * (c1 - c0) > SLOT else 1
        ends.append(n)
    ends.append(n + 2)
    groups = len(ends)
    with stage(nc, "stored_act stored_dve") as (stored_act, stored_dve), nc.Block() as block:
        @block.sync
        def _(sp):
            weights.send(sp, n_proj)

        @block.tensor
        def _(pe):
            for g in range(groups):
                if g >= 2:
                    pe.wait_ge(stored_act, 2 * (g - 1))
                    pe.wait_ge(stored_dve, 2 * (g - 1))
                bank = 4 * (g % 2)
                if g < groups - 1:
                    product_by_tokens(pe, psum, bank, weights, turned_x, ends[g] - (ends[g - 1] if g else 0), KD)
                else:
                    for i in range(2):
                        w = weights.take(pe)
                        for h in range(2):
                            mm = product_by_channels(pe, psum[:, bank + 2 * i + h, :], w, h * P, turned_x, KD)
                        weights.used(mm)

        def place(g, b):
            if g < groups - 1:
                w = chunks[g][1] - chunks[g][0]
                return proj[:, b, chunk_at[g]:chunk_at[g] + w], psum[:, 4 * (g % 2) + b, 0:w]
            return turned[:, DQ + b, :], psum[:, 4 * (g % 2) + b, :]

        @block.scalar
        def _(act):
            for g in range(groups):
                act.wait_ge(weights.items_done, ends[g])
                for b in (0, 1):
                    out, bank = place(g, b)
                    act.activation(out, bank, ACT.Copy).then_inc(stored_act, 1)

        @block.vector
        def _(dve):
            for g in range(groups):
                dve.wait_ge(weights.items_done, ends[g])
                for b in (2, 3):
                    out, bank = place(g, b)
                    dve.tensor_copy(out, bank).then_inc(stored_dve, 1)


def latents(nc, psum, weights, proj, qa, k_nope, v_mla, gates, gains, forget_bias, small, ident, latent, latent_t,
            gate_work, n_latent):
    QW, KW = SPLITS["cq"], SPLITS["ckv"]
    ss, ms, root, rstd = (small[:, 8 * i:8 * i + 8] for i in range(4))
    at_uq, at_ukv = n_latent - 2, n_latent - 1
    f0 = tok("f")

    def by_head(ap):
        return ap.rearrange("p (h c) -> p h c", h=4)

    def q_copies(t):
        bank = by_head(psum[:, 4 + t, 0:384])
        return [(by_head(qa[:, t, 0:256]), bank[:, :, 0:64]), (by_head(qa[:, t, 256:384]), bank[:, :, 64:96])]

    def kv_copies(t):
        bank = by_head(psum[:, t, :])
        return [(by_head(k_nope[:, t, :]), bank[:, :, 0:64]), (by_head(v_mla[:, t, :]), bank[:, :, 64:128])]

    with stage(nc, "squared mean_ready root_ready dve_own scaled turned gates_turned lat_act lat_dve kv_free "
                   "stored_act stored_dve gate_abs gate_exp gate_arg gate_log") as (
            squared, mean_ready, root_ready, dve_own, scaled, turned, gates_turned, lat_act, lat_dve, kv_free,
            stored_act, stored_dve, gate_abs, gate_exp, gate_arg, gate_log), nc.Block() as block:
        @block.sync
        def _(sp):
            weights.send(sp, n_latent)

        @block.scalar
        def _(act):
            for t in range(T):
                act.activation(latent[:, t, 0:QW], proj[:, t, 0:QW], ACT.Square,
                               accum_out=ss[:, t:t + 1]).then_inc(squared, 1)
                act.activation(latent[:, t, QW:QW + KW], proj[:, t, QW:QW + KW], ACT.Square,
                               accum_out=ss[:, 4 + t:5 + t]).then_inc(squared, 1)
            act.wait_ge(mean_ready, 2)
            act.activation(root, ms, ACT.Sqrt).then_inc(root_ready, 1)
            for k in range(2):
                act.wait_ge(turned, k + 1)
                act.activation(latent_t[:, k, :], psum[:, k, :], ACT.Copy,
                               scale=gains[:, 16 + k:17 + k]).then_inc(lat_act, 1)
            act.wait_ge(gate_abs, 1)
            act.activation(gate_work[:, 1, :], gate_work[:, 1, :], ACT.Exp, scale=-1.0).then_inc(gate_exp, 1)
            act.wait_ge(gate_arg, 1)
            act.activation(gate_work[:, 1, :], gate_work[:, 1, :], ACT.Ln).then_inc(gate_log, 1)
            for at, copies in ((at_uq, q_copies), (at_ukv, kv_copies)):
                act.wait_ge(weights.items_done, at + 1)
                for t in (0, 1):
                    for out, bank in copies(t):
                        act.activation(out, bank, ACT.Copy).then_inc(stored_act, 1)

        @block.vector
        def _(dve):
            own = Chain(dve, dve_own)
            dve.wait_ge(squared, 2 * T)
            dve.tensor_scalar(ms[:, 0:4], ss[:, 0:4], 1.0 / QW, EPS, ALU.mult, ALU.add).then_inc(mean_ready, 1)
            dve.tensor_scalar(ms[:, 4:8], ss[:, 4:8], 1.0 / KW, EPS, ALU.mult, ALU.add).then_inc(mean_ready, 1)
            dve.wait_ge(root_ready, 1)
            own(dve.reciprocal(rstd, root))
            for t in range(T):
                dve.tensor_scalar(latent[:, t, 0:QW], proj[:, t, 0:QW], rstd[:, t:t + 1], None,
                                  ALU.mult).then_inc(scaled, 1)
                dve.tensor_scalar(latent[:, t, QW:QW + KW], proj[:, t, QW:QW + KW], rstd[:, 4 + t:5 + t], None,
                                  ALU.mult).then_inc(scaled, 1)
            dve.wait_ge(turned, 3)
            dve.tensor_scalar(latent_t[:, 2, :], psum[:, 2, :], gains[:, 18:19], None, ALU.mult).then_inc(lat_dve, 1)
            dve.wait_ge(gates_turned, 1)
            own(dve.tensor_scalar(gate_work[:, 0, :], psum[0:4, 3, :], forget_bias[:, 0:1], None, ALU.add))
            dve.scalar_tensor_tensor(out=gate_work[:, 1, :], in0=gate_work[:, 0, :], scalar=-1.0,
                                     in1=gate_work[:, 0, :], op0=ALU.mult, op1=ALU.max).then_inc(gate_abs, 1)
            own(dve.memset(gate_work[:, 2, :], 1.0))
            dve.wait_ge(gate_exp, 1)
            dve.tensor_scalar(gate_work[:, 1, :], gate_work[:, 1, :], 1.0, None, ALU.add).then_inc(gate_arg, 1)
            dve.wait_ge(gate_log, 1)
            own(dve.scalar_tensor_tensor(out=gate_work[:, 0, :], in0=gate_work[:, 0, :], scalar=0.0,
                                         in1=gate_work[:, 1, :], op0=ALU.min, op1=ALU.subtract))
            own(dve.tensor_tensor_scan(gate_work[:, 1, :], gate_work[:, 2, :], gate_work[:, 0, :], 0.0,
                                       ALU.mult, ALU.add))
            own(dve.tensor_scalar(gates[:, 0, :], gate_work[:, 1, :], 8.0, None, ALU.mult))
            own(dve.tensor_scalar(gates[:, 1, :], gate_work[:, 1, :], -8.0, None, ALU.mult))
            for at, copies in ((at_uq, q_copies), (at_ukv, kv_copies)):
                dve.wait_ge(weights.items_done, at + 1)
                for t in (2, 3):
                    for out, bank in copies(t):
                        dve.tensor_copy(out, bank).then_inc(stored_dve, 1)

        @block.tensor
        def _(pe):
            for t in range(T):
                mm = pe.transpose(psum[0:4, 3, t * P:(t + 1) * P], proj[:, t, f0:f0 + 4], ident[:])
            mm.then_inc(gates_turned, 1)
            pe.wait_ge(scaled, 2 * T)
            for k in range(3):
                for t in range(T):
                    mm = pe.transpose(psum[:, k, t * P:(t + 1) * P], latent[:, t, k * P:(k + 1) * P], ident[:])
                mm.then_inc(turned, 1)
            pe.wait_ge(lat_act, 2)
            product_by_tokens(pe, psum, 4, weights, latent_t, 1, 2)
            pe.wait_ge(lat_dve, 1)
            pe.wait_ge(dve_own, 2)
            product_by_tokens(pe, psum, 0, weights, latent_t[:, 2:3, :], 1, 1)


def rotate_and_turn(nc, psum, proj, qa, k_nope, turned, rope, ident, rotated, shared, sines):
    BANKS = 8
    N_CHUNKS = N_ROPED + 4
    per_tile = -(-N_CHUNKS // 4)
    def parts(t, b):
        r = rotated[:, b, :]
        s = shared[:, b, :]
        p = proj[:, t, :]
        return [
            (qa[:, t, 256:384], 4, 16, r[:, QR * P:(QR + 1) * P]),
            (p[:, tok("kr"):tok("kr") + 32], 1, 16, s[:, 0:32]),
            (p[:, tok("bq"):tok("bq") + 256], 4, 32, r[:, BQ * P:(BQ + 2) * P]),
            (p[:, tok("bk"):tok("bk") + 128], 2, 32, s[:, 32:160]),
            (p[:, tok("cq_"):tok("cq_") + 512], 8, 32, r[:, CQ * P:(CQ + 4) * P]),
            (p[:, tok("qi"):tok("qi") + 256], 8, 16, r[:, QI * P:(QI + 2) * P]),
            (p[:, tok("ki"):tok("ki") + 32], 1, 16, s[:, 160:192]),
        ]
    n_parts = len(parts(0, 0))
    with stage(nc, "dve_own rotated_done repeated turned_banks stored") as (
            dve_own, rotated_done, repeated, turned_banks, stored), nc.Block() as block:
        @block.vector
        def _(dve):
            own = Chain(dve, dve_own)
            for t in range(T):
                b = t % 2
                if t >= 2:
                    dve.wait_ge(turned_banks, per_tile * (t - 1))
                    dve.wait_ge(repeated, 3 * (t - 1))
                for src, heads, half, out in parts(t, b):
                    step = 32 // half
                    cos, sin = (spread(spread(rope[:, i, t, 0:32:step], 1, 2), 1, heads) for i in range(2))
                    view = lambda a: a.rearrange("p (h a f) -> p h a f", h=heads, a=2)
                    sine = view(sines[:, 0:heads * 2 * half])
                    dve.tensor_tensor(view(out), view(src), cos, ALU.mult).then_inc(dve_own, 1)
                    own.n += 1
                    own(dve.tensor_tensor(sine, view(src), sin, ALU.mult))
                    a, c = view(out)[:, :, 0, :], view(out)[:, :, 1, :]
                    dve.tensor_tensor(a, a, sine[:, :, 1, :], ALU.subtract).then_inc(dve_own, 1)
                    own.n += 1
                    own(dve.tensor_tensor(c, c, sine[:, :, 0, :], ALU.add))
                    dve.sem_inc(rotated_done, 1)

        @block.gpsimd
        def _(pool):
            for t in range(T):
                b = t % 2
                pool.wait_ge(rotated_done, n_parts * (t + 1))
                if t >= 2:
                    pool.wait_ge(turned_banks, per_tile * (t - 1))
                r, s = rotated[:, b, :], shared[:, b, :]
                pool.tensor_copy(r[:, KR * P:(KR + 1) * P].rearrange("p (h c) -> p h c", h=4),
                                 spread(s[:, 0:32], 1, 4)).then_inc(repeated, 1)
                pool.tensor_copy(r[:, BK * P:(BK + 2) * P].rearrange("p (v h c) -> p v h c", v=2, h=2),
                                 spread(s[:, 32:160].rearrange("p (v c) -> p v c", v=2), 2, 2)).then_inc(repeated, 1)
                pool.tensor_copy(r[:, KI * P:(KI + 1) * P].rearrange("p (h c) -> p h c", h=4),
                                 spread(s[:, 160:192], 1, 4)).then_inc(repeated, 1)

        @block.tensor
        def _(pe):
            n = 0
            for t in range(T):
                pe.wait_ge(repeated, 3 * (t + 1))
                for first in range(0, N_CHUNKS, 4):
                    if n >= BANKS:
                        pe.wait_ge(stored, n - BANKS + 1)
                    for c in range(first, min(first + 4, N_CHUNKS)):
                        if c < N_ROPED:
                            src = rotated[:, t % 2, c * P:(c + 1) * P]
                        elif c < KN:
                            src = qa[:, t, (c - QN) * P:(c - QN + 1) * P]
                        else:
                            src = k_nope[:, t, (c - KN) * P:(c - KN + 1) * P]
                        mm = pe.transpose(psum[:, n % BANKS, (c - first) * P:(c - first + 1) * P], src, ident[:])
                    mm.then_inc(turned_banks, 1)
                    n += 1

        @block.scalar
        def _(act):
            n = 0
            for t in range(T):
                for first in range(0, N_CHUNKS, 4):
                    m = min(4, N_CHUNKS - first)
                    act.wait_ge(turned_banks, n + 1)
                    act.activation(turned[:, first:first + m, t * P:(t + 1) * P],
                                   psum[:, n % BANKS, 0:m * P].rearrange("p (c q) -> p c q", c=m),
                                   ACT.Copy).then_inc(stored, 1)
                    n += 1


def select_keys(nc, psum, proj, turned, chosen, causal, relu, score, best):
    HEADS, DIM, TOP_K, B = 8, 32, 128, 3
    assert TOP_K == P
    w0 = tok("w")
    todo = [(t, h) for t in range(1, T) for h in range(HEADS)]
    with stage(nc, "scored rectified weighed dve_own") as (scored, rectified, weighed, dve_own), nc.Block() as block:
        @block.tensor
        def _(pe):
            for j, (t, h) in enumerate(todo):
                if j >= 8:
                    pe.wait_ge(rectified, j - 7)
                r = DIM * (h % 4)
                pe.matmul(psum[:, j % 8, 0:(t + 1) * P], turned[r:r + DIM, QI + h // 4, t * P:(t + 1) * P],
                          turned[r:r + DIM, KI, 0:(t + 1) * P], start=True, stop=True).then_inc(scored, 1)

        @block.scalar
        def _(act):
            for j, (t, h) in enumerate(todo):
                act.wait_ge(scored, j + 1)
                if j >= B:
                    act.wait_ge(weighed, j - B + 1)
                act.activation(relu[:, j % B, 0:(t + 1) * P], psum[:, j % 8, 0:(t + 1) * P],
                               ACT.Relu).then_inc(rectified, 1)

        @block.vector
        def _(dve):
            own = Chain(dve, dve_own)
            own(dve.tensor_copy(chosen[:, 0, 0:P], causal[:, S - P:S]))
            for j, (t, h) in enumerate(todo):
                w = (t + 1) * P
                dve.wait_ge(rectified, j + 1)
                before = causal[:, S - w:S] if h == 0 else score[:, t, 0:w]
                dve.scalar_tensor_tensor(out=score[:, t, 0:w], in0=relu[:, j % B, 0:w],
                                         scalar=proj[:, t, w0 + h:w0 + h + 1], in1=before, op0=ALU.mult,
                                         op1=ALU.add).then_inc(weighed, 1)
                dve.wait_ge(weighed, j + 1)
            for t in range(1, T):
                s = score[:, t, 0:(t + 1) * P]
                for _ in range(TOP_K // 8):
                    own(dve.max(best[:], s))
                    own(dve.match_replace(s, best[:], s, TAKEN))
                own(dve.tensor_scalar(chosen[:, t, 0:(t + 1) * P], s, TAKEN / 2, MASKED, ALU.is_gt, ALU.mult))


def layer_jobs(turned, proj, v_mla, gates, chosen, causal, window, onehot, sinks):
    jobs = []
    for group in "abcd":
        for h in range(4):
            r = 64 * (h % 2)
            for t in range(T):
                w = (t + 1) * P
                q, k0, blocks = slice(t * P, w), 0, list(range(t + 1))
                mask = causal[:, S - w:S]
                sink = None
                scale = 64 ** -0.5
                if group == "a":
                    scale = 96 ** -0.5
                    scores = [(turned[r:r + 64, QN + h // 2, q], turned[r:r + 64, KN + h // 2, 0:w]),
                              (turned[32 * h:32 * h + 32, QR, q], turned[32 * h:32 * h + 32, KR, 0:w])]
                    v = [v_mla[:, b, 64 * h:64 * h + 64] for b in blocks]
                elif group == "b":
                    blocks = list(range(max(t - 1, 0), t + 1))
                    k0 = blocks[0] * P
                    mask = window[:, 2 * P - len(blocks) * P:2 * P]
                    sink = sinks[:, h:h + 1]
                    scores = [(turned[r:r + 64, BQ + h // 2, q], turned[r:r + 64, BK + h // 2, k0:w])]
                    v0 = tok("bv") + 64 * (h // 2)
                    v = [proj[:, b, v0:v0 + 64] for b in blocks]
                elif group == "c":
                    mask = chosen[:, t, 0:w]
                    scores = [(turned[r:r + 64, CQ + h // 2, q], turned[r:r + 64, CK + h // 2, 0:w])]
                    v0 = tok("cv") + 64 * h
                    v = [proj[:, b, v0:v0 + 64] for b in blocks]
                else:
                    scores = [(turned[r:r + 64, DQ + h // 2, q], turned[r:r + 64, DK + h // 2, 0:w]),
                              (onehot[0:4, h, :], gates[:, 1, 0:w]),
                              (gates[:, 0, q], onehot[0:4, h, 0:1].broadcast_to([4, w]))]
                    v0 = tok("dv") + 64 * h
                    v = [proj[:, b, v0:v0 + 64] for b in blocks]
                jobs.append(Job(scores, w - k0, mask, scale, v, r, t * P, sink))
    return jobs



SPLITS_2 = dict(qa=1024, ka=1024, va=1024, za=1024, beta=8, a=8, qb=768, kb=768, vb=768, zb=768, ga=1024, gb=1024)
COL_2 = {}
_n = 0
for _k, _w in SPLITS_2.items():
    COL_2[_k] = _n
    _n += _w
H = 8
CONV = 4
CH = 64
N_CH = S // CH
LEVELS = 6
GROUPS = 3
DILATION = (1, 4, 16)


def norm_rows(nc, x, gain_row, work, small):
    gain, scaled_x = work[:, 0, :], work[:, 1:3, :]
    ss, ms, root, rstd = (small[:, 4 * i:4 * i + 4] for i in range(4))
    with stage(nc, "gain_landed squared mean_ready root_ready dve_own") as (
            gain_landed, squared, mean_ready, root_ready, dve_own), nc.Block() as block:
        @block.sync
        def _(sp):
            sp.dma_start(gain, gain_row.to_broadcast([P, D])).then_inc(gain_landed, 16)

        @block.scalar
        def _(act):
            for t in range(T):
                if t >= 2:
                    act.wait_ge(squared, t - 1)
                act.activation(scaled_x[:, t % 2, :], x[:, t, :], ACT.Square,
                               accum_out=ss[:, t:t + 1]).then_inc(squared, 1)
            act.wait_ge(mean_ready, 1)
            act.activation(root, ms, ACT.Sqrt).then_inc(root_ready, 1)

        @block.vector
        def _(dve):
            own = Chain(dve, dve_own)
            dve.wait_ge(squared, T)
            dve.tensor_scalar(ms, ss, 1.0 / D, EPS, ALU.mult, ALU.add).then_inc(mean_ready, 1)
            dve.wait_ge(root_ready, 1)
            own(dve.reciprocal(rstd, root))
            dve.wait_ge(gain_landed, 16)
            for t in range(T):
                own(dve.scalar_tensor_tensor(out=x[:, t, :], in0=x[:, t, :], scalar=rstd[:, t:t + 1], in1=gain,
                                             op0=ALU.mult, op1=ALU.mult))


def second_constants(nc, ctx):
    def sb(name, shape):
        return ctx.enter_context(nc.sbuf_tensor(name, shape, F32))

    decay_mask = sb("decay_mask", [P, P])
    level_masks = sb("level_masks", [P, LEVELS, P])
    window_incl = sb("window_incl", [P, 2 * P])
    residues = sb("residues", [P, P])
    pick = sb("pick", [P, 31])
    with stage(nc, "filled masked") as (filled, masked), nc.Block() as block:
        @block.vector
        def _(dve):
            own = Chain(dve, filled)
            own(dve.memset(decay_mask[:], 0.0))
            own(dve.memset(level_masks[:], 0.0))
            for i in range(LEVELS):
                s = 1 << i
                own(dve.memset(level_masks[:, i, :].rearrange("p (j a w) -> p j a w", a=2, w=s)[:, :, 1, :], 1.0))
            own(dve.memset(window_incl[:], 0.0))
            own(dve.memset(residues[:], 0.0))
            own(dve.memset(pick[:], 0.0))
            own(dve.memset(pick[:, 15:16], 1.0))

        @block.gpsimd
        def _(pool):
            pool.wait_ge(filled, 6 + LEVELS)
            own = Chain(pool, masked)

            def keep(view, pattern, base, channel, fill):
                own(pool.affine_select(out=view, in_=view, compare_op=ALU.is_ge, fill=fill, base=base,
                                       pattern=pattern, channel_multiplier=channel))
            keep(decay_mask[:], [[1, P]], 0, -1, MASKED)
            keep(decay_mask[:].rearrange("p (j w) -> p j w", w=CH), [[-CH, 2], [0, CH]], 0, 1, MASKED)
            for i in range(LEVELS):
                s = 1 << i
                half = level_masks[:, i, :].rearrange("p (j a w) -> p j a w", a=2, w=s)[:, :, 1, :]
                keep(half, [[-2 * s, P // (2 * s)], [0, s]], 0, 1, 0.0)
                keep(half, [[2 * s, P // (2 * s)], [0, s]], s - 1, -1, 0.0)
            keep(window_incl[:], [[1, 2 * P]], 0, -1, MASKED)
            keep(window_incl[:], [[-1, 2 * P]], P, 1, MASKED)
            keep(residues[:], [[-1, P]], 0, 1, MASKED)
            keep(residues[:].rearrange("p (j w) -> p j w", w=32), [[32, 4], [0, 32]], 31, -1, MASKED)
    return decay_mask, level_masks, window_incl, residues, pick


def modulation(nc, psum, weights, a, ident, ones, work, cols, conv_cols, modulated, gate_row, head_vecs, n_ada):
    vec_rows, conv_rows, silu_c, silu_rows, gate_bias = work
    n_cols = 41
    with stage(nc, "landed conv_landed bias_landed head_landed cleared turned dve_own silu_ready products_ready") as (
            landed, conv_landed, bias_landed, head_landed, cleared, turned, dve_own, silu_ready,
            products_ready), nc.Block() as block:
        @block.sync
        def _(sp):
            sp.wait_ge(cleared, 1)
            for r, name in ((0, "norm_w_2"), (8, "c_2"), (16, "ada_b_2"), (40, "dn_norm_w_2")):
                n = a[name].shape[1] // P
                sp.dma_start(vec_rows[r:r + n, :],
                             a[name].rearrange("o (r c) -> (o r) c", c=P)).then_inc(landed, 16)
            sp.dma_start(conv_rows[:], a["conv_w_2"].rearrange("o j (r c) -> (o j r) c", c=P)).then_inc(conv_landed, 16)
            weights.send(sp, n_ada)
            sp.dma_start(gate_bias[:], a["ada_b_2"][:, 2 * D:3 * D].to_broadcast([P, D])).then_inc(bias_landed, 16)
            for i, name in enumerate(("a_log_2", "dt_bias_2")):
                sp.dma_start(head_vecs[:, i:i + 1], a[name].rearrange("o (h u) -> (o h) u", u=1)).then_inc(head_landed, 16)
            sp.wait_ge(head_landed, 32)

        @block.tensor
        def _(pe):
            pe.wait_ge(landed, 64)
            pe.wait_ge(conv_landed, 16)
            pe.transpose(psum[:, 3, 0:64], vec_rows[:], ident[0:64, 0:64])
            pe.transpose(psum[:, 3, 64:160], conv_rows[:], ident[0:96, 0:96]).then_inc(turned, 1)
            pe.wait_ge(dve_own, 3 + KD)
            for i in range(8):
                w = weights.take(pe)
                for half in range(2):
                    for k in range(KD):
                        mm = pe.matmul(psum[:, 0, 2 * i + half:2 * i + half + 1], w[:, k, half * P:(half + 1) * P],
                                       silu_c[:, k:k + 1], start=(k == 0), stop=(k == KD - 1))
                weights.used(mm)
            for i in range(4):
                w = weights.take(pe)
                for k in range(KD):
                    mm = pe.matmul(psum[:, 1 + i // 2, 256 * (i % 2):256 * (i % 2 + 1)], silu_rows[:, k, :],
                                   w[:, k, :], start=(k == 0), stop=(k == KD - 1))
                weights.used(mm)

        @block.scalar
        def _(act):
            act.wait_ge(dve_own, 2)
            act.activation(silu_c[:], cols[:, 8:16], ACT.Silu).then_inc(silu_ready, 1)

        @block.vector
        def _(dve):
            own = Chain(dve, dve_own)
            dve.memset(vec_rows[:], 0.0).then_inc(cleared, 1)
            dve.wait_ge(turned, 1)
            own(dve.tensor_copy(cols[:], psum[:, 3, 0:64]))
            own(dve.tensor_copy(conv_cols[:], psum[:, 3, 64:160]))
            dve.wait_ge(silu_ready, 1)
            for k in range(KD):
                own(dve.tensor_scalar(silu_rows[:, k, :], ones[:], silu_c[:, k:k + 1], None, ALU.mult))
            own(dve.tensor_scalar(cols[:, 48:56], cols[:, 24:32], 1.0, None, ALU.add))
            dve.wait_ge(weights.items_done, n_ada)
            own(dve.tensor_tensor(modulated[:, 8:16], psum[:, 0, 0:8], cols[:, 16:24], ALU.add))
            own(dve.tensor_tensor(modulated[:, 0:8], psum[:, 0, 8:16], cols[:, 48:56], ALU.add))
            own(dve.tensor_tensor(modulated[:, 0:8], modulated[:, 0:8], cols[:, 0:8], ALU.mult))
            dve.wait_ge(bias_landed, 16)
            for i in range(2):
                own(dve.tensor_tensor(gate_row[:, 512 * i:512 * (i + 1)], psum[:, 1 + i, :],
                                      gate_bias[:, 512 * i:512 * (i + 1)], ALU.add))


def conv_projection(nc, psum, weights, turned_x, qkv, rows, conv_cols, pick, head_vecs, work, end):
    before, squares, soft = work
    NB, SQ, BETA, DECAY = 4, 7, 5, 6
    CHUNKS = 3 * H
    with stage(nc, "computed copied convolved activated squared summed dve_own rows_exp rows_log "
                   "a_ready beta_ready zeroed") as (
            computed, copied, convolved, activated, squared, summed, dve_own, rows_exp, rows_log,
            a_ready, beta_ready, zeroed), nc.Block() as block:
        @block.sync
        def _(sp):
            weights.send(sp, end)

        @block.tensor
        def _(pe):
            w = weights.take(pe)
            for bank, c in ((BETA, 0), (DECAY, H)):
                for k in range(KD):
                    mm = pe.matmul(psum[0:H, bank, :], w[:, k, c:c + H], turned_x[:, k, :], start=(k == 0),
                                   stop=(k == KD - 1))
            weights.used(mm)

            def sum_squares(c):
                pe.wait_ge(squared, c + 1)
                pe.matmul(psum[0:16, SQ, :], pick[:, 15 - c:31 - c], squares[:, c % 2, :], start=(c == 0),
                          stop=(c == 2 * H - 1)).then_inc(summed, 1)

            for c in range(CHUNKS + 2):
                if c < CHUNKS:
                    if c % 2 == 0:
                        w = weights.take(pe)
                    if c >= NB:
                        pe.wait_ge(copied, c - NB + 1)
                    mm = product_by_channels(pe, psum[:, c % NB, :], w, P * (c % 2), turned_x, KD)
                    if c % 2 == 0:
                        mm.then_inc(computed, 1)
                    else:
                        weights.used(mm)
                if 2 <= c < 2 * H + 2:
                    sum_squares(c - 2)

        start = end - CHUNKS // 2

        @block.scalar
        def _(act):
            act.wait_ge(zeroed, 1)

            def silu(c):
                act.wait_ge(convolved, c + 1)
                act.activation(qkv[:, c, :], before[:, c % 3, 3:3 + S], ACT.Silu).then_inc(activated, 1)

            for c in range(CHUNKS + 1):
                if c < CHUNKS:
                    if c % 2 == 0:
                        act.wait_ge(computed, c // 2 + 1)
                    else:
                        act.wait_ge(weights.items_done, start + c // 2 + 1)
                    if c >= 3:
                        act.wait_ge(activated, c - 2)
                    act.activation(before[:, c % 3, 3:3 + S], psum[:, c % NB, :], ACT.Copy).then_inc(copied, 1)
                if c >= 1:
                    silu(c - 1)
            act.wait_ge(a_ready, 1)
            act.activation(soft[:, 1, :], soft[:, 1, :], ACT.Exp, scale=-1.0).then_inc(rows_exp, 1)
            act.activation(head_vecs[:, 2:3], head_vecs[:, 0:1], ACT.Exp).then_inc(rows_exp, 1)
            act.wait_ge(a_ready, 2)
            act.activation(soft[:, 1, :], soft[:, 1, :], ACT.Ln).then_inc(rows_log, 1)
            act.wait_ge(weights.items_done, start)
            act.activation(rows[:, 0, :], psum[0:H, BETA, :], ACT.Sigmoid).then_inc(beta_ready, 1)

        def square(dve, c):
            dve.wait_ge(activated, c + 1)
            if c >= 2:
                dve.wait_ge(summed, c - 1)
            dve.tensor_tensor(squares[:, c % 2, :], qkv[:, c, :], qkv[:, c, :], ALU.mult).then_inc(squared, 1)

        @block.vector
        def _(dve):
            own = Chain(dve, dve_own)
            dve.memset(before[:, :, 0:3], 0.0).then_inc(zeroed, 1)
            for c in range(CHUNKS):
                dve.wait_ge(copied, c + 1)
                b = before[:, c % 3, :]
                acc = squares[:, 2 + c % 2, :]
                own(dve.tensor_scalar(acc, b[:, 0:S], conv_cols[:, c:c + 1], None, ALU.mult))
                for j in (1, 2):
                    own(dve.scalar_tensor_tensor(out=acc, in0=b[:, j:j + S], scalar=conv_cols[:, 24 * j + c:24 * j + c + 1],
                                                 in1=acc, op0=ALU.mult, op1=ALU.add))
                dve.scalar_tensor_tensor(out=b[:, 3:3 + S], in0=b[:, 3:3 + S],
                                         scalar=conv_cols[:, 72 + c:73 + c], in1=acc, op0=ALU.mult,
                                         op1=ALU.add).then_inc(convolved, 1)
                if c >= 1 and c - 1 < 2 * H:
                    square(dve, c - 1)
            own(dve.tensor_scalar(soft[:, 0, :], psum[0:H, DECAY, :], head_vecs[:, 1:2], None, ALU.add))
            dve.scalar_tensor_tensor(out=soft[:, 1, :], in0=soft[:, 0, :], scalar=-1.0, in1=soft[:, 0, :],
                                     op0=ALU.mult, op1=ALU.max).then_inc(a_ready, 1)
            dve.wait_ge(rows_exp, 2)
            dve.tensor_scalar(soft[:, 1, :], soft[:, 1, :], 1.0, None, ALU.add).then_inc(a_ready, 1)
            own(dve.tensor_scalar(head_vecs[:, 3:4], head_vecs[:, 2:3], -1.0, None, ALU.mult))
            dve.wait_ge(rows_log, 1)
            own(dve.scalar_tensor_tensor(out=soft[:, 0, :], in0=soft[:, 0, :], scalar=0.0, in1=soft[:, 1, :],
                                         op0=ALU.max, op1=ALU.add))
            own(dve.tensor_scalar(rows[:, 1, :], soft[:, 0, :], head_vecs[:, 3:4], None, ALU.mult))



def normalize_and_spread(nc, psum, qkv, rows, ident, onehot, k_tok, v_tok, tok_cols, last_decay, work,
                         row_stats):
    SQ = 7
    norms, = row_stats
    exps, lasts, restart = work
    with stage(nc, "dve_own q_done root_ready spread_done scaled k_turned stored_act stored_dve rows_exp lasts_ready "
                   "rows_turned") as (
            dve_own, q_done, root_ready, spread_done, scaled, k_turned, stored_act, stored_dve, rows_exp, lasts_ready,
            rows_turned), nc.Block() as block:
        @block.scalar
        def _(act):
            act.wait_ge(q_done, 1)
            act.activation(norms[:, 0, :], norms[:, 0, :], ACT.Sqrt).then_inc(root_ready, 1)
            act.wait_ge(lasts_ready, 1)
            act.activation(exps[:, 0, :], rows[:, 1, :], ACT.Exp).then_inc(rows_exp, 1)
            act.activation(exps[:, 1, :], exps[:, 1, :], ACT.Exp).then_inc(rows_exp, 1)
            act.activation(lasts[:], lasts[:], ACT.Exp).then_inc(rows_exp, 1)
            for i in range(16):
                act.wait_ge(k_turned, i + 1)
                if i % 2 == 0:
                    h = i % H
                    out = (k_tok if i < H else v_tok)[:, :, h * P:(h + 1) * P]
                    act.activation(out, psum[:, i % 4, :].rearrange("p (t c) -> p t c", t=T), ACT.Copy
                                   ).then_inc(stored_act, 1)

        @block.vector
        def _(dve):
            own = Chain(dve, dve_own)
            dve.tensor_scalar(norms[:, 0, :], psum[0:16, SQ, :], EPS, None, ALU.add).then_inc(q_done, 1)
            own(dve.memset(restart[:], 1.0))
            own(dve.memset(restart[:].rearrange("p (n c) -> p n c", c=CH)[:, :, 0:1], 0.0))
            own(dve.tensor_tensor_scan(exps[:, 0, :], restart[:], rows[:, 1, :], 0.0, ALU.mult, ALU.add))
            own(dve.tensor_copy(rows[:, 1, :], exps[:, 0, :]))
            by_chunk = rows[:, 1, :].rearrange("p (n c) -> p n c", c=CH)
            own(dve.tensor_copy(lasts[:].unsqueeze(2), by_chunk[:, :, CH - 1:CH]))
            dve.tensor_tensor(exps[:, 1, :].rearrange("p (n c) -> p n c", c=CH),
                              spread(lasts[:], 2, CH), by_chunk, ALU.subtract).then_inc(lasts_ready, 1)
            dve.wait_ge(root_ready, 1)
            own(dve.reciprocal(norms[:, 1, :], norms[:, 0, :]))
            for c in range(2 * H):
                dve.wait_ge(spread_done, c + 1)
                if c < H:
                    dve.scalar_tensor_tensor(out=qkv[:, c, :], in0=qkv[:, c, :], scalar=float(P) ** -0.5,
                                             in1=psum[:, 4 + c % 3, :], op0=ALU.mult, op1=ALU.mult).then_inc(scaled, 1)
                else:
                    dve.tensor_tensor(qkv[:, c, :], qkv[:, c, :], psum[:, 4 + c % 3, :], ALU.mult).then_inc(scaled, 1)
            for i in range(16):
                dve.wait_ge(k_turned, i + 1)
                if i % 2 == 1:
                    h = i % H
                    out = (k_tok if i < H else v_tok)[:, :, h * P:(h + 1) * P]
                    dve.tensor_copy(out, psum[:, i % 4, :].rearrange("p (t c) -> p t c", t=T)).then_inc(stored_dve, 1)
            dve.wait_ge(rows_turned, 1)
            own(dve.tensor_copy(tok_cols[:].rearrange("p a t h -> p (a t h)"), psum[:, 4, 0:4 * T * H]))
            own(dve.tensor_tensor(tok_cols[:, 2], tok_cols[:, 2], tok_cols[:, 0], ALU.mult))
            own(dve.tensor_copy(last_decay[:].rearrange("p h n -> p (h n)"), psum[:, 5, 0:H * N_CH]))

        @block.tensor
        def _(pe):
            pe.wait_ge(dve_own, 6)
            for c in range(2 * H):
                if c >= 3:
                    pe.wait_ge(scaled, c - 2)
                pe.matmul(psum[:, 4 + c % 3, :], onehot[0:16, c, :], norms[:, 1, :], start=True,
                          stop=True).then_inc(spread_done, 1)
            for i in range(16):
                if i < H:
                    pe.wait_ge(scaled, H + i + 1)
                if i >= 4:
                    if i % 2 == 0:
                        pe.wait_ge(stored_act, (i - 4) // 2 + 1)
                    else:
                        pe.wait_ge(stored_dve, (i - 4) // 2 + 1)
                for t in range(T):
                    mm = pe.transpose(psum[:, i % 4, t * P:(t + 1) * P], qkv[:, H + i, t * P:(t + 1) * P], ident[:])
                mm.then_inc(k_turned, 1)
            pe.wait_ge(scaled, 2 * H)
            pe.wait_ge(rows_exp, 3)
            for i, src in enumerate((rows[:, 0, :], rows[:, 1, :], exps[:, 0, :], exps[:, 1, :])):
                for t in range(T):
                    o = (i * T + t) * H
                    pe.transpose(psum[:, 4, o:o + H], src[:, t * P:(t + 1) * P], ident[0:H, 0:H])
            for h in range(H):
                mm = pe.matmul(psum[:, 5, h * N_CH:(h + 1) * N_CH], onehot[0:H, h, :], lasts[:], start=True, stop=True)
            mm.then_inc(rows_turned, 1)


def delta_prepare(nc, psum, q_t, k_t, attn_t, k_tok, v_tok, rows, tok_cols, decay_mask, level_masks, ident, onehot,
                  sbx):
    G, HG = 2, 4
    dec, lt, x_m, x_t, y = (sbx(n, [P, G, HG * P]) for n in ("decays", "lower_t", "inverse", "inverse_t", "y"))
    eg = y
    lms = sbx("level_lower", [P, G, 2, HG * P])
    heads = lambda ap: ap.rearrange("p (h c) -> p h c", h=HG)
    ML = LEVELS - 1
    order = [(t, g) for t in range(T) for g in range(G)]
    with stage(nc, "formed argued decayed exp_ready attn_ready lower_ready started level_ready flipped inverse_ready y_done y_copied "
                   "z_done refined v_ready k_ready solved stored dve_own pool_own q_decayed") as (
            formed, argued, decayed, exp_ready, attn_ready, lower_ready, started, level_ready, flipped, inverse_ready,
            y_done, y_copied, z_done, refined, v_ready, k_ready, solved, stored, dve_own, pool_own,
            q_decayed), nc.Block() as block:
        @block.tensor
        def _(pe):
            for t in range(T):
                tile = slice(t * P, (t + 1) * P)
                for g in range(G):
                    i = t * G + g
                    if t:
                        pe.wait_ge(stored, i - 1)
                    b = 4 * g
                    for hh in range(HG):
                        h = HG * g + hh
                        c = slice(hh * P, (hh + 1) * P)
                        pe.matmul(psum[:, b, c], onehot[0:H, h, :], rows[:, 1, tile], start=True, stop=True)
                        pe.matmul(psum[:, b + 1, c], onehot[0:H, h, :], rows[:, 0, tile], start=True, stop=True)
                        pe.matmul(psum[:, b + 2, c], k_t[:, h, tile], k_t[:, h, tile], start=True, stop=True)
                        mm = pe.matmul(psum[:, b + 3, c], k_t[:, h, tile], q_t[:, h, tile], start=True, stop=True)
                    mm.then_inc(formed, 1)
                for g in range(G):
                    pe.wait_ge(started, t * G + g + 1)
                    pe.wait_ge(exp_ready, t * G + g + 1)
                    for hh in range(HG):
                        c = slice(hh * P, (hh + 1) * P)
                        mm = pe.transpose(psum[:, 4 * g, c], x_t[:, g, c], ident[:])
                    mm.then_inc(flipped, 1)
                for lv in range(ML):
                    for g in range(G):
                        i = (t * ML + lv) * G + g
                        pe.wait_ge(level_ready, i + 1)
                        if lv == 0:
                            pe.wait_ge(inverse_ready, t * G + g + 1)
                        else:
                            pe.wait_ge(refined, i - G + 1)
                        for hh in range(HG):
                            c = slice(hh * P, (hh + 1) * P)
                            mm = pe.matmul(psum[:, 4 * g + 1, c], lms[:, g, lv % 2, c], x_m[:, g, c], start=True, stop=True)
                        mm.then_inc(y_done, 1)
                    for g in range(G):
                        i = (t * ML + lv) * G + g
                        pe.wait_ge(y_copied, i + 1)
                        for hh in range(HG):
                            c = slice(hh * P, (hh + 1) * P)
                            mm = pe.matmul(psum[:, 4 * g + 2, c], y[:, g, c], x_t[:, g, c], start=True, stop=True)
                            if lv < ML - 1:
                                mm = pe.matmul(psum[:, 4 * g + 3, c], x_t[:, g, c], y[:, g, c], start=True, stop=True)
                        mm.then_inc(z_done, 1)
                for g in range(G):
                    i = t * G + g
                    pe.wait_ge(refined, (t * ML + ML - 1) * G + g + 1)
                    pe.wait_ge(v_ready, i + 1)
                    pe.wait_ge(k_ready, i + 1)
                    for hh in range(HG):
                        c = slice(hh * P, (hh + 1) * P)
                        pe.matmul(psum[:, 4 * g, c], x_t[:, g, c], dec[:, g, c], start=True, stop=True)
                        mm = pe.matmul(psum[:, 4 * g + 1, c], lt[:, g, c], x_t[:, g, c], start=True, stop=True)
                    mm.then_inc(solved, 1)

        @block.scalar
        def _(act):
            for t in range(T):
                tile = slice(t * P, (t + 1) * P)
                for g in range(G):
                    i = t * G + g
                    act.wait_ge(argued, i + 1)
                    act.activation(dec[:, g, :], dec[:, g, :], ACT.Exp).then_inc(decayed, 1)
                    act.activation(eg[:, g, :], psum[:, 4 * g, :], ACT.Exp).then_inc(exp_ready, 1)
                for g in range(G):
                    act.wait_ge(flipped, t * G + g + 1)
                    act.activation(x_m[:, g, :], psum[:, 4 * g, :], ACT.Copy).then_inc(inverse_ready, 1)
                for lv in range(ML):
                    for g in range(G):
                        i = (t * ML + lv) * G + g
                        act.wait_ge(y_done, i + 1)
                        if lv == 0:
                            act.wait_ge(q_decayed, t * G + g + 1)
                        act.activation(y[:, g, :], psum[:, 4 * g + 1, :], ACT.Copy).then_inc(y_copied, 1)
                for g in range(G):
                    i = t * G + g
                    act.wait_ge(solved, i + 1)
                    act.activation(v_tok[:, t, HG * g * P:HG * (g + 1) * P], psum[:, 4 * g, :], ACT.Copy)
                    act.activation(k_t[:, HG * g:HG * (g + 1), tile], heads(psum[:, 4 * g + 1, :]),
                                   ACT.Copy).then_inc(stored, 1)

        @block.vector
        def _(dve):
            own = Chain(dve, dve_own)
            for t in range(T):
                for g in range(G):
                    i = t * G + g
                    dve.wait_ge(formed, i + 1)
                    if t:
                        dve.wait_ge(solved, i - 1)
                    cols = tok_cols[:, 1, t, HG * g:HG * (g + 1)]
                    own(dve.tensor_tensor(heads(dec[:, g, :]), heads(psum[:, 4 * g, :]), spread(cols, 2, P), ALU.subtract))
                    dve.tensor_tensor(heads(dec[:, g, :]), heads(dec[:, g, :]), spread(decay_mask[:], 1, HG),
                                      ALU.add).then_inc(argued, 1)
                for g in range(G):
                    i = t * G + g
                    dve.wait_ge(decayed, i + 1)
                    dve.tensor_tensor(attn_t[:, t, HG * g * P:HG * (g + 1) * P], psum[:, 4 * g + 3, :],
                                      dec[:, g, :], ALU.mult).then_inc(attn_ready, 1)
                    own(dve.tensor_tensor(lt[:, g, :], psum[:, 4 * g + 2, :], dec[:, g, :], ALU.mult))
                    own(dve.tensor_tensor(lt[:, g, :], lt[:, g, :], psum[:, 4 * g + 1, :], ALU.mult))
                    dve.sem_inc(lower_ready, 1)
                    own(dve.tensor_tensor(heads(x_t[:, g, :]), heads(lt[:, g, :]), spread(level_masks[:, 0, :], 1, HG), ALU.mult))
                    dve.tensor_tensor(heads(x_t[:, g, :]), spread(ident[:], 1, HG), heads(x_t[:, g, :]),
                                      ALU.subtract).then_inc(started, 1)
                for lv in range(ML):
                    for g in range(G):
                        i = (t * ML + lv) * G + g
                        dve.wait_ge(z_done, i + 1)
                        if lv < ML - 1:
                            own(dve.tensor_tensor(x_m[:, g, :], x_m[:, g, :], psum[:, 4 * g + 3, :], ALU.subtract))
                        dve.tensor_tensor(x_t[:, g, :], x_t[:, g, :], psum[:, 4 * g + 2, :], ALU.subtract).then_inc(refined, 1)

        @block.gpsimd
        def _(pool):
            own = Chain(pool, pool_own)
            for t in range(T):
                tile = slice(t * P, (t + 1) * P)
                for lv in range(ML):
                    for g in range(G):
                        i = (t * ML + lv) * G + g
                        if lv == 0:
                            pool.wait_ge(lower_ready, t * G + g + 1)
                        if i - 2 * G >= 0:
                            pool.wait_ge(y_done, i - 2 * G + 1)
                        pool.tensor_tensor(heads(lms[:, g, lv % 2, :]), heads(lt[:, g, :]),
                                           spread(level_masks[:, lv + 1, :], 1, HG), ALU.mult).then_inc(level_ready, 1)
                    if lv == 0:
                        for g in range(G):
                            i = t * G + g
                            hs = slice(HG * g, HG * (g + 1))
                            pool.wait_ge(exp_ready, i + 1)
                            pool.tensor_tensor(q_t[:, hs, tile], q_t[:, hs, tile], heads(eg[:, g, :]), ALU.mult).then_inc(q_decayed, 1)
                            pool.wait_ge(attn_ready, i + 1)
                            pool.tensor_tensor(heads(dec[:, g, :]), heads(v_tok[:, t, HG * g * P:HG * (g + 1) * P]),
                                               spread(tok_cols[:, 0, t, hs], 2, P), ALU.mult).then_inc(v_ready, 1)
                for g in range(G):
                    i = t * G + g
                    hs = slice(HG * g, HG * (g + 1))
                    kk = heads(k_tok[:, t, HG * g * P:HG * (g + 1) * P])
                    pool.wait_ge(level_ready, (t * ML + ML - 1) * G + g + 1)
                    pool.wait_ge(started, i + 1)
                    pool.tensor_tensor(heads(lt[:, g, :]), kk, spread(tok_cols[:, 2, t, hs], 2, P), ALU.mult).then_inc(k_ready, 1)
                    pool.wait_ge(k_ready, i + 1)
                    own(pool.tensor_tensor(kk, kk, spread(tok_cols[:, 3, t, hs], 2, P), ALU.mult))


def delta_scan(nc, psum, q_t, w_t, attn_t, k_tok, u, last_decay, state):
    with stage(nc, "read_state v_ready products o_stored state_ready dve_own") as (
            read_state, v_ready, products, o_stored, state_ready, dve_own), nc.Block() as block:
        def place(n):
            return n // 2, CH * (n % 2)

        @block.tensor
        def _(pe):
            for n in range(N_CH):
                t, b = place(n)
                chunk = slice(t * P + b, t * P + b + CH)
                if n:
                    pe.wait_ge(state_ready, n)
                    for h in range(H):
                        c = slice((h % 4) * P, (h % 4 + 1) * P)
                        mm = pe.matmul(psum[b:b + CH, h // 4, c], w_t[:, h, chunk], state[:, h, :], start=True, stop=True)
                    mm.then_inc(read_state, 1)
                    pe.wait_ge(o_stored, n)
                    pe.wait_ge(v_ready, n)
                for h in range(H):
                    c = slice((h % 4) * P, (h % 4 + 1) * P)
                    hc = slice(h * P, (h + 1) * P)
                    if n:
                        pe.matmul(psum[b:b + CH, 2 + h // 4, c], q_t[:, h, chunk], state[:, h, :], start=True, stop=False)
                    pe.matmul(psum[b:b + CH, 2 + h // 4, c], attn_t[b:b + CH, t, h * P + b:h * P + b + CH],
                              u[b:b + CH, t, hc], start=(n == 0), stop=True)
                    mm = pe.matmul(psum[:, 4 + h // 4, c], k_tok[b:b + CH, t, hc], u[b:b + CH, t, hc], start=True, stop=True)
                mm.then_inc(products, 1)

        @block.vector
        def _(dve):
            own = Chain(dve, dve_own)
            for n in range(N_CH):
                t, b = place(n)
                if n:
                    dve.wait_ge(read_state, n)
                    for j in range(2):
                        c = slice(512 * j, 512 * (j + 1))
                        ins = dve.tensor_tensor(u[b:b + CH, t, c], u[b:b + CH, t, c], psum[b:b + CH, j, :], ALU.subtract)
                        if j == 0:
                            own(ins)
                        else:
                            ins.then_inc(v_ready, 1)
                dve.wait_ge(products, n + 1)
                flat = state[:].rearrange("p h c -> p (h c)")
                if n:
                    own(dve.tensor_tensor(state[:], state[:], spread(last_decay[:, :, n], 2, P), ALU.mult))
                for j in range(2):
                    c = slice(512 * j, 512 * (j + 1))
                    if n:
                        ins = dve.tensor_tensor(flat[:, c], flat[:, c], psum[:, 4 + j, :], ALU.add)
                    else:
                        ins = dve.tensor_copy(flat[:, c], psum[:, 4 + j, :])
                    if j == 0:
                        own(ins)
                    else:
                        ins.then_inc(state_ready, 1)

        @block.scalar
        def _(act):
            for n in range(N_CH):
                t, b = place(n)
                act.wait_ge(products, n + 1)
                for j in range(2):
                    ins = act.activation(attn_t[b:b + CH, t, 512 * j:512 * (j + 1)], psum[b:b + CH, 2 + j, :], ACT.Copy)
                ins.then_inc(o_stored, 1)


def channel_products(nc, psum, weights, lhs, chunks, epilogues, end, also=None, names=""):
    n = len(epilogues)
    n_act = lambda c: sum(1 for e in epilogues[:c] if e[0] == "act")
    n_dve = lambda c: sum(1 for e in epilogues[:c] if e[0] == "dve")
    with stage(nc, "computed stored_act stored_dve dve_own " + names) as sems, nc.Block() as block:
        computed, stored_act, stored_dve, dve_own = sems[0:4]
        start = weights.taken

        @block.sync
        def _(sp):
            weights.send(sp, end)

        @block.tensor
        def _(pe):
            for c in range(n):
                if c % 2 == 0:
                    w = weights.take(pe)
                if c >= 8:
                    if epilogues[c - 8][0] == "act":
                        pe.wait_ge(stored_act, n_act(c - 8) + 1)
                    else:
                        pe.wait_ge(stored_dve, n_dve(c - 8) + 1)
                mm = product_by_channels(pe, psum[:, c % 8, :], w, P * (c % 2), lhs, chunks)
                if c % 2 == 0:
                    mm.then_inc(computed, 1)
                else:
                    weights.used(mm)

        def ready(eng, c):
            if c % 2 == 0:
                eng.wait_ge(computed, c // 2 + 1)
            else:
                eng.wait_ge(weights.items_done, start + c // 2 + 1)

        @block.scalar
        def _(act):
            if also:
                also[0](act, sems[4:])
            for c, e in enumerate(epilogues):
                if e[0] == "act":
                    ready(act, c)
                    act.activation(e[2], e[3](psum[:, c % 8, :]), e[1]).then_inc(stored_act, 1)

        @block.vector
        def _(dve):
            if also:
                also[1](dve, sems[4:])
            own = Chain(dve, dve_own)
            for c, e in enumerate(epilogues):
                if e[0] == "dve":
                    ready(dve, c)
                    for s in e[1][:-1]:
                        own(s(dve, psum[:, c % 8, :]))
                    e[1][-1](dve, psum[:, c % 8, :]).then_inc(stored_dve, 1)


def same(bank):
    return bank


def permuted(view, group):
    if group == 0:
        return view
    return view.rearrange("p (s r) -> p r s", r=DILATION[group])


def in_order(view, group):
    if group == 0:
        return view
    return view.rearrange("p (r s) -> p r s", r=DILATION[group])


def second_part(nc, psum, x, weights, consts, a):
    ident, ones, causal, window, onehot = consts

    with ExitStack() as all2:
        def sb(name, shape, ctx=all2):
            return ctx.enter_context(nc.sbuf_tensor(name, shape, F32))

        one = lambda name: a[name].rearrange("o r c -> (o r) c")
        ada, win, wa, wb, wout = (one(n) for n in ("ada_w_2", "w_in_2", "w_proj_a_2", "w_proj_b_2", "w_out_2"))
        KB = wb.shape[0] // P
        items = [rows(ada, 0, KD, c, c + 256) for c in range(0, 3 * D, 256)]
        n_ada = len(items)

        def project(name):
            c0 = COL_2[name]
            return [rows(win, 0, KD, c, c + 256) for c in range(c0, c0 + SPLITS_2[name], 256)]

        items.append(rows(win, 0, KD, COL_2["beta"], COL_2["beta"] + 16))
        items += project("qa") + project("ka") + project("va")
        n_conv = len(items)
        items += project("za")
        n_za = len(items)
        items += project("ga")
        n_ga = len(items)
        items += [rows(wa, 0, KD, c, c + 256) for c in range(0, D, 256)]
        n_wa = len(items)
        items += project("qb") + project("kb") + project("vb") + project("zb")
        n_dil = len(items)
        items += project("gb")
        n_gb = len(items)
        items += [rows(wb, 0, KB, c, c + 256) for c in range(0, D, 256)]
        n_wb = len(items)
        items += [rows(wout, k, 4, c, c + 512) for c in (0, 512) for k in (0, 4)]
        n_all = len(items)
        weights.restart(items)

        small = sb("small_2", [P, 32])
        cols = sb("cols_2", [P, 64])
        conv_cols = sb("conv_cols", [P, CONV * 3 * H])
        modulated = sb("modulated", [P, 16])
        gate_row = sb("gate_row", [P, D])
        head_vecs = sb("head_vecs", [H, 4])
        decay_mask, level_masks, window_incl, residues, pick = second_constants(nc, all2)
        with ExitStack() as ctx:
            norm_rows(nc, x, a["final_norm"].rearrange("(o d) -> o d", o=1), sb("norm_work", [P, 3, D], ctx), small)
            work = (sb("vec_rows_2", [64, P], ctx), sb("conv_rows", [96, P], ctx), sb("silu_c", [P, KD], ctx),
                    sb("silu_rows", [P, KD, P], ctx), sb("gate_bias", [P, D], ctx))
            modulation(nc, psum, weights, a, ident, ones, work, cols, conv_cols, modulated, gate_row, head_vecs, n_ada)
        turned_x = sb("turned_x2", [P, KD, S])
        with ExitStack() as ctx:
            norm_and_turn(nc, psum, x, sb("rows_x", [P, T, D], ctx), modulated[:, 0:8], turned_x, ident, small,
                          bias=modulated[:, 8:16])

        with ExitStack() as delta:
            k_tok = sb("k_tok", [P, T, D], delta)
            qkv = sb("qkv", [P, 3 * H, S], delta)
            v_tok = sb("v_tok", [P, T, D], delta)
            attn_t = qkv[:].rearrange("p c s -> p (c s)")[:, 2 * H * S:3 * H * S].rearrange("p (t c) -> p t c", t=T)
            with ExitStack() as mid:
                heads_rows = sb("heads_rows", [H, 2, S], mid)
                tok_cols = sb("tok_cols", [P, 4, T, H], mid)
                last_decay = sb("last_decay", [P, H, N_CH], mid)
                with ExitStack() as ctx:
                    conv_projection(nc, psum, weights, turned_x, qkv, heads_rows, conv_cols, pick, head_vecs,
                                    (sb("before", [P, 3, S + 3], ctx), sb("squares", [P, 4, S], ctx),
                                     sb("soft", [H, 2, S], ctx)), n_conv)
                with ExitStack() as ctx:
                    normalize_and_spread(nc, psum, qkv, heads_rows, ident, onehot, k_tok, v_tok, tok_cols,
                                         last_decay, (sb("exps", [H, 2, S], ctx), sb("lasts", [H, N_CH], ctx),
                                          sb("restart", [H, S], ctx)),
                                         (sb("norms", [16, 2, S], ctx),))
                with ExitStack() as ctx:
                    delta_prepare(nc, psum, qkv[:, 0:H, :], qkv[:, H:2 * H, :], attn_t, k_tok, v_tok, heads_rows,
                                  tok_cols, decay_mask, level_masks, ident, onehot,
                                  lambda n, s: sb(n, s, ctx))
                with ExitStack() as ctx:
                    delta_scan(nc, psum, qkv[:, 0:H, :], qkv[:, H:2 * H, :], attn_t, k_tok, v_tok, last_decay,
                               sb("state", [P, H, P], ctx))
            o_stats = sb("o_stats", [P, 4, T * H], delta)
            y_a = qkv[:, 0:H, :]

            def square_o(act, sems):
                for i in range(T * H):
                    t, h = divmod(i, H)
                    act.activation(v_tok[:, t, h * P:(h + 1) * P], attn_t[:, t, h * P:(h + 1) * P], ACT.Square,
                                   accum_out=o_stats[:, 0, i:i + 1]).then_inc(sems[0], 1)
                act.wait_ge(sems[1], 1)
                act.activation(o_stats[:, 2, :], o_stats[:, 1, :], ACT.Sqrt).then_inc(sems[2], 1)

            def norm_o(dve, sems):
                own = Chain(dve, sems[3])
                dve.wait_ge(sems[0], T * H)
                dve.tensor_scalar(o_stats[:, 1, :], o_stats[:, 0, :], 1.0 / P, EPS, ALU.mult, ALU.add).then_inc(sems[1], 1)
                dve.wait_ge(sems[2], 1)
                own(dve.reciprocal(o_stats[:, 3, :], o_stats[:, 2, :]))
                for t in range(T):
                    o = attn_t[:, t, :].rearrange("p (h c) -> p h c", h=H)
                    own(dve.tensor_tensor(o, o, spread(o_stats[:, 3, t * H:(t + 1) * H], 2, P), ALU.mult))

            channel_products(nc, psum, weights, turned_x, KD,
                             [("act", ACT.Silu, y_a[:, c, :], same) for c in range(H)], n_za,
                             also=(square_o, norm_o), names="o_squared o_mean o_root o_own")
            with stage(nc, "turned gated") as (turned, gated), nc.Block() as block:
                @block.tensor
                def _(pe):
                    for h in range(H):
                        for t in range(T):
                            mm = pe.transpose(psum[:, h, t * P:(t + 1) * P], attn_t[:, t, h * P:(h + 1) * P], ident[:])
                        mm.then_inc(turned, 1)

                @block.vector
                def _(dve):
                    for h in range(H):
                        dve.wait_ge(turned, h + 1)
                        dve.scalar_tensor_tensor(out=y_a[:, h, :], in0=psum[:, h, :], scalar=cols[:, 40:41],
                                                 in1=y_a[:, h, :], op0=ALU.mult, op1=ALU.mult).then_inc(gated, 1)
            gate_a = qkv[:, H:2 * H, :]
            merged_v = k_tok[:].rearrange("p t c -> p (t c)").rearrange("p (k s) -> p k s", k=KD)
            channel_products(nc, psum, weights, turned_x, KD,
                             [("act", ACT.Sigmoid, gate_a[:, c, :], same) for c in range(KD)], n_ga)

            def times(c, gate, out):
                return lambda dve, bank: dve.tensor_tensor(out[:, c, :], bank, gate[:, c, :], ALU.mult)

            channel_products(nc, psum, weights, y_a, KD,
                             [("dve", [times(c, gate_a, merged_v)]) for c in range(KD)], n_wa)
            dilated(nc, psum, weights, turned_x, qkv, v_tok, merged_v, (n_dil, n_gb, n_wb, KB), window_incl, causal,
                    residues, ident, onehot, sb, delta)
            output_products(nc, psum, x, weights, merged_v, KD, 2, n_all,
                            gate=(gate_row, qkv[:, 0:2, :]))
        with ExitStack() as ctx:
            norm_rows(nc, x, a["final_norm_w_2"].rearrange("(o d) -> o d", o=1), sb("norm_work_2", [P, 3, D], ctx), small)


def dilated(nc, psum, weights, turned_x, free_chunks, free_tok, merged, ends, window_incl, causal, residues, ident,
            onehot, sb, ctx):
    n_dil, n_gb, n_wb, KB = ends
    C = 6
    q, k, v_t, z = (free_chunks[:, C * i:C * (i + 1), :] for i in range(4))
    v = free_tok[:].rearrange("p t c -> p (t c)")[:, 0:T * C * P].rearrange("p (t c) -> p t c", t=T)
    eps = []
    for name, dst in (("q", q), ("k", k), ("v", v_t)):
        for c in range(C):
            g = c // 2
            eps.append(("act", ACT.Copy, in_order(dst[:, c, :], g), lambda bank, g=g: permuted(bank, g)))
    eps += [("act", ACT.Silu, z[:, c, :], same) for c in range(C)]
    channel_products(nc, psum, weights, turned_x, KD, eps, n_dil)
    with stage(nc, "turned stored") as (turned, stored), nc.Block() as block:
        @block.tensor
        def _(pe):
            for c in range(C):
                for b in range(T):
                    mm = pe.transpose(psum[:, c, b * P:(b + 1) * P], v_t[:, c, b * P:(b + 1) * P], ident[:])
                mm.then_inc(turned, 1)

        @block.scalar
        def _(act):
            for c in range(C):
                act.wait_ge(turned, c + 1)
                act.activation(v[:, :, c * P:(c + 1) * P], psum[:, c, :].rearrange("p (t c) -> p t c", t=T),
                               ACT.Copy).then_inc(stored, 1)

    y = v_t
    jobs = []
    for g in range(GROUPS):
        for i in range(4):
            c = 2 * g + i // 2
            r = 64 * (i % 2)
            for b in range(T):
                blocks = [b] if g else list(range(max(b - 1, 0), b + 1))
                w = len(blocks) * P
                keys = slice(blocks[0] * P, (b + 1) * P)
                mask = (window_incl[:, 2 * P - w:2 * P], causal[:, S - P:S], residues[:])[g]
                jobs.append(Job([(q[r:r + 64, c, b * P:(b + 1) * P], k[r:r + 64, c, keys])], w, mask, 64 ** -0.5,
                                [v[:, kb, c * P + r:c * P + r + 64] for kb in blocks], r, b * P))
    stores = [(permuted(y[:, c, :], c // 2), lambda bank, g=c // 2: in_order(bank, g)) for c in range(C)]
    stats = sb("stats_2", [P, 5, len(jobs)], ctx)
    with ExitStack() as c2:
        with stage(nc, ATTENTION_SEMS) as sems:
            attention(nc, psum, jobs, stores, ident, sb("masked_s2", [P, 3, 2 * P], c2), sb("probs2", [P, 3, 2 * P], c2),
                      sb("probs_t2", [P, 3, 2 * P], c2), stats, sems)
    with ExitStack() as c2:
        lse = sb("lse", [4, GROUPS, S], c2)
        top = sb("top", [4, 2, S], c2)
        pair = sb("pair", [4, 2, P], c2)
        with stage(nc, "logged lse_ready turned dve_own powered spread_done weighed") as (
                logged, lse_ready, turned, dve_own, powered, spread_done, weighed), nc.Block() as block:
            @block.scalar
            def _(act):
                act.activation(stats[:, 2, :], stats[:, 1, :], ACT.Ln).then_inc(logged, 1)
                act.wait_ge(dve_own, 3 + GROUPS + 2 + GROUPS)
                act.activation(lse[:], lse[:], ACT.Exp).then_inc(powered, 1)

            @block.vector
            def _(dve):
                own = Chain(dve, dve_own)
                dve.wait_ge(logged, 1)
                own(dve.tensor_tensor(stats[:, 3, :], stats[:, 2, :], stats[:, 0, :], ALU.subtract))
                for j in range(2):
                    own(dve.tensor_copy(pair[:, j, :].rearrange("p (a c) -> p a c", a=2),
                                        onehot[0:4, 2 * j:2 * j + 2, 0:64]))
                dve.wait_ge(turned, 1)
                for g in range(GROUPS):
                    own(dve.tensor_copy(lse[:, g, :], psum[0:4, g, :]))
                own(dve.tensor_tensor(top[:, 0, :], lse[:, 0, :], lse[:, 1, :], ALU.max))
                own(dve.tensor_tensor(top[:, 0, :], top[:, 0, :], lse[:, 2, :], ALU.max))
                for g in range(GROUPS):
                    own(dve.tensor_tensor(lse[:, g, :], lse[:, g, :], top[:, 0, :], ALU.subtract))
                dve.wait_ge(powered, 1)
                own(dve.tensor_tensor(top[:, 0, :], lse[:, 0, :], lse[:, 1, :], ALU.add))
                own(dve.tensor_tensor(top[:, 0, :], top[:, 0, :], lse[:, 2, :], ALU.add))
                own(dve.reciprocal(top[:, 1, :], top[:, 0, :]))
                for g in range(GROUPS):
                    own(dve.tensor_tensor(lse[:, g, :], lse[:, g, :], top[:, 1, :], ALU.mult))
                for c in range(C):
                    dve.wait_ge(spread_done, c + 1)
                    own(dve.tensor_tensor(y[:, c, :], y[:, c, :], psum[:, c, :], ALU.mult))
                    dve.tensor_tensor(y[:, c, :], y[:, c, :], z[:, c, :], ALU.mult).then_inc(weighed, 1)

            @block.tensor
            def _(pe):
                pe.wait_ge(dve_own, 1)
                for g in range(GROUPS):
                    for b in range(T):
                        src = stats[:, 3, 16 * g + b:16 * g + b + 13:4]
                        out = permuted(psum[0:4, g, :], g)
                        if g == 0:
                            out = out[:, b * P:(b + 1) * P]
                        elif g == 1:
                            out = out[:, b, :]
                        else:
                            out = out[:, 4 * b:4 * b + 4, :]
                        mm = pe.transpose(out, src, ident[:])
                mm.then_inc(turned, 1)
                pe.wait_ge(dve_own, 3 + GROUPS + 2 + GROUPS + 3 + GROUPS)
                for c in range(C):
                    pe.matmul(psum[:, c, :], pair[:, c % 2, :], lse[:, c // 2, :], start=True, stop=True).then_inc(spread_done, 1)

    gate_b = free_chunks[:, 0:KD, :]
    channel_products(nc, psum, weights, turned_x, KD,
                     [("act", ACT.Sigmoid, gate_b[:, c, :], same) for c in range(KD)], n_gb)

    def steps(c):
        return [lambda dve, bank: dve.tensor_tensor(gate_b[:, c, :], bank, gate_b[:, c, :], ALU.mult),
                lambda dve, bank: dve.tensor_tensor(merged[:, c, :], merged[:, c, :], gate_b[:, c, :], ALU.add)]

    channel_products(nc, psum, weights, y, KB, [("dve", steps(c)) for c in range(KD)], n_wb)


def program(nc, a, out, first_only=False):
    with ExitStack() as ctx:
        def sb(name, shape):
            return ctx.enter_context(nc.sbuf_tensor(name, shape, F32))

        psum = ctx.enter_context(nc.psum_tensor("psum", [P, 8, 512], F32))
        x = sb("x_stream", [P, T, D])
        weights = WeightRing(nc, ctx)
        consts = constants(nc, sb, psum)
        with stage(nc, "x_landed other") as (x_landed, other), nc.Block() as block:
            @block.sync
            def _(sp):
                sp.dma_start(x[:], a["x"][0].rearrange("(t p) d -> p t d", p=P)).then_inc(x_landed, 16)
                sp.wait_ge(x_landed, 16)
        names = ("norm1 w_in mla_q_norm mla_kv_norm mla_w_uq mla_w_ukv swa_sinks fox_b_f w_out norm2 w_up "
                 "w_down").split()
        layers(nc, psum, x, weights, consts, *[a[n] for n in names])
        if not first_only:
            second_part(nc, psum, x, weights, consts, a)
        with stage(nc, "out_landed other") as (out_landed, other), nc.Block() as block:
            @block.sync
            def _(sp):
                sp.dma_start(out[0].rearrange("(t p) d -> p t d", p=P), x[:]).then_inc(out_landed, 16)
                sp.wait_ge(out_landed, 16)


_INS = ["x", "norm1", "w_in", "mla_q_norm", "mla_kv_norm", "mla_w_uq", "mla_w_ukv", "swa_sinks", "fox_b_f", "w_out",
        "norm2", "w_up", "w_down", "final_norm", "c_2", "norm_w_2", "ada_w_2", "ada_b_2", "w_in_2", "conv_w_2",
        "a_log_2", "dt_bias_2", "dn_norm_w_2", "w_proj_a_2", "w_proj_b_2", "w_out_2", "final_norm_w_2"]


def kernel(**inputs):
    import numpy as _np
    import concourse.bacc as _bacc
    from concourse import mybir as _mybir
    from concourse.bass_utils import run_bass_kernel_spmd as _run

    nc = _bacc.Bacc("TRN2", target_bir_lowering=False, num_devices=1)
    arrays, args = {}, {}
    for name in _INS:
        a = _np.ascontiguousarray(inputs[name])
        arrays[f"in_{name}_dram"] = a
        args[name] = nc.dram_tensor(f"in_{name}_dram", a.shape, _mybir.dt.from_np(a.dtype), kind="ExternalInput").ap()
    out = nc.dram_tensor("out_0_dram", (1, S, D), _mybir.dt.float32, kind="ExternalOutput").ap()
    program(nc, args, out)
    r = _run(nc, [arrays], core_ids=[0])
    return r.results[0]["out_0_dram"]
```

```python
from contextlib import ExitStack, contextmanager

import numpy as np

import concourse.bass as bass
from concourse import mybir

F32 = mybir.dt.float32
F32R = mybir.dt.float32r
ACT = mybir.ActivationFunctionType
ALU = mybir.AluOpType
AX_X = mybir.AxisListType.X

P = 128
S = 512
D = 1024
T = S // P
KD = D // P
DEPTH = 2
EPS = 1e-6
MASKED = -1e30
TAKEN = -3e38
ROPE_THETA = 10000.0

SPLITS = dict(cq=256, ckv=128, kr=32, bq=256, bk=128, bv=128, cq_=256, ck_=256, cv=256, qi=256, ki=32,
              w=8, dq=256, dk=256, dv=256, f=4)
COL = {}
_n = 0
for _k, _w in SPLITS.items():
    COL[_k] = _n
    _n += _w
IN_WIDTH = _n

PIECES = []
PLACE = {}
_at = {"proj": 0, "values": 0}
for _k, _w in SPLITS.items():
    if _k not in ("dq", "dk"):
        _b = "values" if _k in ("bv", "cv", "dv", "w", "f") else "proj"
        PLACE[_k] = _at[_b]
        if PIECES and PIECES[-1][1:3] == (COL[_k], _b):
            PIECES[-1] = (PIECES[-1][0], COL[_k] + _w, _b, PIECES[-1][3])
        else:
            PIECES.append((COL[_k], COL[_k] + _w, _b, _at[_b]))
        _at[_b] += _w
PROJ_W = _at["proj"]
V_MLA = _at["values"]
VALUES_W = V_MLA + 256


def tok(name):
    return PLACE[name]


QR, KR, BQ, BK, CQ, CK, QI, KI, QN, KN, DQ, DK = 0, 1, 2, 4, 6, 8, 10, 12, 13, 15, 17, 19
N_TURNED = 21
N_ROPED = 13

RING = 6
SPLIT_RING = 3
SLOT = 1040


class Chain:

    def __init__(self, eng, sem):
        self.eng, self.sem, self.n = eng, sem, 0

    def __call__(self, instruction):
        self.n += 1
        instruction.then_inc(self.sem, 1)
        self.eng.wait_ge(self.sem, self.n)


class WeightRing:

    def __init__(self, nc, ctx):
        self.buf = ctx.enter_context(nc.sbuf_tensor("weight_ring", [P, RING, SLOT], F32))
        self.pairs = ctx.enter_context(nc.sbuf_tensor("weight_pairs", [P, SPLIT_RING, 2, SLOT], F32R))
        self.landed = [ctx.enter_context(nc.semaphore(f"weights_landed_{i}")) for i in range(RING)]
        self.rounded = ctx.enter_context(nc.semaphore("weights_rounded"))
        self.split = ctx.enter_context(nc.semaphore("weights_split"))
        self.items_done = ctx.enter_context(nc.semaphore("items_done"))
        self.restart([])

    def restart(self, items):
        self.items, self.sent, self.taken, self.n_high, self.n_low = items, 0, 0, 0, 0

    def size(self, i):
        return self.items[i].shape[1] * self.items[i].shape[2]

    def send(self, sp, end):
        last = min(len(self.items), RING + (end - 1 + SPLIT_RING if end else 0))
        while self.sent < last:
            i = self.sent
            if i >= RING:
                sp.wait_ge(self.split, i - RING + 1)
            raw = self.buf[:, i % RING, 0:self.size(i)].rearrange("p (k c) -> p k c", k=self.items[i].shape[1])
            sp.dma_start(raw, self.items[i]).then_inc(self.landed[i % RING], 16)
            self.sent += 1

    def high(self, act, using):
        while self.n_high < min(len(self.items), using + SPLIT_RING):
            i, n = self.n_high, self.size(self.n_high)
            act.wait_ge(self.landed[i % RING], 16 * (i // RING + 1))
            if i >= SPLIT_RING:
                act.wait_ge(self.items_done, i - SPLIT_RING + 1)
            act.activation(self.pairs[:, i % SPLIT_RING, 0, 0:n], self.buf[:, i % RING, 0:n],
                           ACT.Copy).then_inc(self.rounded, 1)
            self.n_high += 1

    def low(self, dve, using):
        while self.n_low < min(len(self.items), using + SPLIT_RING):
            i, n = self.n_low, self.size(self.n_low)
            dve.wait_ge(self.rounded, i + 1)
            dve.tensor_tensor(self.pairs[:, i % SPLIT_RING, 1, 0:n], self.buf[:, i % RING, 0:n],
                              self.pairs[:, i % SPLIT_RING, 0, 0:n].bitcast(F32), ALU.subtract).then_inc(self.split, 1)
            self.n_low += 1

    def take(self, pe):
        i = self.taken
        self.taken += 1
        pe.wait_ge(self.split, i + 1)
        return [self.pairs[:, i % SPLIT_RING, j, 0:self.size(i)].rearrange("p (k c) -> p k c",
                                                                          k=self.items[i].shape[1]) for j in (0, 1)]

    def used(self, last_matmul):
        last_matmul.then_inc(self.items_done, 1)

    def sems(self):
        return self.landed + [self.rounded, self.split, self.items_done]


def product(pe, out, lhs, rhs, start, stop):
    pe.matmul(out, lhs[0], rhs[0], start=start, stop=False)
    pe.matmul(out, lhs[0], rhs[1], start=False, stop=False)
    return pe.matmul(out, lhs[1], rhs[0], start=False, stop=stop)


@contextmanager
def stage(nc, names):
    with ExitStack() as ctx:
        sems = [ctx.enter_context(nc.semaphore(n)) for n in names.split()]
        yield sems
        clear(nc, sems)


def clear(nc, sems):
    nums = sorted(s.num for s in sems)
    starts = [n for n in nums if n - 1 not in nums]
    for start in starts:
        end = start
        while end in nums:
            end += 1
        nc.all_engine_barrier(sems_to_clear=range(start, end))


def spread(ap, axis, n):
    ap = ap.unsqueeze(axis)
    shape = list(ap.shape)
    shape[axis] = n
    return ap.broadcast_to(shape)


def rope_tables():
    half = 32
    freq = (1.0 / (ROPE_THETA ** (np.arange(half, dtype=np.float32) * np.float32(2.0) / 64))).astype(np.float32)
    ang = np.arange(S, dtype=np.float32)[:, None] * freq[None, :]
    both = np.stack([np.cos(ang), np.sin(ang)], 0).astype(np.float32)
    return np.ascontiguousarray(both.reshape(2, T, P, half).transpose(2, 0, 1, 3))



def constants(nc, sb, psum):
    ident = sb("ident", [P, P])
    ones = sb("ones", [P, P])
    causal = sb("causal", [P, S])
    window = sb("window", [P, 2 * P])
    onehot = sb("onehot", [16, 16, P])
    with stage(nc, "filled masked") as (filled, masked), nc.Block() as block:
        @block.vector
        def _(dve):
            dve.memset(ident[:], 0.0).then_inc(filled, 1)
            dve.memset(ones[:], 1.0).then_inc(filled, 1)
            dve.memset(causal[:], 0.0).then_inc(filled, 1)
            dve.memset(window[:], 0.0).then_inc(filled, 1)
            dve.memset(onehot[:], 0.0).then_inc(filled, 1)

        @block.gpsimd
        def _(pool):
            pool.wait_ge(filled, 5)
            own = Chain(pool, masked)
            own(pool.affine_select(out=ident[:], in_=ident[:], compare_op=ALU.not_equal, fill=1.0, base=0,
                                   pattern=[[-1, P]], channel_multiplier=1))
            own(pool.affine_select(out=causal[:], in_=causal[:], compare_op=ALU.is_ge, fill=MASKED, base=S - P,
                                   pattern=[[-1, S]], channel_multiplier=1))
            own(pool.affine_select(out=window[:], in_=window[:], compare_op=ALU.is_ge, fill=MASKED, base=P,
                                   pattern=[[-1, 2 * P]], channel_multiplier=1))
            own(pool.affine_select(out=window[:], in_=window[:], compare_op=ALU.is_gt, fill=MASKED, base=0,
                                   pattern=[[1, 2 * P]], channel_multiplier=-1))
            own(pool.affine_select(out=onehot[:], in_=onehot[:], compare_op=ALU.not_equal, fill=1.0, base=0,
                                   pattern=[[-1, 16], [0, P]], channel_multiplier=1))
    return ident, ones, causal, window, onehot



def norm_and_turn(nc, psum, x, xn, gains, pair, ident, small, bias=None, work=None):
    ss, ms, root, rstd = (small[:, 4 * i:4 * i + 4] for i in range(4))
    with stage(nc, "squared mean_ready root_ready dve_own scaled turned shifted high low") as (
            squared, mean_ready, root_ready, dve_own, scaled, turned, shifted, high, low), nc.Block() as block:
        @block.scalar
        def _(act):
            for t in range(T):
                act.activation(xn[:, t, :], x[:, t, :], ACT.Square, accum_out=ss[:, t:t + 1]).then_inc(squared, 1)
            act.wait_ge(mean_ready, 1)
            act.activation(root, ms, ACT.Sqrt).then_inc(root_ready, 1)
            for k in range(KD):
                if bias is None:
                    act.wait_ge(turned, k + 1)
                    act.activation(pair[:, k, 0, :], psum[:, k, :], ACT.Copy, scale=gains[:, k:k + 1]).then_inc(high, 1)
                else:
                    act.wait_ge(shifted, k + 1)
                    act.activation(pair[:, k, 0, :], work[:, k % 2, :], ACT.Copy).then_inc(high, 1)

        @block.vector
        def _(dve):
            own = Chain(dve, dve_own)
            dve.wait_ge(squared, T)
            dve.tensor_scalar(ms, ss, 1.0 / D, EPS, ALU.mult, ALU.add).then_inc(mean_ready, 1)
            dve.wait_ge(root_ready, 1)
            own(dve.reciprocal(rstd, root))
            for t in range(T):
                dve.tensor_scalar(xn[:, t, :], x[:, t, :], rstd[:, t:t + 1], None, ALU.mult).then_inc(scaled, 1)

            def rest(k):
                dve.wait_ge(high, k + 1)
                if bias is None:
                    dve.scalar_tensor_tensor(out=pair[:, k, 1, :], in0=psum[:, k, :], scalar=gains[:, k:k + 1],
                                             in1=pair[:, k, 0, :].bitcast(F32), op0=ALU.mult,
                                             op1=ALU.subtract).then_inc(low, 1)
                else:
                    dve.tensor_tensor(pair[:, k, 1, :], work[:, k % 2, :], pair[:, k, 0, :].bitcast(F32),
                                      ALU.subtract).then_inc(low, 1)

            for k in range(KD):
                if bias is None:
                    rest(k)
                    continue
                dve.wait_ge(turned, k + 1)
                if k >= 2:
                    dve.wait_ge(low, k - 1)
                dve.tensor_scalar(work[:, k % 2, :], psum[:, k, :], gains[:, k:k + 1], bias[:, k:k + 1],
                                  ALU.mult, ALU.add).then_inc(shifted, 1)
                if k >= 1:
                    rest(k - 1)
            if bias is not None:
                rest(KD - 1)

        @block.tensor
        def _(pe):
            pe.wait_ge(scaled, T)
            for k in range(KD):
                for t in range(T):
                    mm = pe.transpose(psum[:, k, t * P:(t + 1) * P], xn[:, t, k * P:(k + 1) * P], ident[:])
                mm.then_inc(turned, 1)


def split_operand(nc, source, pair, n):
    with stage(nc, "high low") as (high, low), nc.Block() as block:
        @block.scalar
        def _(act):
            for k in range(n):
                act.activation(pair[:, k, 0, :], source(k), ACT.Copy).then_inc(high, 1)

        @block.vector
        def _(dve):
            for k in range(n):
                dve.wait_ge(high, k + 1)
                dve.tensor_tensor(pair[:, k, 1, :], source(k), pair[:, k, 0, :].bitcast(F32),
                                  ALU.subtract).then_inc(low, 1)



class Job:

    def __init__(self, scores, width, mask, scale, values, row, col, sink=None):
        self.scores, self.width, self.mask, self.scale = scores, width, mask, scale
        self.values, self.row, self.col, self.sink = values, row, col, sink


def attention(nc, psum, jobs, stores, ident, probs, probs_t, stats, sems, besides=()):
    (scored, added, shifted, powered, normed, turned, copied, valued, stored, stored_low, dve_own, act_own) = sems
    in_pairs = stores[0][2] is not None
    RUN, TURN, VALUES = 8, 2, 3
    n = len(jobs)
    SB, TB, PB = 3, 3, probs.shape[1]
    OUT = SB + TB
    with nc.Block() as block:
        @block.tensor
        def _(pe):
            def scores(j):
                if j >= SB:
                    pe.wait_ge(added, j - SB + 1)
                job = jobs[j]
                for i, (lhs, rhs) in enumerate(job.scores):
                    mm = pe.matmul(psum[:, j % SB, 0:job.width], lhs, rhs, start=(i == 0),
                                   stop=(i == len(job.scores) - 1))
                mm.then_inc(scored, 1)

            def turn(j):
                pe.wait_ge(normed, j + 1)
                if j >= TB:
                    pe.wait_ge(copied, j - TB + 1)
                for b in range(jobs[j].width // P):
                    mm = pe.transpose(psum[:, SB + j % TB, b * P:(b + 1) * P],
                                      probs[:, j % PB, b * P:(b + 1) * P], ident[:])
                mm.then_inc(turned, 1)

            def values(j):
                job = jobs[j]
                run = j // RUN
                pe.wait_ge(copied, j + 1)
                if run >= 2 and j % RUN == 0:
                    pe.wait_ge(stored_low if in_pairs else stored, run - 1)
                nb = len(job.values)
                for b, v in enumerate(job.values):
                    mm = pe.matmul(psum[job.row:job.row + 64, OUT + run % 2, job.col:job.col + P], v,
                                   probs_t[:, j % TB, b * P:(b + 1) * P], start=(b == 0), stop=(b == nb - 1))
                mm.then_inc(valued, 1)

            for j in range(n + VALUES):
                if j < n:
                    scores(j)
                if 0 <= j - TURN < n:
                    turn(j - TURN)
                if j >= VALUES:
                    values(j - VALUES)

        @block.vector
        def _(dve):
            own = Chain(dve, dve_own)

            def add_mask(j):
                job = jobs[j]
                w = job.width
                dve.wait_ge(scored, j + 1)
                if j >= PB:
                    dve.wait_ge(turned, j - PB + 1)
                dve.scalar_tensor_tensor(out=probs[:, j % PB, 0:w], in0=psum[:, j % SB, 0:w], scalar=job.scale,
                                         in1=job.mask, op0=ALU.mult, op1=ALU.add).then_inc(added, 1)
                dve.wait_ge(added, j + 1)
                if job.sink is None:
                    dve.tensor_reduce(stats[:, 0, j:j + 1], probs[:, j % PB, 0:w], AX_X, ALU.max,
                                      negate=True).then_inc(shifted, 1)
                else:
                    own(dve.tensor_reduce(stats[:, 4, j:j + 1], probs[:, j % PB, 0:w], AX_X, ALU.max))
                    dve.tensor_scalar(stats[:, 0, j:j + 1], stats[:, 4, j:j + 1], job.sink, -1.0, ALU.max,
                                      ALU.mult).then_inc(shifted, 1)

            def norm(j):
                job = jobs[j]
                dve.wait_ge(powered, j + 1)
                total = stats[:, 1, j:j + 1]
                if job.sink is not None:
                    own(dve.tensor_scalar(stats[:, 2, j:j + 1], total, stats[:, 3, j:j + 1], None, ALU.add))
                    total = stats[:, 2, j:j + 1]
                own(dve.reciprocal(stats[:, 4, j:j + 1], total))
                dve.tensor_scalar(probs[:, j % PB, 0:job.width], probs[:, j % PB, 0:job.width],
                                  stats[:, 4, j:j + 1], None, ALU.mult).then_inc(normed, 1)

            def store_low(run):
                dve.wait_ge(stored, run + 1)
                high, _, low = stores[run]
                dve.tensor_tensor(low, psum[:, OUT + run % 2, :], high.bitcast(F32), ALU.subtract).then_inc(stored_low, 1)

            done = 0
            for j in range(n + 1):
                if j < n:
                    add_mask(j)
                if j >= 1:
                    norm(j - 1)
                for step in besides[j] if j < len(besides) else ():
                    step(dve, own)
                if in_pairs and j > RUN * (done + 1) + VALUES + 1:
                    store_low(done)
                    done += 1
            while in_pairs and done < n // RUN:
                store_low(done)
                done += 1

        @block.scalar
        def _(act):
            own = Chain(act, act_own)

            def power(j):
                job = jobs[j]
                act.wait_ge(shifted, j + 1)
                if job.sink is not None:
                    own(act.activation(stats[:, 3, j:j + 1], job.sink, ACT.Exp, bias=stats[:, 0, j:j + 1]))
                p = probs[:, j % PB, 0:job.width]
                act.activation(p, p, ACT.Exp, bias=stats[:, 0, j:j + 1],
                               accum_out=stats[:, 1, j:j + 1]).then_inc(powered, 1)

            def copy(j):
                act.wait_ge(turned, j + 1)
                if j >= TB:
                    act.wait_ge(valued, j - TB + 1)
                w = jobs[j].width
                act.activation(probs_t[:, j % TB, 0:w], psum[:, SB + j % TB, 0:w], ACT.Copy).then_inc(copied, 1)

            def store(run):
                act.wait_ge(valued, RUN * (run + 1))
                out, bank_view, _ = stores[run]
                act.activation(out, bank_view(psum[:, OUT + run % 2, :]), ACT.Copy).then_inc(stored, 1)

            done = 0
            for j in range(n + TURN):
                if j < n:
                    power(j)
                if j >= TURN:
                    copy(j - TURN)
                if j > RUN * (done + 1) + VALUES:
                    store(done)
                    done += 1
            while done < n // RUN:
                store(done)
                done += 1


ATTENTION_SEMS = "scored added shifted powered normed turned copied valued stored stored_low dve_own act_own"



def product_by_tokens(pe, psum, bank, weights, lhs, n_items, chunks):
    k = 0
    for i in range(n_items):
        w = weights.take(pe)
        for kk in range(w[0].shape[1]):
            for t in range(T):
                tile = slice(t * P, (t + 1) * P)
                mm = product(pe, psum[:, bank + t, 0:w[0].shape[2]], [lhs[:, k, j, tile] for j in (0, 1)],
                             [w[j][:, kk, :] for j in (0, 1)], start=(k == 0), stop=(k == chunks - 1))
            k += 1
        weights.used(mm)
    assert k == chunks


def product_by_channels(pe, psum, banks, weights, pair, chunks):
    k = 0
    for i in range(2):
        w = weights.take(pe)
        n = w[0].shape[1]
        for h, bank in enumerate(banks):
            for kk in range(n):
                mm = product(pe, psum[:, bank, :], [w[j][:, kk, h * P:(h + 1) * P] for j in (0, 1)],
                             [pair[:, k + kk, j, :] for j in (0, 1)], start=(k + kk == 0),
                             stop=(k + kk == chunks - 1))
        k += n
        weights.used(mm)
    assert k == chunks


def rows(w, k0, kk, c0, c1):
    return w[k0 * P:(k0 + kk) * P, c0:c1].rearrange("(k p) c -> p k c", p=P)


def for_tokens(w, chunks, c0, c1, k0=0):
    per = max(kk for kk in range(1, chunks + 1) if chunks % kk == 0 and kk * (c1 - c0) <= SLOT)
    return [rows(w, k0 + k, per, c0, c1) for k in range(0, chunks, per)]


def for_channels(w, chunks, c0, c1):
    return [rows(w, k, chunks // 2, c, c + 256) for c in range(c0, c1, 256) for k in (0, chunks // 2)]


def output_products(nc, psum, x, weights, lhs, chunks, per_half, gate=None):
    start = weights.taken
    end = start + 2 * per_half
    with stage(nc, "summed gated") as (summed, gated), nc.Block() as block:
        @block.sync
        def _(sp):
            weights.send(sp, end)

        @block.tensor
        def _(pe):
            for c in range(2):
                product_by_tokens(pe, psum, 4 * c, weights, lhs, per_half, chunks)

        @block.scalar
        def _(act):
            for i in range(start, end):
                weights.high(act, i)

        @block.vector
        def _(dve):
            for c in range(2):
                for i in range(per_half):
                    weights.low(dve, start + c * per_half + i)
                dve.wait_ge(weights.items_done, start + (c + 1) * per_half)
                for t in range(T):
                    cols = slice(c * 512, (c + 1) * 512)
                    prod = psum[:, 4 * c + t, :]
                    if gate is not None:
                        if 4 * c + t >= 2:
                            dve.wait_ge(summed, 4 * c + t - 1)
                        dve.tensor_tensor(gate[1][:, t % 2, :], prod, gate[0][:, cols], ALU.mult).then_inc(gated, 1)
                        dve.wait_ge(gated, 4 * c + t + 1)
                        prod = gate[1][:, t % 2, :]
                    dve.tensor_tensor(x[:, t, cols], prod, x[:, t, cols], ALU.add).then_inc(summed, 1)


def layers(nc, psum, x, weights, consts, norm1, w_in, mla_q_norm, mla_kv_norm, mla_w_uq, mla_w_ukv,
           swa_sinks, fox_b_f, w_out, norm2, w_up, w_down):
    ident, ones, causal, window, onehot = consts
    F = w_up.shape[2]
    KH = F // P // 2
    chunks = [(0, 512), (512, 1024), (1024, 1536), (1536, COL["dq"]), (COL["dv"], IN_WIDTH)]

    rope_table = nc.inline_tensor(rope_tables(), name="rope_table")
    with nc.Fori(0, DEPTH) as l, ExitStack() as lay:
        def sb(name, shape, ctx=lay, dtype=F32):
            return ctx.enter_context(nc.sbuf_tensor(name, shape, dtype))

        def one(a):
            return a[bass.ds(l, 1)].rearrange("o a b -> (o a) b")

        win, wuq, wukv, wout, wup, wdown = (one(a) for a in (w_in, mla_w_uq, mla_w_ukv, w_out, w_up, w_down))
        items, ends = [], []
        for c0, c1 in chunks:
            items += for_tokens(win, KD, c0, c1)
            ends.append(len(items))
        items += for_channels(win, KD, COL["dq"], COL["dv"])
        ends.append(len(items))
        items += for_tokens(wuq, 2, 0, 384) + for_tokens(wukv, 1, 0, 512)
        out_items = for_tokens(wout, KD, 0, 512) + for_tokens(wout, KD, 512, D)
        items += out_items
        for half in range(2):
            items += for_channels(wup, KD, half * KH * P, (half + 1) * KH * P)
            down_items = [i for c in (0, 512) for i in for_tokens(wdown, KH, c, c + 512, k0=half * KH)]
            items += down_items
        weights.restart(items)

        gains = sb("gains", [P, 32])
        sinks = sb("sinks", [P, 4])
        rope = sb("rope", [P, 2, T, 32])
        forget_bias = sb("forget_bias", [4, 1])
        small = sb("small", [P, 32])
        with ExitStack() as ctx:
            vec_rows = sb("vec_rows", [32, P], ctx)
            with stage(nc, "vectors_landed cleared vectors_turned vectors_stored") as (
                    vectors_landed, cleared, vectors_turned, vectors_stored), nc.Block() as block:
                @block.sync
                def _(sp):
                    sp.wait_ge(cleared, 1)
                    for r, v in ((0, norm1), (8, norm2), (16, mla_q_norm), (18, mla_kv_norm)):
                        n = v.shape[1] // P
                        sp.dma_start(vec_rows[r:r + n, :],
                                     v[bass.ds(l, 1), :].rearrange("o (r c) -> (o r) c", c=P)).then_inc(vectors_landed, 16)
                    sp.dma_start(sinks[:], swa_sinks[bass.ds(l, 1), :].to_broadcast([P, 4])).then_inc(vectors_landed, 16)
                    sp.dma_start(forget_bias[:], fox_b_f[bass.ds(l, 1), :].rearrange("o (h u) -> (o h) u", u=1)
                                 ).then_inc(vectors_landed, 16)
                    sp.dma_start(rope[:], rope_table[:]).then_inc(vectors_landed, 16)
                    weights.send(sp, 0)
                    sp.wait_ge(vectors_landed, 112)

                @block.vector
                def _(dve):
                    dve.memset(vec_rows[:], 0.0).then_inc(cleared, 1)
                    dve.wait_ge(vectors_turned, 1)
                    dve.tensor_copy(gains[:], psum[:, 0, 0:32]).then_inc(vectors_stored, 1)

                @block.tensor
                def _(pe):
                    pe.wait_ge(vectors_landed, 112)
                    pe.transpose(psum[:, 0, 0:32], vec_rows[:], ident[0:32, 0:32]).then_inc(vectors_turned, 1)

        with ExitStack() as mix:
            values = sb("values", [P, T, VALUES_W], mix)
            gates = sb("gates", [4, 2, S], mix)
            turned = sb("turned_qk", [P, N_TURNED, S], mix)
            with ExitStack() as ctx:
                proj = sb("proj", [P, T, PROJ_W], ctx)
                with ExitStack() as c2:
                    turned_x = sb("turned_x", [P, KD, 2, S], c2, F32R)
                    rows_x = proj[:].rearrange("p t c -> p (t c)")[:, 0:T * D].rearrange("p (t c) -> p t c", t=T)
                    norm_and_turn(nc, psum, x, rows_x, gains[:, 0:8], turned_x, ident, small)
                    in_projection(nc, psum, weights, turned_x, dict(proj=proj, values=values), turned, chunks, ends)
                qa = sb("qa", [P, T, 384], ctx)
                k_nope = sb("k_nope", [P, T, 256], ctx)
                with ExitStack() as c2:
                    latents(nc, psum, weights, proj, qa, k_nope, values, gates, gains, forget_bias, small, ident,
                            sb("latent", [P, T, 384], c2), sb("latent_t", [P, 3, 2, S], c2, F32R),
                            sb("gate_work", [4, 3, S], c2))
                with ExitStack() as c2:
                    rotate_and_turn(nc, psum, proj, qa, k_nope, turned, rope, ident,
                                    sb("rotated", [P, 2, N_ROPED * P], c2), sb("shared", [P, 2, 192], c2),
                                    sb("sines", [P, 512], c2))
            chosen = sb("chosen", [P, T, S], mix)
            with ExitStack() as ctx:
                score_keys(nc, psum, values, turned, chosen, causal, sb("relu", [P, 3, S], ctx))
            mixed = sb("mixed", [P, KD, 2, S], mix, F32R)
            with ExitStack() as ctx:
                jobs = layer_jobs(turned, values, gates, chosen, causal, window, onehot, sinks)
                stores = [(mixed[:, c, 0, :], lambda bank: bank, mixed[:, c, 1, :])
                          for g in JOB_ORDER for c in (2 * "abcd".index(g), 2 * "abcd".index(g) + 1)]
                with stage(nc, ATTENTION_SEMS) as sems:
                    attention(nc, psum, jobs, stores, ident, sb("probs", [P, 4, S], ctx),
                              sb("probs_t", [P, 3, S], ctx), sb("stats", [P, 5, len(jobs)], ctx), sems,
                              besides=select_keys(chosen, sb("best", [P, 8], ctx), 3 * len(jobs) // 4 - 2))
            output_products(nc, psum, x, weights, mixed, KD, len(out_items) // 2)

        with ExitStack() as ctx:
            turned_x = sb("turned_x_mlp", [P, KD, 2, S], ctx, F32R)
            with ExitStack() as c2:
                norm_and_turn(nc, psum, x, sb("rows_mlp", [P, T, D], c2), gains[:, 8:16], turned_x, ident, small)
            hidden = sb("hidden", [P, KH, 2, S], ctx, F32R)
            relu = sb("relu_mlp", [P, 3, S], ctx)
            square = sb("square_mlp", [P, 3, S], ctx)
            for half in range(2):
                up_products(nc, psum, weights, turned_x, hidden, KH, relu, square)
                output_products(nc, psum, x, weights, hidden, KH, len(down_items) // 2)
        clear(nc, weights.sems())


def up_products(nc, psum, weights, turned_x, hidden, n, relu, square):
    B = 3
    start = weights.taken
    with stage(nc, "rectified squared high low") as (rectified, squared, high, low), nc.Block() as block:
        @block.sync
        def _(sp):
            weights.send(sp, start + n)

        @block.tensor
        def _(pe):
            for f in range(0, n, 2):
                if f >= 8:
                    pe.wait_ge(rectified, f - 6)
                product_by_channels(pe, psum, (f % 8, f % 8 + 1), weights, turned_x, KD)

        @block.scalar
        def _(act):
            def round_square(f):
                act.wait_ge(squared, f + 1)
                act.activation(hidden[:, f, 0, :], square[:, f % B, :], ACT.Copy).then_inc(high, 1)

            for f in range(0, n, 2):
                weights.high(act, start + f)
                weights.high(act, start + f + 1)
                act.wait_ge(weights.items_done, start + f + 2)
                for g in (f, f + 1):
                    if g >= B:
                        act.wait_ge(squared, g - B + 1)
                    act.activation(relu[:, g % B, :], psum[:, g % 8, :], ACT.Relu).then_inc(rectified, 1)
                    if g >= 1:
                        round_square(g - 1)
            round_square(n - 1)

        @block.vector
        def _(dve):
            def rest(f):
                dve.wait_ge(high, f + 1)
                dve.tensor_tensor(hidden[:, f, 1, :], square[:, f % B, :], hidden[:, f, 0, :].bitcast(F32),
                                  ALU.subtract).then_inc(low, 1)

            for f in range(n):
                weights.low(dve, start + f)
                dve.wait_ge(rectified, f + 1)
                if f >= B:
                    dve.wait_ge(low, f - B + 1)
                dve.tensor_tensor(square[:, f % B, :], relu[:, f % B, :], relu[:, f % B, :], ALU.mult).then_inc(squared, 1)
                if f >= 1:
                    rest(f - 1)
            rest(n - 1)


def in_projection(nc, psum, weights, turned_x, buffers, turned, chunks, ends):
    groups = len(ends)

    def copies(g, b):
        bank = 4 * (g % 2) + b
        if g == groups - 1:
            return [(turned[:, DQ + b, :], psum[:, bank, :])]
        c0, c1 = chunks[g]
        found = []
        for p0, p1, name, at in PIECES:
            a, e = max(p0, c0), min(p1, c1)
            if a < e:
                found.append((buffers[name][:, b, at + a - p0:at + e - p0], psum[:, bank, a - c0:e - c0]))
        return found

    def copied(g):
        return sum(2 * len(copies(i, 0)) for i in range(g + 1))

    with stage(nc, "stored_act stored_dve") as (stored_act, stored_dve), nc.Block() as block:
        @block.sync
        def _(sp):
            weights.send(sp, ends[-1])

        @block.tensor
        def _(pe):
            for g in range(groups):
                if g >= 2:
                    pe.wait_ge(stored_act, copied(g - 2))
                    pe.wait_ge(stored_dve, copied(g - 2))
                bank = 4 * (g % 2)
                if g < groups - 1:
                    product_by_tokens(pe, psum, bank, weights, turned_x, ends[g] - (ends[g - 1] if g else 0), KD)
                else:
                    product_by_channels(pe, psum, (bank, bank + 1), weights, turned_x, KD)
                    product_by_channels(pe, psum, (bank + 2, bank + 3), weights, turned_x, KD)

        @block.scalar
        def _(act):
            done = 0
            for g in range(groups):
                for i in range(done, ends[g]):
                    weights.high(act, i)
                done = ends[g]
                act.wait_ge(weights.items_done, ends[g])
                for b in (0, 1):
                    for out, bank in copies(g, b):
                        act.activation(out, bank, ACT.Copy).then_inc(stored_act, 1)

        @block.vector
        def _(dve):
            done = 0
            for g in range(groups):
                for i in range(done, ends[g]):
                    weights.low(dve, i)
                done = ends[g]
                dve.wait_ge(weights.items_done, ends[g])
                for b in (2, 3):
                    for out, bank in copies(g, b):
                        dve.tensor_copy(out, bank).then_inc(stored_dve, 1)


def latents(nc, psum, weights, proj, qa, k_nope, values, gates, gains, forget_bias, small, ident, latent, latent_t,
            gate_work):
    QW, KW = SPLITS["cq"], SPLITS["ckv"]
    ss, ms, root, rstd = (small[:, 8 * i:8 * i + 8] for i in range(4))
    at_uq = weights.taken
    at_ukv = at_uq + 1
    v_mla = values[:, :, V_MLA:V_MLA + 256]
    f0 = tok("f")

    def by_head(ap):
        return ap.rearrange("p (h c) -> p h c", h=4)

    def q_copies(t):
        bank = by_head(psum[:, 4 + t, 0:384])
        return [(by_head(qa[:, t, 0:256]), bank[:, :, 0:64]), (by_head(qa[:, t, 256:384]), bank[:, :, 64:96])]

    def kv_copies(t):
        bank = by_head(psum[:, t, :])
        return [(by_head(k_nope[:, t, :]), bank[:, :, 0:64]), (by_head(v_mla[:, t, :]), bank[:, :, 64:128])]

    with stage(nc, "squared mean_ready root_ready dve_own scaled turned gates_turned high low "
                   "stored_act stored_dve gate_abs gate_exp gate_arg gate_log") as (
            squared, mean_ready, root_ready, dve_own, scaled, turned, gates_turned, high, low,
            stored_act, stored_dve, gate_abs, gate_exp, gate_arg, gate_log), nc.Block() as block:
        @block.sync
        def _(sp):
            weights.send(sp, at_ukv + 1)

        @block.scalar
        def _(act):
            for t in range(T):
                act.activation(latent[:, t, 0:QW], proj[:, t, 0:QW], ACT.Square,
                               accum_out=ss[:, t:t + 1]).then_inc(squared, 1)
                act.activation(latent[:, t, QW:QW + KW], proj[:, t, QW:QW + KW], ACT.Square,
                               accum_out=ss[:, 4 + t:5 + t]).then_inc(squared, 1)
            act.wait_ge(mean_ready, 2)
            act.activation(root, ms, ACT.Sqrt).then_inc(root_ready, 1)
            for k in range(3):
                act.wait_ge(turned, k + 1)
                act.activation(latent_t[:, k, 0, :], psum[:, k, :], ACT.Copy,
                               scale=gains[:, 16 + k:17 + k]).then_inc(high, 1)
            act.wait_ge(gate_abs, 1)
            act.activation(gate_work[:, 1, :], gate_work[:, 1, :], ACT.Exp, scale=-1.0).then_inc(gate_exp, 1)
            act.wait_ge(gate_arg, 1)
            act.activation(gate_work[:, 1, :], gate_work[:, 1, :], ACT.Ln).then_inc(gate_log, 1)
            for at, copies in ((at_uq, q_copies), (at_ukv, kv_copies)):
                weights.high(act, at)
                act.wait_ge(weights.items_done, at + 1)
                for t in (0, 1):
                    for out, bank in copies(t):
                        act.activation(out, bank, ACT.Copy).then_inc(stored_act, 1)

        @block.vector
        def _(dve):
            own = Chain(dve, dve_own)
            dve.wait_ge(squared, 2 * T)
            dve.tensor_scalar(ms[:, 0:4], ss[:, 0:4], 1.0 / QW, EPS, ALU.mult, ALU.add).then_inc(mean_ready, 1)
            dve.tensor_scalar(ms[:, 4:8], ss[:, 4:8], 1.0 / KW, EPS, ALU.mult, ALU.add).then_inc(mean_ready, 1)
            dve.wait_ge(root_ready, 1)
            own(dve.reciprocal(rstd, root))
            for t in range(T):
                dve.tensor_scalar(latent[:, t, 0:QW], proj[:, t, 0:QW], rstd[:, t:t + 1], None,
                                  ALU.mult).then_inc(scaled, 1)
                dve.tensor_scalar(latent[:, t, QW:QW + KW], proj[:, t, QW:QW + KW], rstd[:, 4 + t:5 + t], None,
                                  ALU.mult).then_inc(scaled, 1)
            for k in range(3):
                dve.wait_ge(high, k + 1)
                dve.scalar_tensor_tensor(out=latent_t[:, k, 1, :], in0=psum[:, k, :], scalar=gains[:, 16 + k:17 + k],
                                         in1=latent_t[:, k, 0, :].bitcast(F32), op0=ALU.mult,
                                         op1=ALU.subtract).then_inc(low, 1)
            dve.wait_ge(gates_turned, 1)
            own(dve.tensor_scalar(gate_work[:, 0, :], psum[0:4, 3, :], forget_bias[:, 0:1], None, ALU.add))
            dve.scalar_tensor_tensor(out=gate_work[:, 1, :], in0=gate_work[:, 0, :], scalar=-1.0,
                                     in1=gate_work[:, 0, :], op0=ALU.mult, op1=ALU.max).then_inc(gate_abs, 1)
            own(dve.memset(gate_work[:, 2, :], 1.0))
            dve.wait_ge(gate_exp, 1)
            dve.tensor_scalar(gate_work[:, 1, :], gate_work[:, 1, :], 1.0, None, ALU.add).then_inc(gate_arg, 1)
            dve.wait_ge(gate_log, 1)
            own(dve.scalar_tensor_tensor(out=gate_work[:, 0, :], in0=gate_work[:, 0, :], scalar=0.0,
                                         in1=gate_work[:, 1, :], op0=ALU.min, op1=ALU.subtract))
            own(dve.tensor_tensor_scan(gate_work[:, 1, :], gate_work[:, 2, :], gate_work[:, 0, :], 0.0,
                                       ALU.mult, ALU.add))
            own(dve.tensor_scalar(gates[:, 0, :], gate_work[:, 1, :], 8.0, None, ALU.mult))
            own(dve.tensor_scalar(gates[:, 1, :], gate_work[:, 1, :], -8.0, None, ALU.mult))
            for at, copies in ((at_uq, q_copies), (at_ukv, kv_copies)):
                weights.low(dve, at)
                dve.wait_ge(weights.items_done, at + 1)
                for t in (2, 3):
                    for out, bank in copies(t):
                        dve.tensor_copy(out, bank).then_inc(stored_dve, 1)

        @block.tensor
        def _(pe):
            for t in range(T):
                mm = pe.transpose(psum[0:4, 3, t * P:(t + 1) * P], values[:, t, f0:f0 + 4], ident[:])
            mm.then_inc(gates_turned, 1)
            pe.wait_ge(scaled, 2 * T)
            for k in range(3):
                for t in range(T):
                    mm = pe.transpose(psum[:, k, t * P:(t + 1) * P], latent[:, t, k * P:(k + 1) * P], ident[:])
                mm.then_inc(turned, 1)
            pe.wait_ge(low, 2)
            product_by_tokens(pe, psum, 4, weights, latent_t[:, 0:2], 1, 2)
            pe.wait_ge(low, 3)
            pe.wait_ge(dve_own, 2)
            product_by_tokens(pe, psum, 0, weights, latent_t[:, 2:3], 1, 1)


def rotate_and_turn(nc, psum, proj, qa, k_nope, turned, rope, ident, rotated, shared, sines):
    BANKS = 8
    N_CHUNKS = N_ROPED + 4
    per_tile = -(-N_CHUNKS // 4)
    def parts(t, b):
        r = rotated[:, b, :]
        s = shared[:, b, :]
        p = proj[:, t, :]
        return [
            (qa[:, t, 256:384], 4, 16, r[:, QR * P:(QR + 1) * P]),
            (p[:, tok("kr"):tok("kr") + 32], 1, 16, s[:, 0:32]),
            (p[:, tok("bq"):tok("bq") + 256], 4, 32, r[:, BQ * P:(BQ + 2) * P]),
            (p[:, tok("bk"):tok("bk") + 128], 2, 32, s[:, 32:160]),
            (p[:, tok("cq_"):tok("cq_") + 512], 8, 32, r[:, CQ * P:(CQ + 4) * P]),
            (p[:, tok("qi"):tok("qi") + 256], 8, 16, r[:, QI * P:(QI + 2) * P]),
            (p[:, tok("ki"):tok("ki") + 32], 1, 16, s[:, 160:192]),
        ]
    n_parts = len(parts(0, 0))
    with stage(nc, "dve_own rotated_done repeated turned_banks stored") as (
            dve_own, rotated_done, repeated, turned_banks, stored), nc.Block() as block:
        @block.vector
        def _(dve):
            own = Chain(dve, dve_own)
            for t in range(T):
                b = t % 2
                if t >= 2:
                    dve.wait_ge(turned_banks, per_tile * (t - 1))
                    dve.wait_ge(repeated, 3 * (t - 1))
                for src, heads, half, out in parts(t, b):
                    step = 32 // half
                    cos, sin = (spread(spread(rope[:, i, t, 0:32:step], 1, 2), 1, heads) for i in range(2))
                    view = lambda a: a.rearrange("p (h a f) -> p h a f", h=heads, a=2)
                    sine = view(sines[:, 0:heads * 2 * half])
                    dve.tensor_tensor(view(out), view(src), cos, ALU.mult).then_inc(dve_own, 1)
                    own.n += 1
                    own(dve.tensor_tensor(sine, view(src), sin, ALU.mult))
                    a, c = view(out)[:, :, 0, :], view(out)[:, :, 1, :]
                    dve.tensor_tensor(a, a, sine[:, :, 1, :], ALU.subtract).then_inc(dve_own, 1)
                    own.n += 1
                    own(dve.tensor_tensor(c, c, sine[:, :, 0, :], ALU.add))
                    dve.sem_inc(rotated_done, 1)

        @block.gpsimd
        def _(pool):
            for t in range(T):
                b = t % 2
                pool.wait_ge(rotated_done, n_parts * (t + 1))
                if t >= 2:
                    pool.wait_ge(turned_banks, per_tile * (t - 1))
                r, s = rotated[:, b, :], shared[:, b, :]
                pool.tensor_copy(r[:, KR * P:(KR + 1) * P].rearrange("p (h c) -> p h c", h=4),
                                 spread(s[:, 0:32], 1, 4)).then_inc(repeated, 1)
                pool.tensor_copy(r[:, BK * P:(BK + 2) * P].rearrange("p (v h c) -> p v h c", v=2, h=2),
                                 spread(s[:, 32:160].rearrange("p (v c) -> p v c", v=2), 2, 2)).then_inc(repeated, 1)
                pool.tensor_copy(r[:, KI * P:(KI + 1) * P].rearrange("p (h c) -> p h c", h=4),
                                 spread(s[:, 160:192], 1, 4)).then_inc(repeated, 1)

        @block.tensor
        def _(pe):
            n = 0
            for t in range(T):
                pe.wait_ge(repeated, 3 * (t + 1))
                for first in range(0, N_CHUNKS, 4):
                    if n >= BANKS:
                        pe.wait_ge(stored, n - BANKS + 1)
                    for c in range(first, min(first + 4, N_CHUNKS)):
                        if c < N_ROPED:
                            src = rotated[:, t % 2, c * P:(c + 1) * P]
                        elif c < KN:
                            src = qa[:, t, (c - QN) * P:(c - QN + 1) * P]
                        else:
                            src = k_nope[:, t, (c - KN) * P:(c - KN + 1) * P]
                        mm = pe.transpose(psum[:, n % BANKS, (c - first) * P:(c - first + 1) * P], src, ident[:])
                    mm.then_inc(turned_banks, 1)
                    n += 1

        @block.scalar
        def _(act):
            n = 0
            for t in range(T):
                for first in range(0, N_CHUNKS, 4):
                    m = min(4, N_CHUNKS - first)
                    act.wait_ge(turned_banks, n + 1)
                    act.activation(turned[:, first:first + m, t * P:(t + 1) * P],
                                   psum[:, n % BANKS, 0:m * P].rearrange("p (c q) -> p c q", c=m),
                                   ACT.Copy).then_inc(stored, 1)
                    n += 1


TOP_K = 128
JOB_ORDER = "abdc"


def score_keys(nc, psum, values, turned, score, causal, relu):
    HEADS, DIM, B = 8, 32, 3
    assert TOP_K == P
    w0 = tok("w")
    todo = [(t, h) for t in range(1, T) for h in range(HEADS)]
    with stage(nc, "scored rectified weighed") as (scored, rectified, weighed), nc.Block() as block:
        @block.tensor
        def _(pe):
            for j, (t, h) in enumerate(todo):
                if j >= 8:
                    pe.wait_ge(rectified, j - 7)
                r = DIM * (h % 4)
                pe.matmul(psum[:, j % 8, 0:(t + 1) * P], turned[r:r + DIM, QI + h // 4, t * P:(t + 1) * P],
                          turned[r:r + DIM, KI, 0:(t + 1) * P], start=True, stop=True).then_inc(scored, 1)

        @block.scalar
        def _(act):
            for j, (t, h) in enumerate(todo):
                act.wait_ge(scored, j + 1)
                if j >= B:
                    act.wait_ge(weighed, j - B + 1)
                act.activation(relu[:, j % B, 0:(t + 1) * P], psum[:, j % 8, 0:(t + 1) * P],
                               ACT.Relu).then_inc(rectified, 1)

        @block.vector
        def _(dve):
            for j, (t, h) in enumerate(todo):
                w = (t + 1) * P
                dve.wait_ge(rectified, j + 1)
                before = causal[:, S - w:S] if h == 0 else score[:, t, 0:w]
                dve.scalar_tensor_tensor(out=score[:, t, 0:w], in0=relu[:, j % B, 0:w],
                                         scalar=values[:, t, w0 + h:w0 + h + 1], in1=before, op0=ALU.mult,
                                         op1=ALU.add).then_inc(weighed, 1)
                dve.wait_ge(weighed, j + 1)


def select_keys(chosen, best, n_jobs):
    steps = []
    for t in range(1, T):
        s = chosen[:, t, 0:(t + 1) * P]

        def take_eight(dve, own, s=s):
            own(dve.max(best[:], s))
            own(dve.match_replace(s, best[:], s, TAKEN))

        def finish(dve, own, s=s):
            own(dve.tensor_scalar(s, s, TAKEN / 2, MASKED, ALU.is_gt, ALU.mult))
        steps += [take_eight] * (TOP_K // 8) + [finish]
    return [steps[len(steps) * j // n_jobs:len(steps) * (j + 1) // n_jobs] for j in range(n_jobs)]


def layer_jobs(turned, values, gates, chosen, causal, window, onehot, sinks):
    jobs = []
    for group in JOB_ORDER:
        for h in range(4):
            r = 64 * (h % 2)
            for t in range(T):
                w = (t + 1) * P
                q, k0, blocks = slice(t * P, w), 0, list(range(t + 1))
                mask = causal[:, S - w:S]
                sink = None
                scale = 64 ** -0.5
                if group == "a":
                    scale = 96 ** -0.5
                    scores = [(turned[r:r + 64, QN + h // 2, q], turned[r:r + 64, KN + h // 2, 0:w]),
                              (turned[32 * h:32 * h + 32, QR, q], turned[32 * h:32 * h + 32, KR, 0:w])]
                    v0 = V_MLA + 64 * h
                    v = [values[:, b, v0:v0 + 64] for b in blocks]
                elif group == "b":
                    blocks = list(range(max(t - 1, 0), t + 1))
                    k0 = blocks[0] * P
                    mask = window[:, 2 * P - len(blocks) * P:2 * P]
                    sink = sinks[:, h:h + 1]
                    scores = [(turned[r:r + 64, BQ + h // 2, q], turned[r:r + 64, BK + h // 2, k0:w])]
                    v0 = tok("bv") + 64 * (h // 2)
                    v = [values[:, b, v0:v0 + 64] for b in blocks]
                elif group == "c":
                    if t:
                        mask = chosen[:, t, 0:w]
                    scores = [(turned[r:r + 64, CQ + h // 2, q], turned[r:r + 64, CK + h // 2, 0:w])]
                    v0 = tok("cv") + 64 * h
                    v = [values[:, b, v0:v0 + 64] for b in blocks]
                else:
                    scores = [(turned[r:r + 64, DQ + h // 2, q], turned[r:r + 64, DK + h // 2, 0:w]),
                              (onehot[0:4, h, :], gates[:, 1, 0:w]),
                              (gates[:, 0, q], onehot[0:4, h, 0:1].broadcast_to([4, w]))]
                    v0 = tok("dv") + 64 * h
                    v = [values[:, b, v0:v0 + 64] for b in blocks]
                jobs.append(Job(scores, w - k0, mask, scale, v, r, t * P, sink))
    return jobs



SPLITS_2 = dict(qa=1024, ka=1024, va=1024, za=1024, beta=8, a=8, qb=768, kb=768, vb=768, zb=768, ga=1024, gb=1024)
COL_2 = {}
_n = 0
for _k, _w in SPLITS_2.items():
    COL_2[_k] = _n
    _n += _w
H = 8
CONV = 4
CH = 64
N_CH = S // CH
LEVELS = 6
GROUPS = 3
DILATION = (1, 4, 16)


def norm_rows(nc, x, gain_row, work, small):
    gain, scaled_x = work[:, 0, :], work[:, 1:3, :]
    ss, ms, root, rstd = (small[:, 4 * i:4 * i + 4] for i in range(4))
    with stage(nc, "gain_landed squared mean_ready root_ready dve_own") as (
            gain_landed, squared, mean_ready, root_ready, dve_own), nc.Block() as block:
        @block.sync
        def _(sp):
            sp.dma_start(gain, gain_row.to_broadcast([P, D])).then_inc(gain_landed, 16)

        @block.scalar
        def _(act):
            for t in range(T):
                if t >= 2:
                    act.wait_ge(squared, t - 1)
                act.activation(scaled_x[:, t % 2, :], x[:, t, :], ACT.Square,
                               accum_out=ss[:, t:t + 1]).then_inc(squared, 1)
            act.wait_ge(mean_ready, 1)
            act.activation(root, ms, ACT.Sqrt).then_inc(root_ready, 1)

        @block.vector
        def _(dve):
            own = Chain(dve, dve_own)
            dve.wait_ge(squared, T)
            dve.tensor_scalar(ms, ss, 1.0 / D, EPS, ALU.mult, ALU.add).then_inc(mean_ready, 1)
            dve.wait_ge(root_ready, 1)
            own(dve.reciprocal(rstd, root))
            dve.wait_ge(gain_landed, 16)
            for t in range(T):
                own(dve.scalar_tensor_tensor(out=x[:, t, :], in0=x[:, t, :], scalar=rstd[:, t:t + 1], in1=gain,
                                             op0=ALU.mult, op1=ALU.mult))


def second_constants(nc, decay_mask, level_masks, pick, window_incl, residues):
    with stage(nc, "filled masked") as (filled, masked), nc.Block() as block:
        @block.vector
        def _(dve):
            own = Chain(dve, filled)
            own(dve.memset(decay_mask[:], 0.0))
            own(dve.memset(level_masks[:], 0.0))
            for i in range(LEVELS):
                s = 1 << i
                own(dve.memset(level_masks[:, i, :].rearrange("p (j a w) -> p j a w", a=2, w=s)[:, :, 1, :], 1.0))
            own(dve.memset(window_incl[:], 0.0))
            own(dve.memset(residues[:], 0.0))
            own(dve.memset(pick[:], 0.0))
            own(dve.memset(pick[:, 15:16], 1.0))

        @block.gpsimd
        def _(pool):
            pool.wait_ge(filled, 6 + LEVELS)
            own = Chain(pool, masked)

            def keep(view, pattern, base, channel, fill):
                own(pool.affine_select(out=view, in_=view, compare_op=ALU.is_ge, fill=fill, base=base,
                                       pattern=pattern, channel_multiplier=channel))
            keep(decay_mask[:], [[1, P]], 0, -1, MASKED)
            keep(decay_mask[:].rearrange("p (j w) -> p j w", w=CH), [[-CH, 2], [0, CH]], 0, 1, MASKED)
            for i in range(LEVELS):
                s = 1 << i
                half = level_masks[:, i, :].rearrange("p (j a w) -> p j a w", a=2, w=s)[:, :, 1, :]
                keep(half, [[-2 * s, P // (2 * s)], [0, s]], 0, 1, 0.0)
                keep(half, [[2 * s, P // (2 * s)], [0, s]], s - 1, -1, 0.0)
            keep(window_incl[:], [[1, 2 * P]], 0, -1, MASKED)
            keep(window_incl[:], [[-1, 2 * P]], P, 1, MASKED)
            keep(residues[:], [[-1, P]], 0, 1, MASKED)
            keep(residues[:].rearrange("p (j w) -> p j w", w=32), [[32, 4], [0, 32]], 31, -1, MASKED)


def modulation(nc, psum, weights, a, ident, ones, work, cols, conv_cols, modulated, gate_row, head_vecs, n_ada):
    vec_rows, conv_rows, silu_c, silu_pair, gate_bias = work
    n_cols = 41
    with stage(nc, "landed conv_landed bias_landed head_landed cleared turned dve_own silu_ready high low") as (
            landed, conv_landed, bias_landed, head_landed, cleared, turned, dve_own, silu_ready,
            high, low), nc.Block() as block:
        @block.sync
        def _(sp):
            sp.wait_ge(cleared, 1)
            for r, name in ((0, "norm_w_2"), (8, "c_2"), (16, "ada_b_2"), (40, "dn_norm_w_2")):
                n = a[name].shape[1] // P
                sp.dma_start(vec_rows[r:r + n, :],
                             a[name].rearrange("o (r c) -> (o r) c", c=P)).then_inc(landed, 16)
            sp.dma_start(conv_rows[:], a["conv_w_2"].rearrange("o j (r c) -> (o j r) c", c=P)).then_inc(conv_landed, 16)
            weights.send(sp, n_ada)
            sp.dma_start(gate_bias[:], a["ada_b_2"][:, 2 * D:3 * D].to_broadcast([P, D])).then_inc(bias_landed, 16)
            for i, name in enumerate(("a_log_2", "dt_bias_2")):
                sp.dma_start(head_vecs[:, i:i + 1], a[name].rearrange("o (h u) -> (o h) u", u=1)).then_inc(head_landed, 16)
            sp.wait_ge(head_landed, 32)

        @block.tensor
        def _(pe):
            pe.wait_ge(landed, 64)
            pe.wait_ge(conv_landed, 16)
            pe.transpose(psum[:, 3, 0:64], vec_rows[:], ident[0:64, 0:64])
            pe.transpose(psum[:, 3, 64:160], conv_rows[:], ident[0:96, 0:96]).then_inc(turned, 1)
            pe.wait_ge(low, KD)
            for p in range(2 * D // 256):
                for i in range(2):
                    w = weights.take(pe)
                    for h in range(2):
                        for kk in range(KD // 2):
                            k = i * (KD // 2) + kk
                            mm = product(pe, psum[:, h, 2 * p:2 * p + 2], [w[j][:, kk, h * P:(h + 1) * P] for j in (0, 1)],
                                         [silu_pair[:, k, j, 0:2] for j in (0, 1)], start=(k == 0), stop=(k == KD - 1))
                    weights.used(mm)
            for p in range(D // 256):
                for i in range(2):
                    w = weights.take(pe)
                    for kk in range(KD // 2):
                        k = i * (KD // 2) + kk
                        mm = product(pe, psum[:, 4 + p // 2, 256 * (p % 2):256 * (p % 2 + 1)],
                                     [silu_pair[:, k, j, :] for j in (0, 1)], [w[j][:, kk, :] for j in (0, 1)],
                                     start=(k == 0), stop=(k == KD - 1))
                    weights.used(mm)

        @block.scalar
        def _(act):
            act.wait_ge(dve_own, 2)
            act.activation(silu_c[:], cols[:, 8:16], ACT.Silu).then_inc(silu_ready, 1)
            act.wait_ge(silu_ready, 1)
            for k in range(KD):
                act.activation(silu_pair[:, k, 0, :], ones[:], ACT.Copy, scale=silu_c[:, k:k + 1]).then_inc(high, 1)
            for i in range(n_ada):
                weights.high(act, i)

        @block.vector
        def _(dve):
            own = Chain(dve, dve_own)
            dve.memset(vec_rows[:], 0.0).then_inc(cleared, 1)
            dve.wait_ge(turned, 1)
            own(dve.tensor_copy(cols[:], psum[:, 3, 0:64]))
            own(dve.tensor_copy(conv_cols[:], psum[:, 3, 64:160]))
            dve.wait_ge(silu_ready, 1)
            for k in range(KD):
                dve.wait_ge(high, k + 1)
                dve.scalar_tensor_tensor(out=silu_pair[:, k, 1, :], in0=ones[:], scalar=silu_c[:, k:k + 1],
                                         in1=silu_pair[:, k, 0, :].bitcast(F32), op0=ALU.mult,
                                         op1=ALU.subtract).then_inc(low, 1)
            own(dve.tensor_scalar(cols[:, 48:56], cols[:, 24:32], 1.0, None, ALU.add))
            for i in range(n_ada):
                weights.low(dve, i)
            dve.wait_ge(weights.items_done, n_ada)
            for h in range(2):
                own(dve.tensor_tensor(modulated[:, 8 + h:16:2], psum[:, h, 0:8:2], cols[:, 16 + h:24:2], ALU.add))
                own(dve.tensor_tensor(modulated[:, h:8:2], psum[:, h, 8:16:2], cols[:, 48 + h:56:2], ALU.add))
            own(dve.tensor_tensor(modulated[:, 0:8], modulated[:, 0:8], cols[:, 0:8], ALU.mult))
            dve.wait_ge(bias_landed, 16)
            for i in range(2):
                own(dve.tensor_tensor(gate_row[:, 512 * i:512 * (i + 1)], psum[:, 4 + i, :],
                                      gate_bias[:, 512 * i:512 * (i + 1)], ALU.add))


def conv_projection(nc, psum, weights, turned_x, qkv, rows, conv_cols, pick, head_vecs, work, end):
    before, squares, soft = work
    NB, SQ, BETA, DECAY = 4, 7, 5, 6
    NQ = 4
    CHUNKS = 3 * H
    with stage(nc, "copied convolved activated squared summed dve_own rows_exp rows_log "
                   "a_ready beta_ready zeroed") as (
            copied, convolved, activated, squared, summed, dve_own, rows_exp, rows_log,
            a_ready, beta_ready, zeroed), nc.Block() as block:
        @block.sync
        def _(sp):
            weights.send(sp, end)

        @block.tensor
        def _(pe):
            w = weights.take(pe)
            for bank, c in ((BETA, 0), (DECAY, H)):
                for k in range(KD):
                    mm = product(pe, psum[0:H, bank, :], [w[j][:, k, c:c + H] for j in (0, 1)],
                                 [turned_x[:, k, j, :] for j in (0, 1)], start=(k == 0), stop=(k == KD - 1))
            weights.used(mm)

            def sum_squares(c):
                pe.wait_ge(squared, c + 1)
                pe.matmul(psum[0:16, SQ, :], pick[:, 15 - c:31 - c], squares[:, c % NQ, :], start=(c == 0),
                          stop=(c == 2 * H - 1)).then_inc(summed, 1)

            for c in range(0, CHUNKS, 2):
                if c >= NB:
                    pe.wait_ge(copied, c - NB + 2)
                product_by_channels(pe, psum, (c % NB, c % NB + 1), weights, turned_x, KD)
                if 4 <= c < 2 * H + 4:
                    sum_squares(c - 4)
                    sum_squares(c - 3)

        start = end - CHUNKS

        @block.scalar
        def _(act):
            weights.high(act, start - 1)
            act.wait_ge(zeroed, 1)

            def silu(c):
                act.wait_ge(convolved, c + 1)
                act.activation(qkv[:, c, :], before[:, c % 3, 3:3 + S], ACT.Silu).then_inc(activated, 1)

            for c in range(CHUNKS + 1):
                if c < CHUNKS:
                    weights.high(act, start + c + 1)
                    if c % 2 == 0:
                        act.wait_ge(weights.items_done, start + c + 2)
                    if c >= 3:
                        act.wait_ge(activated, c - 2)
                    act.activation(before[:, c % 3, 3:3 + S], psum[:, c % NB, :], ACT.Copy).then_inc(copied, 1)
                if c >= 1:
                    silu(c - 1)
            act.wait_ge(a_ready, 1)
            act.activation(soft[:, 1, :], soft[:, 1, :], ACT.Exp, scale=-1.0).then_inc(rows_exp, 1)
            act.activation(head_vecs[:, 2:3], head_vecs[:, 0:1], ACT.Exp).then_inc(rows_exp, 1)
            act.wait_ge(a_ready, 2)
            act.activation(soft[:, 1, :], soft[:, 1, :], ACT.Ln).then_inc(rows_log, 1)
            act.wait_ge(weights.items_done, start)
            act.activation(rows[:, 0, :], psum[0:H, BETA, :], ACT.Sigmoid).then_inc(beta_ready, 1)

        def square(dve, c):
            dve.wait_ge(activated, c + 1)
            if c >= NQ:
                dve.wait_ge(summed, c - NQ + 1)
            dve.tensor_tensor(squares[:, c % NQ, :], qkv[:, c, :], qkv[:, c, :], ALU.mult).then_inc(squared, 1)

        @block.vector
        def _(dve):
            own = Chain(dve, dve_own)
            dve.memset(before[:, :, 0:3], 0.0).then_inc(zeroed, 1)
            weights.low(dve, start - 1)
            for c in range(CHUNKS):
                weights.low(dve, start + c + 1)
                dve.wait_ge(copied, c + 1)
                b = before[:, c % 3, :]
                acc = squares[:, NQ + c % 2, :]
                own(dve.tensor_scalar(acc, b[:, 0:S], conv_cols[:, c:c + 1], None, ALU.mult))
                for j in (1, 2):
                    own(dve.scalar_tensor_tensor(out=acc, in0=b[:, j:j + S], scalar=conv_cols[:, 24 * j + c:24 * j + c + 1],
                                                 in1=acc, op0=ALU.mult, op1=ALU.add))
                dve.scalar_tensor_tensor(out=b[:, 3:3 + S], in0=b[:, 3:3 + S],
                                         scalar=conv_cols[:, 72 + c:73 + c], in1=acc, op0=ALU.mult,
                                         op1=ALU.add).then_inc(convolved, 1)
                if c >= 1 and c - 1 < 2 * H:
                    square(dve, c - 1)
            own(dve.tensor_scalar(soft[:, 0, :], psum[0:H, DECAY, :], head_vecs[:, 1:2], None, ALU.add))
            dve.scalar_tensor_tensor(out=soft[:, 1, :], in0=soft[:, 0, :], scalar=-1.0, in1=soft[:, 0, :],
                                     op0=ALU.mult, op1=ALU.max).then_inc(a_ready, 1)
            dve.wait_ge(rows_exp, 2)
            dve.tensor_scalar(soft[:, 1, :], soft[:, 1, :], 1.0, None, ALU.add).then_inc(a_ready, 1)
            own(dve.tensor_scalar(head_vecs[:, 3:4], head_vecs[:, 2:3], -1.0, None, ALU.mult))
            dve.wait_ge(rows_log, 1)
            own(dve.scalar_tensor_tensor(out=soft[:, 0, :], in0=soft[:, 0, :], scalar=0.0, in1=soft[:, 1, :],
                                         op0=ALU.max, op1=ALU.add))
            own(dve.tensor_scalar(rows[:, 1, :], soft[:, 0, :], head_vecs[:, 3:4], None, ALU.mult))



def normalize_and_spread(nc, psum, qkv, rows, ident, onehot, k_tok, v_tok, tok_cols, last_decay, work,
                         row_stats):
    SQ = 7
    norms, = row_stats
    exps, lasts, restart = work
    with stage(nc, "dve_own q_done root_ready spread_done scaled k_turned stored_act stored_dve rows_exp lasts_ready "
                   "rows_turned") as (
            dve_own, q_done, root_ready, spread_done, scaled, k_turned, stored_act, stored_dve, rows_exp, lasts_ready,
            rows_turned), nc.Block() as block:
        @block.scalar
        def _(act):
            act.wait_ge(q_done, 1)
            act.activation(norms[:, 0, :], norms[:, 0, :], ACT.Sqrt).then_inc(root_ready, 1)
            act.wait_ge(lasts_ready, 1)
            act.activation(exps[:, 0, :], rows[:, 1, :], ACT.Exp).then_inc(rows_exp, 1)
            act.activation(exps[:, 1, :], exps[:, 1, :], ACT.Exp).then_inc(rows_exp, 1)
            act.activation(lasts[:], lasts[:], ACT.Exp).then_inc(rows_exp, 1)
            for i in range(16):
                act.wait_ge(k_turned, i + 1)
                if i % 2 == 0:
                    h = i % H
                    out = (k_tok if i < H else v_tok)[:, :, h * P:(h + 1) * P]
                    act.activation(out, psum[:, i % 4, :].rearrange("p (t c) -> p t c", t=T), ACT.Copy
                                   ).then_inc(stored_act, 1)

        @block.vector
        def _(dve):
            own = Chain(dve, dve_own)
            dve.tensor_scalar(norms[:, 0, :], psum[0:16, SQ, :], EPS, None, ALU.add).then_inc(q_done, 1)
            own(dve.memset(restart[:], 1.0))
            own(dve.memset(restart[:].rearrange("p (n c) -> p n c", c=CH)[:, :, 0:1], 0.0))
            own(dve.tensor_tensor_scan(exps[:, 0, :], restart[:], rows[:, 1, :], 0.0, ALU.mult, ALU.add))
            own(dve.tensor_copy(rows[:, 1, :], exps[:, 0, :]))
            by_chunk = rows[:, 1, :].rearrange("p (n c) -> p n c", c=CH)
            own(dve.tensor_copy(lasts[:].unsqueeze(2), by_chunk[:, :, CH - 1:CH]))
            dve.tensor_tensor(exps[:, 1, :].rearrange("p (n c) -> p n c", c=CH),
                              spread(lasts[:], 2, CH), by_chunk, ALU.subtract).then_inc(lasts_ready, 1)
            dve.wait_ge(root_ready, 1)
            own(dve.reciprocal(norms[:, 1, :], norms[:, 0, :]))
            for c in range(2 * H):
                dve.wait_ge(spread_done, c + 1)
                if c < H:
                    dve.scalar_tensor_tensor(out=qkv[:, c, :], in0=qkv[:, c, :], scalar=float(P) ** -0.5,
                                             in1=psum[:, 4 + c % 3, :], op0=ALU.mult, op1=ALU.mult).then_inc(scaled, 1)
                else:
                    dve.tensor_tensor(qkv[:, c, :], qkv[:, c, :], psum[:, 4 + c % 3, :], ALU.mult).then_inc(scaled, 1)
            for i in range(16):
                dve.wait_ge(k_turned, i + 1)
                if i % 2 == 1:
                    h = i % H
                    out = (k_tok if i < H else v_tok)[:, :, h * P:(h + 1) * P]
                    dve.tensor_copy(out, psum[:, i % 4, :].rearrange("p (t c) -> p t c", t=T)).then_inc(stored_dve, 1)
            dve.wait_ge(rows_turned, 1)
            own(dve.tensor_copy(tok_cols[:].rearrange("p a t h -> p (a t h)"), psum[:, 4, 0:4 * T * H]))
            own(dve.tensor_tensor(tok_cols[:, 2], tok_cols[:, 2], tok_cols[:, 0], ALU.mult))
            own(dve.tensor_copy(last_decay[:].rearrange("p h n -> p (h n)"), psum[:, 5, 0:H * N_CH]))

        @block.tensor
        def _(pe):
            pe.wait_ge(dve_own, 6)
            for c in range(2 * H):
                if c >= 3:
                    pe.wait_ge(scaled, c - 2)
                pe.matmul(psum[:, 4 + c % 3, :], onehot[0:16, c, :], norms[:, 1, :], start=True,
                          stop=True).then_inc(spread_done, 1)
            for i in range(16):
                if i < H:
                    pe.wait_ge(scaled, H + i + 1)
                if i >= 4:
                    if i % 2 == 0:
                        pe.wait_ge(stored_act, (i - 4) // 2 + 1)
                    else:
                        pe.wait_ge(stored_dve, (i - 4) // 2 + 1)
                for t in range(T):
                    mm = pe.transpose(psum[:, i % 4, t * P:(t + 1) * P], qkv[:, H + i, t * P:(t + 1) * P], ident[:])
                mm.then_inc(k_turned, 1)
            pe.wait_ge(scaled, 2 * H)
            pe.wait_ge(rows_exp, 3)
            for i, src in enumerate((rows[:, 0, :], rows[:, 1, :], exps[:, 0, :], exps[:, 1, :])):
                for t in range(T):
                    o = (i * T + t) * H
                    pe.transpose(psum[:, 4, o:o + H], src[:, t * P:(t + 1) * P], ident[0:H, 0:H])
            for h in range(H):
                mm = pe.matmul(psum[:, 5, h * N_CH:(h + 1) * N_CH], onehot[0:H, h, :], lasts[:], start=True, stop=True)
            mm.then_inc(rows_turned, 1)


def delta_prepare(nc, psum, q_t, k_t, attn_t, k_tok, v_tok, rows, tok_cols, decay_mask, level_masks, ident, onehot,
                  sbx):
    G, HG = 2, 4
    dec, lt, x_m, x_t, y = (sbx(n, [P, G, HG * P]) for n in ("decays", "lower_t", "inverse", "inverse_t", "y"))
    eg = y
    lms = sbx("level_lower", [P, G, 2, HG * P])
    heads = lambda ap: ap.rearrange("p (h c) -> p h c", h=HG)
    ML = LEVELS - 1
    order = [(t, g) for t in range(T) for g in range(G)]
    with stage(nc, "formed argued decayed exp_ready attn_ready lower_ready started level_ready flipped inverse_ready y_done y_copied "
                   "z_done refined v_ready k_ready solved stored dve_own pool_own q_decayed") as (
            formed, argued, decayed, exp_ready, attn_ready, lower_ready, started, level_ready, flipped, inverse_ready,
            y_done, y_copied, z_done, refined, v_ready, k_ready, solved, stored, dve_own, pool_own,
            q_decayed), nc.Block() as block:
        @block.tensor
        def _(pe):
            for t in range(T):
                tile = slice(t * P, (t + 1) * P)
                for g in range(G):
                    i = t * G + g
                    if t:
                        pe.wait_ge(stored, i - 1)
                    b = 4 * g
                    for hh in range(HG):
                        h = HG * g + hh
                        c = slice(hh * P, (hh + 1) * P)
                        pe.matmul(psum[:, b, c], onehot[0:H, h, :], rows[:, 1, tile], start=True, stop=True)
                        pe.matmul(psum[:, b + 1, c], onehot[0:H, h, :], rows[:, 0, tile], start=True, stop=True)
                        pe.matmul(psum[:, b + 2, c], k_t[:, h, tile], k_t[:, h, tile], start=True, stop=True)
                        mm = pe.matmul(psum[:, b + 3, c], k_t[:, h, tile], q_t[:, h, tile], start=True, stop=True)
                    mm.then_inc(formed, 1)
                for g in range(G):
                    pe.wait_ge(started, t * G + g + 1)
                    pe.wait_ge(exp_ready, t * G + g + 1)
                    for hh in range(HG):
                        c = slice(hh * P, (hh + 1) * P)
                        mm = pe.transpose(psum[:, 4 * g, c], x_t[:, g, c], ident[:])
                    mm.then_inc(flipped, 1)
                for lv in range(ML):
                    for g in range(G):
                        i = (t * ML + lv) * G + g
                        pe.wait_ge(level_ready, i + 1)
                        if lv == 0:
                            pe.wait_ge(inverse_ready, t * G + g + 1)
                        else:
                            pe.wait_ge(refined, i - G + 1)
                        for hh in range(HG):
                            c = slice(hh * P, (hh + 1) * P)
                            mm = pe.matmul(psum[:, 4 * g + 1, c], lms[:, g, lv % 2, c], x_m[:, g, c], start=True, stop=True)
                        mm.then_inc(y_done, 1)
                    for g in range(G):
                        i = (t * ML + lv) * G + g
                        pe.wait_ge(y_copied, i + 1)
                        for hh in range(HG):
                            c = slice(hh * P, (hh + 1) * P)
                            mm = pe.matmul(psum[:, 4 * g + 2, c], y[:, g, c], x_t[:, g, c], start=True, stop=True)
                            if lv < ML - 1:
                                mm = pe.matmul(psum[:, 4 * g + 3, c], x_t[:, g, c], y[:, g, c], start=True, stop=True)
                        mm.then_inc(z_done, 1)
                for g in range(G):
                    i = t * G + g
                    pe.wait_ge(refined, (t * ML + ML - 1) * G + g + 1)
                    pe.wait_ge(v_ready, i + 1)
                    pe.wait_ge(k_ready, i + 1)
                    for hh in range(HG):
                        c = slice(hh * P, (hh + 1) * P)
                        pe.matmul(psum[:, 4 * g, c], x_t[:, g, c], dec[:, g, c], start=True, stop=True)
                        mm = pe.matmul(psum[:, 4 * g + 1, c], lt[:, g, c], x_t[:, g, c], start=True, stop=True)
                    mm.then_inc(solved, 1)

        @block.scalar
        def _(act):
            for t in range(T):
                tile = slice(t * P, (t + 1) * P)
                for g in range(G):
                    i = t * G + g
                    act.wait_ge(argued, i + 1)
                    act.activation(dec[:, g, :], dec[:, g, :], ACT.Exp).then_inc(decayed, 1)
                    act.activation(eg[:, g, :], psum[:, 4 * g, :], ACT.Exp).then_inc(exp_ready, 1)
                for g in range(G):
                    act.wait_ge(flipped, t * G + g + 1)
                    act.activation(x_m[:, g, :], psum[:, 4 * g, :], ACT.Copy).then_inc(inverse_ready, 1)
                for lv in range(ML):
                    for g in range(G):
                        i = (t * ML + lv) * G + g
                        act.wait_ge(y_done, i + 1)
                        if lv == 0:
                            act.wait_ge(q_decayed, t * G + g + 1)
                        act.activation(y[:, g, :], psum[:, 4 * g + 1, :], ACT.Copy).then_inc(y_copied, 1)
                for g in range(G):
                    i = t * G + g
                    act.wait_ge(solved, i + 1)
                    act.activation(v_tok[:, t, HG * g * P:HG * (g + 1) * P], psum[:, 4 * g, :], ACT.Copy)
                    act.activation(k_t[:, HG * g:HG * (g + 1), tile], heads(psum[:, 4 * g + 1, :]),
                                   ACT.Copy).then_inc(stored, 1)

        @block.vector
        def _(dve):
            own = Chain(dve, dve_own)
            for t in range(T):
                for g in range(G):
                    i = t * G + g
                    dve.wait_ge(formed, i + 1)
                    if t:
                        dve.wait_ge(solved, i - 1)
                    cols = tok_cols[:, 1, t, HG * g:HG * (g + 1)]
                    own(dve.tensor_tensor(heads(dec[:, g, :]), heads(psum[:, 4 * g, :]), spread(cols, 2, P), ALU.subtract))
                    dve.tensor_tensor(heads(dec[:, g, :]), heads(dec[:, g, :]), spread(decay_mask[:], 1, HG),
                                      ALU.add).then_inc(argued, 1)
                for g in range(G):
                    i = t * G + g
                    dve.wait_ge(decayed, i + 1)
                    dve.tensor_tensor(attn_t[:, t, HG * g * P:HG * (g + 1) * P], psum[:, 4 * g + 3, :],
                                      dec[:, g, :], ALU.mult).then_inc(attn_ready, 1)
                    own(dve.tensor_tensor(lt[:, g, :], psum[:, 4 * g + 2, :], dec[:, g, :], ALU.mult))
                    own(dve.tensor_tensor(lt[:, g, :], lt[:, g, :], psum[:, 4 * g + 1, :], ALU.mult))
                    dve.sem_inc(lower_ready, 1)
                    own(dve.tensor_tensor(heads(x_t[:, g, :]), heads(lt[:, g, :]), spread(level_masks[:, 0, :], 1, HG), ALU.mult))
                    dve.tensor_tensor(heads(x_t[:, g, :]), spread(ident[:], 1, HG), heads(x_t[:, g, :]),
                                      ALU.subtract).then_inc(started, 1)
                for lv in range(ML):
                    for g in range(G):
                        i = (t * ML + lv) * G + g
                        dve.wait_ge(z_done, i + 1)
                        if lv < ML - 1:
                            own(dve.tensor_tensor(x_m[:, g, :], x_m[:, g, :], psum[:, 4 * g + 3, :], ALU.subtract))
                        dve.tensor_tensor(x_t[:, g, :], x_t[:, g, :], psum[:, 4 * g + 2, :], ALU.subtract).then_inc(refined, 1)

        @block.gpsimd
        def _(pool):
            own = Chain(pool, pool_own)
            for t in range(T):
                tile = slice(t * P, (t + 1) * P)
                for lv in range(ML):
                    for g in range(G):
                        i = (t * ML + lv) * G + g
                        if lv == 0:
                            pool.wait_ge(lower_ready, t * G + g + 1)
                        if i - 2 * G >= 0:
                            pool.wait_ge(y_done, i - 2 * G + 1)
                        pool.tensor_tensor(heads(lms[:, g, lv % 2, :]), heads(lt[:, g, :]),
                                           spread(level_masks[:, lv + 1, :], 1, HG), ALU.mult).then_inc(level_ready, 1)
                    if lv == 0:
                        for g in range(G):
                            i = t * G + g
                            hs = slice(HG * g, HG * (g + 1))
                            pool.wait_ge(exp_ready, i + 1)
                            pool.tensor_tensor(q_t[:, hs, tile], q_t[:, hs, tile], heads(eg[:, g, :]), ALU.mult).then_inc(q_decayed, 1)
                            pool.wait_ge(attn_ready, i + 1)
                            pool.tensor_tensor(heads(dec[:, g, :]), heads(v_tok[:, t, HG * g * P:HG * (g + 1) * P]),
                                               spread(tok_cols[:, 0, t, hs], 2, P), ALU.mult).then_inc(v_ready, 1)
                for g in range(G):
                    i = t * G + g
                    hs = slice(HG * g, HG * (g + 1))
                    kk = heads(k_tok[:, t, HG * g * P:HG * (g + 1) * P])
                    pool.wait_ge(level_ready, (t * ML + ML - 1) * G + g + 1)
                    pool.wait_ge(started, i + 1)
                    pool.tensor_tensor(heads(lt[:, g, :]), kk, spread(tok_cols[:, 2, t, hs], 2, P), ALU.mult).then_inc(k_ready, 1)
                    pool.wait_ge(k_ready, i + 1)
                    own(pool.tensor_tensor(kk, kk, spread(tok_cols[:, 3, t, hs], 2, P), ALU.mult))


def delta_scan(nc, psum, q_t, w_t, attn_t, k_tok, u, last_decay, state):
    with stage(nc, "read_state v_ready products o_stored state_ready dve_own") as (
            read_state, v_ready, products, o_stored, state_ready, dve_own), nc.Block() as block:
        def place(n):
            return n // 2, CH * (n % 2)

        @block.tensor
        def _(pe):
            for n in range(N_CH):
                t, b = place(n)
                chunk = slice(t * P + b, t * P + b + CH)
                if n:
                    pe.wait_ge(state_ready, n)
                    for h in range(H):
                        c = slice((h % 4) * P, (h % 4 + 1) * P)
                        mm = pe.matmul(psum[b:b + CH, h // 4, c], w_t[:, h, chunk], state[:, h, :], start=True, stop=True)
                    mm.then_inc(read_state, 1)
                    pe.wait_ge(o_stored, n)
                    pe.wait_ge(v_ready, n)
                for h in range(H):
                    c = slice((h % 4) * P, (h % 4 + 1) * P)
                    hc = slice(h * P, (h + 1) * P)
                    if n:
                        pe.matmul(psum[b:b + CH, 2 + h // 4, c], q_t[:, h, chunk], state[:, h, :], start=True, stop=False)
                    pe.matmul(psum[b:b + CH, 2 + h // 4, c], attn_t[b:b + CH, t, h * P + b:h * P + b + CH],
                              u[b:b + CH, t, hc], start=(n == 0), stop=True)
                    mm = pe.matmul(psum[:, 4 + h // 4, c], k_tok[b:b + CH, t, hc], u[b:b + CH, t, hc], start=True, stop=True)
                mm.then_inc(products, 1)

        @block.vector
        def _(dve):
            own = Chain(dve, dve_own)
            for n in range(N_CH):
                t, b = place(n)
                if n:
                    dve.wait_ge(read_state, n)
                    for j in range(2):
                        c = slice(512 * j, 512 * (j + 1))
                        ins = dve.tensor_tensor(u[b:b + CH, t, c], u[b:b + CH, t, c], psum[b:b + CH, j, :], ALU.subtract)
                        if j == 0:
                            own(ins)
                        else:
                            ins.then_inc(v_ready, 1)
                dve.wait_ge(products, n + 1)
                flat = state[:].rearrange("p h c -> p (h c)")
                if n:
                    own(dve.tensor_tensor(state[:], state[:], spread(last_decay[:, :, n], 2, P), ALU.mult))
                for j in range(2):
                    c = slice(512 * j, 512 * (j + 1))
                    if n:
                        ins = dve.tensor_tensor(flat[:, c], flat[:, c], psum[:, 4 + j, :], ALU.add)
                    else:
                        ins = dve.tensor_copy(flat[:, c], psum[:, 4 + j, :])
                    if j == 0:
                        own(ins)
                    else:
                        ins.then_inc(state_ready, 1)

        @block.scalar
        def _(act):
            for n in range(N_CH):
                t, b = place(n)
                act.wait_ge(products, n + 1)
                for j in range(2):
                    ins = act.activation(attn_t[b:b + CH, t, 512 * j:512 * (j + 1)], psum[b:b + CH, 2 + j, :], ACT.Copy)
                ins.then_inc(o_stored, 1)


def channel_products(nc, psum, weights, pair, chunks, epilogues, also=None, names=""):
    n = len(epilogues)
    start = weights.taken
    end = start + n
    act_before = [sum(1 for e in epilogues[:c] if e[0] == "act") for c in range(n + 1)]
    dve_before = [c - act_before[c] for c in range(n + 1)]
    with stage(nc, "stored_act stored_dve dve_own " + names) as sems, nc.Block() as block:
        stored_act, stored_dve, dve_own = sems[0:3]

        @block.sync
        def _(sp):
            weights.send(sp, end)

        @block.tensor
        def _(pe):
            for c in range(0, n, 2):
                if c >= 8:
                    if act_before[c - 6]:
                        pe.wait_ge(stored_act, act_before[c - 6])
                    if dve_before[c - 6]:
                        pe.wait_ge(stored_dve, dve_before[c - 6])
                product_by_channels(pe, psum, (c % 8, c % 8 + 1), weights, pair, chunks)

        @block.scalar
        def _(act):
            for c, e in enumerate(epilogues):
                weights.high(act, start + c)
                if also and c < len(also[0]):
                    also[0][c](act, sems[3:])
                weights.high(act, start + c + 1)
                if e[0] == "act":
                    act.wait_ge(weights.items_done, start + 2 * (c // 2) + 2)
                    act.activation(e[2], e[3](psum[:, c % 8, :]), e[1]).then_inc(stored_act, 1)

        @block.vector
        def _(dve):
            own = Chain(dve, dve_own)
            for c, e in enumerate(epilogues):
                weights.low(dve, start + c)
                if also and c < len(also[1]):
                    also[1][c](dve, sems[3:])
                weights.low(dve, start + c + 1)
                if e[0] == "dve":
                    dve.wait_ge(weights.items_done, start + 2 * (c // 2) + 2)
                    for s in e[1][:-1]:
                        own(s(dve, psum[:, c % 8, :]))
                    e[1][-1](dve, psum[:, c % 8, :]).then_inc(stored_dve, 1)


def same(bank):
    return bank


def permuted(view, group):
    if group == 0:
        return view
    return view.rearrange("p (s r) -> p r s", r=DILATION[group])


def in_order(view, group):
    if group == 0:
        return view
    return view.rearrange("p (r s) -> p r s", r=DILATION[group])


def second_part(nc, psum, x, weights, consts, a):
    ident, ones, causal, window, onehot = consts

    with ExitStack() as all2:
        def sb(name, shape, ctx=all2, dtype=F32):
            return ctx.enter_context(nc.sbuf_tensor(name, shape, dtype))

        one = lambda name: a[name].rearrange("o r c -> (o r) c")
        ada, win, wa, wb, wout = (one(n) for n in ("ada_w_2", "w_in_2", "w_proj_a_2", "w_proj_b_2", "w_out_2"))
        KB = wb.shape[0] // P

        def project(*names):
            return [i for n in names for i in for_channels(win, KD, COL_2[n], COL_2[n] + SPLITS_2[n])]

        items = for_channels(ada, KD, 0, 3 * D)
        n_ada = len(items)
        items.append(rows(win, 0, KD, COL_2["beta"], COL_2["beta"] + 16))
        items += project("qa", "ka", "va")
        n_conv = len(items)
        items += project("za", "ga") + for_channels(wa, KD, 0, D)
        items += project("qb", "kb", "vb", "zb", "gb") + for_channels(wb, KB, 0, D)
        out_items = for_tokens(wout, KD, 0, 512) + for_tokens(wout, KD, 512, D)
        weights.restart(items + out_items)

        small = sb("small_2", [P, 32])
        cols = sb("cols_2", [P, 64])
        conv_cols = sb("conv_cols", [P, CONV * 3 * H])
        modulated = sb("modulated", [P, 16])
        gate_row = sb("gate_row", [P, D])
        head_vecs = sb("head_vecs", [H, 4])
        window_incl = sb("window_incl", [P, 2 * P])
        residues = sb("residues", [P, P])
        with ExitStack() as ctx:
            norm_rows(nc, x, a["final_norm"].rearrange("(o d) -> o d", o=1), sb("norm_work", [P, 3, D], ctx), small)
            work = (sb("vec_rows_2", [64, P], ctx), sb("conv_rows", [96, P], ctx), sb("silu_c", [P, KD], ctx),
                    sb("silu_pair", [P, KD, 2, P], ctx, F32R), sb("gate_bias", [P, D], ctx))
            modulation(nc, psum, weights, a, ident, ones, work, cols, conv_cols, modulated, gate_row, head_vecs, n_ada)

        qkv = sb("qkv", [P, 3 * H, S])
        part = [qkv[:, H * i:H * (i + 1), :] for i in range(3)]
        token_major = [p.rearrange("p k s -> p (k s)").rearrange("p (t c) -> p t c", t=T) for p in part]
        attn_t = token_major[2]
        with ExitStack() as delta:
            decay_mask = sb("decay_mask", [P, P], delta)
            level_masks = sb("level_masks", [P, LEVELS, P], delta)
            pick = sb("pick", [P, 31], delta)
            second_constants(nc, decay_mask, level_masks, pick, window_incl, residues)
            heads_rows = sb("heads_rows", [H, 2, S], delta)
            tok_cols = sb("tok_cols", [P, 4, T, H], delta)
            last_decay = sb("last_decay", [P, H, N_CH], delta)
            with ExitStack() as ctx:
                turned_x = sb("turned_x2", [P, KD, 2, S], ctx, F32R)
                squares = sb("squares", [P, 6, S], ctx)
                norm_and_turn(nc, psum, x, token_major[2], modulated[:, 0:8], turned_x, ident, small,
                              bias=modulated[:, 8:16], work=squares)
                conv_projection(nc, psum, weights, turned_x, qkv, heads_rows, conv_cols, pick, head_vecs,
                                (sb("before", [P, 3, S + 3], ctx), squares, sb("soft", [H, 2, S], ctx)), n_conv)
            k_tok = sb("k_tok", [P, T, D], delta)
            v_tok = sb("v_tok", [P, T, D], delta)
            with ExitStack() as ctx:
                normalize_and_spread(nc, psum, qkv, heads_rows, ident, onehot, k_tok, v_tok, tok_cols,
                                     last_decay, (sb("exps", [H, 2, S], ctx), sb("lasts", [H, N_CH], ctx),
                                                  sb("restart", [H, S], ctx)),
                                     (sb("norms", [16, 2, S], ctx),))
            with ExitStack() as ctx:
                delta_prepare(nc, psum, part[0], part[1], attn_t, k_tok, v_tok, heads_rows, tok_cols, decay_mask,
                              level_masks, ident, onehot, lambda n, s: sb(n, s, ctx))
            with ExitStack() as ctx:
                delta_scan(nc, psum, part[0], part[1], attn_t, k_tok, v_tok, last_decay,
                           sb("state", [P, H, P], ctx))

        turned_x = sb("turned_x3", [P, KD, 2, S], dtype=F32R)
        norm_and_turn(nc, psum, x, token_major[1], modulated[:, 0:8], turned_x, ident, small,
                      bias=modulated[:, 8:16], work=qkv)
        merged = part[2]
        with ExitStack() as ctx:
            o_stats = sb("o_stats", [P, 4, T * H], ctx)
            y_a = part[0]
            junk = token_major[1]

            def square_o(t):
                def step(act, sems):
                    for h in range(H):
                        i = t * H + h
                        act.activation(junk[:, t, h * P:(h + 1) * P], attn_t[:, t, h * P:(h + 1) * P], ACT.Square,
                                       accum_out=o_stats[:, 0, i:i + 1]).then_inc(sems[0], 1)
                return step

            def root_o(act, sems):
                act.wait_ge(sems[1], 1)
                act.activation(o_stats[:, 2, :], o_stats[:, 1, :], ACT.Sqrt).then_inc(sems[2], 1)

            def mean_o(dve, sems):
                dve.wait_ge(sems[0], T * H)
                dve.tensor_scalar(o_stats[:, 1, :], o_stats[:, 0, :], 1.0 / P, EPS, ALU.mult, ALU.add).then_inc(sems[1], 1)

            def norm_o(dve, sems):
                own = Chain(dve, sems[3])
                dve.wait_ge(sems[2], 1)
                own(dve.reciprocal(o_stats[:, 3, :], o_stats[:, 2, :]))
                for t in range(T):
                    o = attn_t[:, t, :].rearrange("p (h c) -> p h c", h=H)
                    own(dve.tensor_tensor(o, o, spread(o_stats[:, 3, t * H:(t + 1) * H], 2, P), ALU.mult))

            nothing = lambda eng, sems: None
            channel_products(nc, psum, weights, turned_x, KD, [("act", ACT.Silu, y_a[:, c, :], same) for c in range(H)],
                             also=([square_o(t) for t in range(T)] + [root_o], [nothing] * T + [mean_o, norm_o]),
                             names="o_squared o_mean o_root o_own")
            y_pair = sb("y_a_pair", [P, KD, 2, S], ctx, F32R)
            with stage(nc, "turned gated high low") as (turned, gated, high, low), nc.Block() as block:
                @block.tensor
                def _(pe):
                    for h in range(H):
                        for t in range(T):
                            mm = pe.transpose(psum[:, h, t * P:(t + 1) * P], attn_t[:, t, h * P:(h + 1) * P], ident[:])
                        mm.then_inc(turned, 1)

                @block.scalar
                def _(act):
                    for h in range(H):
                        act.wait_ge(gated, h + 1)
                        act.activation(y_pair[:, h, 0, :], y_a[:, h, :], ACT.Copy).then_inc(high, 1)

                @block.vector
                def _(dve):
                    def rest(h):
                        dve.wait_ge(high, h + 1)
                        dve.tensor_tensor(y_pair[:, h, 1, :], y_a[:, h, :], y_pair[:, h, 0, :].bitcast(F32),
                                          ALU.subtract).then_inc(low, 1)

                    for h in range(H):
                        dve.wait_ge(turned, h + 1)
                        dve.scalar_tensor_tensor(out=y_a[:, h, :], in0=psum[:, h, :], scalar=cols[:, 40:41],
                                                 in1=y_a[:, h, :], op0=ALU.mult, op1=ALU.mult).then_inc(gated, 1)
                        if h >= 1:
                            rest(h - 1)
                    rest(H - 1)
            gate_a = part[1]
            channel_products(nc, psum, weights, turned_x, KD,
                             [("act", ACT.Sigmoid, gate_a[:, c, :], same) for c in range(KD)])

            def times(c):
                return lambda dve, bank: dve.tensor_tensor(merged[:, c, :], bank, gate_a[:, c, :], ALU.mult)

            channel_products(nc, psum, weights, y_pair, KD, [("dve", [times(c)]) for c in range(KD)])
        with ExitStack() as ctx:
            dilated(nc, psum, weights, turned_x, qkv, merged, KB, window_incl, causal, residues, ident, onehot, sb, ctx)
        split_operand(nc, lambda k: merged[:, k, :], turned_x, KD)
        output_products(nc, psum, x, weights, turned_x, KD, len(out_items) // 2, gate=(gate_row, qkv[:, 0:2, :]))
        with ExitStack() as ctx:
            norm_rows(nc, x, a["final_norm_w_2"].rearrange("(o d) -> o d", o=1), sb("norm_work_2", [P, 3, D], ctx), small)


def dilated(nc, psum, weights, turned_x, free_chunks, merged, KB, window_incl, causal, residues, ident, onehot, sb,
            ctx):
    C = KB
    q, k = (free_chunks[:, C * i:C * (i + 1), :] for i in range(2))
    v_t = sb("v_turned", [P, C, S], ctx)
    v = sb("v_rows", [P, T, C * P], ctx)
    eps = []
    for name, dst in (("q", q), ("k", k), ("v", v_t)):
        for c in range(C):
            g = c // 2
            eps.append(("act", ACT.Copy, in_order(dst[:, c, :], g), lambda bank, g=g: permuted(bank, g)))
    channel_products(nc, psum, weights, turned_x, KD, eps)
    with stage(nc, "turned stored") as (turned, stored), nc.Block() as block:
        @block.tensor
        def _(pe):
            for c in range(C):
                for b in range(T):
                    mm = pe.transpose(psum[:, c, b * P:(b + 1) * P], v_t[:, c, b * P:(b + 1) * P], ident[:])
                mm.then_inc(turned, 1)

        @block.scalar
        def _(act):
            for c in range(C):
                act.wait_ge(turned, c + 1)
                act.activation(v[:, :, c * P:(c + 1) * P], psum[:, c, :].rearrange("p (t c) -> p t c", t=T),
                               ACT.Copy).then_inc(stored, 1)

    y = v_t
    jobs = []
    for g in range(GROUPS):
        for i in range(4):
            c = 2 * g + i // 2
            r = 64 * (i % 2)
            for b in range(T):
                blocks = [b] if g else list(range(max(b - 1, 0), b + 1))
                w = len(blocks) * P
                keys = slice(blocks[0] * P, (b + 1) * P)
                mask = (window_incl[:, 2 * P - w:2 * P], causal[:, S - P:S], residues[:])[g]
                jobs.append(Job([(q[r:r + 64, c, b * P:(b + 1) * P], k[r:r + 64, c, keys])], w, mask, 64 ** -0.5,
                                [v[:, kb, c * P + r:c * P + r + 64] for kb in blocks], r, b * P))
    stores = [(permuted(y[:, c, :], c // 2), lambda bank, g=c // 2: in_order(bank, g), None)
              for c in range(C)]
    stats = sb("stats_2", [P, 5, len(jobs)], ctx)
    with ExitStack() as c2:
        with stage(nc, ATTENTION_SEMS) as sems:
            attention(nc, psum, jobs, stores, ident, sb("probs2", [P, 4, 2 * P], c2),
                      sb("probs_t2", [P, 3, 2 * P], c2), stats, sems)
    z = free_chunks[:, 0:C, :]
    gate_b = free_chunks[:, C:C + KD, :]
    channel_products(nc, psum, weights, turned_x, KD,
                     [("act", ACT.Silu, z[:, c, :], same) for c in range(C)]
                     + [("act", ACT.Sigmoid, gate_b[:, c, :], same) for c in range(KD)])
    with ExitStack() as c2:
        lse = sb("lse", [4, GROUPS, S], c2)
        top = sb("top", [4, 2, S], c2)
        pair = sb("pair", [4, 2, P], c2)
        with stage(nc, "logged lse_ready turned dve_own powered spread_done weighed") as (
                logged, lse_ready, turned, dve_own, powered, spread_done, weighed), nc.Block() as block:
            @block.scalar
            def _(act):
                act.activation(stats[:, 2, :], stats[:, 1, :], ACT.Ln).then_inc(logged, 1)
                act.wait_ge(dve_own, 3 + GROUPS + 2 + GROUPS)
                act.activation(lse[:], lse[:], ACT.Exp).then_inc(powered, 1)

            @block.vector
            def _(dve):
                own = Chain(dve, dve_own)
                dve.wait_ge(logged, 1)
                own(dve.tensor_tensor(stats[:, 3, :], stats[:, 2, :], stats[:, 0, :], ALU.subtract))
                for j in range(2):
                    own(dve.tensor_copy(pair[:, j, :].rearrange("p (a c) -> p a c", a=2),
                                        onehot[0:4, 2 * j:2 * j + 2, 0:64]))
                dve.wait_ge(turned, 1)
                for g in range(GROUPS):
                    own(dve.tensor_copy(lse[:, g, :], psum[0:4, g, :]))
                own(dve.tensor_tensor(top[:, 0, :], lse[:, 0, :], lse[:, 1, :], ALU.max))
                own(dve.tensor_tensor(top[:, 0, :], top[:, 0, :], lse[:, 2, :], ALU.max))
                for g in range(GROUPS):
                    own(dve.tensor_tensor(lse[:, g, :], lse[:, g, :], top[:, 0, :], ALU.subtract))
                dve.wait_ge(powered, 1)
                own(dve.tensor_tensor(top[:, 0, :], lse[:, 0, :], lse[:, 1, :], ALU.add))
                own(dve.tensor_tensor(top[:, 0, :], top[:, 0, :], lse[:, 2, :], ALU.add))
                own(dve.reciprocal(top[:, 1, :], top[:, 0, :]))
                for g in range(GROUPS):
                    own(dve.tensor_tensor(lse[:, g, :], lse[:, g, :], top[:, 1, :], ALU.mult))
                for c in range(C):
                    dve.wait_ge(spread_done, c + 1)
                    own(dve.tensor_tensor(y[:, c, :], y[:, c, :], psum[:, c, :], ALU.mult))
                    dve.tensor_tensor(y[:, c, :], y[:, c, :], z[:, c, :], ALU.mult).then_inc(weighed, 1)

            @block.tensor
            def _(pe):
                pe.wait_ge(dve_own, 1)
                for g in range(GROUPS):
                    for b in range(T):
                        src = stats[:, 3, 16 * g + b:16 * g + b + 13:4]
                        out = permuted(psum[0:4, g, :], g)
                        if g == 0:
                            out = out[:, b * P:(b + 1) * P]
                        elif g == 1:
                            out = out[:, b, :]
                        else:
                            out = out[:, 4 * b:4 * b + 4, :]
                        mm = pe.transpose(out, src, ident[:])
                mm.then_inc(turned, 1)
                pe.wait_ge(dve_own, 3 + GROUPS + 2 + GROUPS + 3 + GROUPS)
                for c in range(C):
                    pe.matmul(psum[:, c, :], pair[:, c % 2, :], lse[:, c // 2, :], start=True, stop=True).then_inc(spread_done, 1)

    split_operand(nc, lambda c: y[:, c, :], turned_x, C)

    def steps(c):
        return [lambda dve, bank: dve.tensor_tensor(gate_b[:, c, :], bank, gate_b[:, c, :], ALU.mult),
                lambda dve, bank: dve.tensor_tensor(merged[:, c, :], merged[:, c, :], gate_b[:, c, :], ALU.add)]

    channel_products(nc, psum, weights, turned_x[:, 0:C], KB, [("dve", steps(c)) for c in range(KD)])


def program(nc, a, out, first_only=False):
    with ExitStack() as ctx:
        def sb(name, shape):
            return ctx.enter_context(nc.sbuf_tensor(name, shape, F32))

        psum = ctx.enter_context(nc.psum_tensor("psum", [P, 8, 512], F32))
        x = sb("x_stream", [P, T, D])
        weights = WeightRing(nc, ctx)
        consts = constants(nc, sb, psum)
        with stage(nc, "x_landed other") as (x_landed, other), nc.Block() as block:
            @block.sync
            def _(sp):
                sp.dma_start(x[:], a["x"][0].rearrange("(t p) d -> p t d", p=P)).then_inc(x_landed, 16)
                sp.wait_ge(x_landed, 16)
        names = ("norm1 w_in mla_q_norm mla_kv_norm mla_w_uq mla_w_ukv swa_sinks fox_b_f w_out norm2 w_up "
                 "w_down").split()
        layers(nc, psum, x, weights, consts, *[a[n] for n in names])
        if not first_only:
            second_part(nc, psum, x, weights, consts, a)
        with stage(nc, "out_landed other") as (out_landed, other), nc.Block() as block:
            @block.sync
            def _(sp):
                sp.dma_start(out[0].rearrange("(t p) d -> p t d", p=P), x[:]).then_inc(out_landed, 16)
                sp.wait_ge(out_landed, 16)


_INS = ["x", "norm1", "w_in", "mla_q_norm", "mla_kv_norm", "mla_w_uq", "mla_w_ukv", "swa_sinks", "fox_b_f", "w_out",
        "norm2", "w_up", "w_down", "final_norm", "c_2", "norm_w_2", "ada_w_2", "ada_b_2", "w_in_2", "conv_w_2",
        "a_log_2", "dt_bias_2", "dn_norm_w_2", "w_proj_a_2", "w_proj_b_2", "w_out_2", "final_norm_w_2"]


def kernel(**inputs):
    import numpy as _np
    import concourse.bacc as _bacc
    from concourse import mybir as _mybir
    from concourse.bass_utils import run_bass_kernel_spmd as _run

    nc = _bacc.Bacc("TRN2", target_bir_lowering=False, num_devices=1)
    arrays, args = {}, {}
    for name in _INS:
        a = _np.ascontiguousarray(inputs[name])
        arrays[f"in_{name}_dram"] = a
        args[name] = nc.dram_tensor(f"in_{name}_dram", a.shape, _mybir.dt.from_np(a.dtype), kind="ExternalInput").ap()
    out = nc.dram_tensor("out_0_dram", (1, S, D), _mybir.dt.float32, kind="ExternalOutput").ap()
    program(nc, args, out)
    r = _run(nc, [arrays], core_ids=[0])
    return r.results[0]["out_0_dram"]
```

```python
from contextlib import ExitStack, contextmanager

import numpy as np

import concourse.bass as bass
from concourse import mybir

F32 = mybir.dt.float32
F32R = mybir.dt.float32r
ACT = mybir.ActivationFunctionType
ALU = mybir.AluOpType
AX_X = mybir.AxisListType.X

P = 128
S = 512
D = 1024
T = S // P
KD = D // P
DEPTH = 2
EPS = 1e-6
MASKED = -1e30
TAKEN = -3e38
ROPE_THETA = 10000.0

SPLITS = dict(cq=256, ckv=128, kr=32, bq=256, bk=128, bv=128, cq_=256, ck_=256, cv=256, qi=256, ki=32,
              w=8, dq=256, dk=256, dv=256, f=4)
COL = {}
_n = 0
for _k, _w in SPLITS.items():
    COL[_k] = _n
    _n += _w
IN_WIDTH = _n

PIECES = []
PLACE = {}
_at = {"proj": 0, "values": 0}
for _k, _w in SPLITS.items():
    if _k not in ("dq", "dk"):
        _b = "values" if _k in ("bv", "cv", "dv", "w", "f") else "proj"
        PLACE[_k] = _at[_b]
        if PIECES and PIECES[-1][1:3] == (COL[_k], _b):
            PIECES[-1] = (PIECES[-1][0], COL[_k] + _w, _b, PIECES[-1][3])
        else:
            PIECES.append((COL[_k], COL[_k] + _w, _b, _at[_b]))
        _at[_b] += _w
PROJ_W = _at["proj"]
V_MLA = _at["values"]
VALUES_W = V_MLA + 256


def tok(name):
    return PLACE[name]


QA, KA, BQ, BK, CQ, CK, QI, KI, DQ, DK = 0, 4, 8, 10, 12, 14, 16, 18, 19, 21
N_TURNED = 23
N_ROTATED = DQ
MLA_DIM = 96
MLA_NOPE = 64

RING = 6
SPLIT_RING = 3
SLOT = 1040


class Chain:

    def __init__(self, eng, sem):
        self.eng, self.sem, self.n = eng, sem, 0

    def __call__(self, instruction):
        self.n += 1
        instruction.then_inc(self.sem, 1)
        self.eng.wait_ge(self.sem, self.n)


class WeightRing:

    def __init__(self, nc, ctx):
        self.buf = ctx.enter_context(nc.sbuf_tensor("weight_ring", [P, RING, SLOT], F32))
        self.pairs = ctx.enter_context(nc.sbuf_tensor("weight_pairs", [P, SPLIT_RING, 2, SLOT], F32R))
        self.landed = [ctx.enter_context(nc.semaphore(f"weights_landed_{i}")) for i in range(RING)]
        self.rounded = ctx.enter_context(nc.semaphore("weights_rounded"))
        self.split = ctx.enter_context(nc.semaphore("weights_split"))
        self.items_done = ctx.enter_context(nc.semaphore("items_done"))
        self.restart([])

    def restart(self, items):
        self.items, self.sent, self.taken, self.n_high, self.n_low = items, 0, 0, 0, 0

    def size(self, i):
        return self.items[i].shape[1] * self.items[i].shape[2]

    def send(self, sp, end):
        last = min(len(self.items), RING + (end - 1 + SPLIT_RING if end else 0))
        while self.sent < last:
            i = self.sent
            if i >= RING:
                sp.wait_ge(self.split, i - RING + 1)
            raw = self.buf[:, i % RING, 0:self.size(i)].rearrange("p (k c) -> p k c", k=self.items[i].shape[1])
            sp.dma_start(raw, self.items[i]).then_inc(self.landed[i % RING], 16)
            self.sent += 1

    def high(self, act, using):
        while self.n_high < min(len(self.items), using + SPLIT_RING):
            i, n = self.n_high, self.size(self.n_high)
            act.wait_ge(self.landed[i % RING], 16 * (i // RING + 1))
            if i >= SPLIT_RING:
                act.wait_ge(self.items_done, i - SPLIT_RING + 1)
            act.activation(self.pairs[:, i % SPLIT_RING, 0, 0:n], self.buf[:, i % RING, 0:n],
                           ACT.Copy).then_inc(self.rounded, 1)
            self.n_high += 1

    def low(self, dve, using):
        while self.n_low < min(len(self.items), using + SPLIT_RING):
            i, n = self.n_low, self.size(self.n_low)
            dve.wait_ge(self.rounded, i + 1)
            dve.tensor_tensor(self.pairs[:, i % SPLIT_RING, 1, 0:n], self.buf[:, i % RING, 0:n],
                              self.pairs[:, i % SPLIT_RING, 0, 0:n].bitcast(F32), ALU.subtract).then_inc(self.split, 1)
            self.n_low += 1

    def take(self, pe):
        i = self.taken
        self.taken += 1
        pe.wait_ge(self.split, i + 1)
        return [self.pairs[:, i % SPLIT_RING, j, 0:self.size(i)].rearrange("p (k c) -> p k c",
                                                                          k=self.items[i].shape[1]) for j in (0, 1)]

    def used(self, last_matmul):
        last_matmul.then_inc(self.items_done, 1)

    def sems(self):
        return self.landed + [self.rounded, self.split, self.items_done]


def product(pe, out, lhs, rhs, start, stop):
    pe.matmul(out, lhs[0], rhs[0], start=start, stop=False)
    pe.matmul(out, lhs[0], rhs[1], start=False, stop=False)
    return pe.matmul(out, lhs[1], rhs[0], start=False, stop=stop)


@contextmanager
def stage(nc, names):
    with ExitStack() as ctx:
        sems = [ctx.enter_context(nc.semaphore(n)) for n in names.split()]
        yield sems
        clear(nc, sems)


def clear(nc, sems):
    nums = sorted(s.num for s in sems)
    starts = [n for n in nums if n - 1 not in nums]
    for start in starts:
        end = start
        while end in nums:
            end += 1
        nc.all_engine_barrier(sems_to_clear=range(start, end))


def spread(ap, axis, n):
    ap = ap.unsqueeze(axis)
    shape = list(ap.shape)
    shape[axis] = n
    return ap.broadcast_to(shape)


def rope_tables():
    half = 32
    freq = (1.0 / (ROPE_THETA ** (np.arange(half, dtype=np.float32) * np.float32(2.0) / 64))).astype(np.float32)
    ang = np.arange(S, dtype=np.float32)[:, None] * freq[None, :]
    both = np.stack([np.cos(ang), np.sin(ang)], 0).astype(np.float32)
    return np.ascontiguousarray(both.reshape(2, T, P, half).transpose(2, 0, 1, 3))



def constants(nc, sb, psum):
    ident = sb("ident", [P, P])
    ones = sb("ones", [P, P])
    causal = sb("causal", [P, S])
    window = sb("window", [P, 2 * P])
    onehot = sb("onehot", [16, 16, P])
    gate_forms = sb("gate_forms", [P, 4])
    with stage(nc, "filled masked formed") as (filled, masked, formed), nc.Block() as block:
        @block.vector
        def _(dve):
            dve.memset(ident[:], 0.0).then_inc(filled, 1)
            dve.memset(ones[:], 1.0).then_inc(filled, 1)
            dve.memset(causal[:], 0.0).then_inc(filled, 1)
            dve.memset(window[:], 0.0).then_inc(filled, 1)
            dve.memset(onehot[:], 0.0).then_inc(filled, 1)
            dve.wait_ge(masked, 1)
            own = Chain(dve, formed)
            own(dve.tensor_reduce(gate_forms[:, 1:2], ident[:, 0:97:32], AX_X, ALU.add))
            own(dve.tensor_reduce(gate_forms[:, 3:4], ident[:, 1:98:32], AX_X, ALU.add))
            own(dve.tensor_scalar(gate_forms[:, 0:1], gate_forms[:, 3:4], 8.0, None, ALU.mult))
            own(dve.tensor_scalar(gate_forms[:, 2:3], gate_forms[:, 1:2], -8.0, None, ALU.mult))

        @block.gpsimd
        def _(pool):
            pool.wait_ge(filled, 5)
            own = Chain(pool, masked)
            own(pool.affine_select(out=ident[:], in_=ident[:], compare_op=ALU.not_equal, fill=1.0, base=0,
                                   pattern=[[-1, P]], channel_multiplier=1))
            own(pool.affine_select(out=causal[:], in_=causal[:], compare_op=ALU.is_ge, fill=MASKED, base=S - P,
                                   pattern=[[-1, S]], channel_multiplier=1))
            own(pool.affine_select(out=window[:], in_=window[:], compare_op=ALU.is_ge, fill=MASKED, base=P,
                                   pattern=[[-1, 2 * P]], channel_multiplier=1))
            own(pool.affine_select(out=window[:], in_=window[:], compare_op=ALU.is_gt, fill=MASKED, base=0,
                                   pattern=[[1, 2 * P]], channel_multiplier=-1))
            own(pool.affine_select(out=onehot[:], in_=onehot[:], compare_op=ALU.not_equal, fill=1.0, base=0,
                                   pattern=[[-1, 16], [0, P]], channel_multiplier=1))
    return ident, ones, causal, window, onehot, gate_forms



def norm_and_turn(nc, psum, x, xn, gains, pair, ident, small, bias=None, work=None):
    ss, ms, root, rstd = (small[:, 4 * i:4 * i + 4] for i in range(4))
    with stage(nc, "squared mean_ready root_ready dve_own scaled turned shifted high low") as (
            squared, mean_ready, root_ready, dve_own, scaled, turned, shifted, high, low), nc.Block() as block:
        @block.scalar
        def _(act):
            for t in range(T):
                act.activation(xn[:, t, :], x[:, t, :], ACT.Square, accum_out=ss[:, t:t + 1]).then_inc(squared, 1)
            act.wait_ge(mean_ready, 1)
            act.activation(root, ms, ACT.Sqrt).then_inc(root_ready, 1)
            for k in range(KD):
                if bias is None:
                    act.wait_ge(turned, k + 1)
                    act.activation(pair[:, k, 0, :], psum[:, k, :], ACT.Copy, scale=gains[:, k:k + 1]).then_inc(high, 1)
                else:
                    act.wait_ge(shifted, k + 1)
                    act.activation(pair[:, k, 0, :], work[:, k % 2, :], ACT.Copy).then_inc(high, 1)

        @block.vector
        def _(dve):
            own = Chain(dve, dve_own)
            dve.wait_ge(squared, T)
            dve.tensor_scalar(ms, ss, 1.0 / D, EPS, ALU.mult, ALU.add).then_inc(mean_ready, 1)
            dve.wait_ge(root_ready, 1)
            own(dve.reciprocal(rstd, root))
            for t in range(T):
                dve.tensor_scalar(xn[:, t, :], x[:, t, :], rstd[:, t:t + 1], None, ALU.mult).then_inc(scaled, 1)

            def rest(k):
                dve.wait_ge(high, k + 1)
                if bias is None:
                    dve.scalar_tensor_tensor(out=pair[:, k, 1, :], in0=psum[:, k, :], scalar=gains[:, k:k + 1],
                                             in1=pair[:, k, 0, :].bitcast(F32), op0=ALU.mult,
                                             op1=ALU.subtract).then_inc(low, 1)
                else:
                    dve.tensor_tensor(pair[:, k, 1, :], work[:, k % 2, :], pair[:, k, 0, :].bitcast(F32),
                                      ALU.subtract).then_inc(low, 1)

            for k in range(KD):
                if bias is None:
                    rest(k)
                    continue
                dve.wait_ge(turned, k + 1)
                if k >= 2:
                    dve.wait_ge(low, k - 1)
                dve.tensor_scalar(work[:, k % 2, :], psum[:, k, :], gains[:, k:k + 1], bias[:, k:k + 1],
                                  ALU.mult, ALU.add).then_inc(shifted, 1)
                if k >= 1:
                    rest(k - 1)
            if bias is not None:
                rest(KD - 1)

        @block.tensor
        def _(pe):
            pe.wait_ge(scaled, T)
            for k in range(KD):
                for t in range(T):
                    mm = pe.transpose(psum[:, k, t * P:(t + 1) * P], xn[:, t, k * P:(k + 1) * P], ident[:])
                mm.then_inc(turned, 1)


def split_operand(nc, source, pair, n):
    with stage(nc, "high low") as (high, low), nc.Block() as block:
        @block.scalar
        def _(act):
            for k in range(n):
                act.activation(pair[:, k, 0, :], source(k), ACT.Copy).then_inc(high, 1)

        @block.vector
        def _(dve):
            for k in range(n):
                dve.wait_ge(high, k + 1)
                dve.tensor_tensor(pair[:, k, 1, :], source(k), pair[:, k, 0, :].bitcast(F32),
                                  ALU.subtract).then_inc(low, 1)



class Job:

    def __init__(self, scores, width, mask, scale, values, row, col, sink=None, dense=False):
        self.scores, self.width, self.mask, self.scale = scores, width, mask, scale
        self.values, self.row, self.col, self.sink, self.dense = values, row, col, sink, dense


LAG = 5


def attention(nc, psum, jobs, stores, ident, probs, probs_t, stats, sems, besides=None):
    (scored, found, shifted, powered, normed, turned, copied, valued, stored, stored_low, dve_own, act_own,
     inverted, besides_done) = sems
    in_pairs = stores[0][2] is not None
    RUN, TURN, VALUES = 8, LAG, LAG + 1
    n = len(jobs)
    SB, TB, PB = 4, 2, probs.shape[1]
    OUT = SB + TB
    with nc.Block() as block:
        @block.tensor
        def _(pe):
            def scores(j):
                if j >= SB:
                    pe.wait_ge(powered, j - SB + 1)
                job = jobs[j]
                for i, (lhs, rhs) in enumerate(job.scores):
                    mm = pe.matmul(psum[:, j % SB, 0:job.width], lhs, rhs, start=(i == 0),
                                   stop=(job.dense and i == len(job.scores) - 1))
                if not job.dense:
                    first = job.width - job.mask.shape[1]
                    mm = pe.matmul(psum[:, j % SB, first:job.width], ident[:], job.mask, start=False, stop=True)
                mm.then_inc(scored, 1)

            def turn(j):
                pe.wait_ge(normed, j + 1)
                if j >= TB:
                    pe.wait_ge(copied, j - TB + 1)
                for b in range(jobs[j].width // P):
                    mm = pe.transpose(psum[:, SB + j % TB, b * P:(b + 1) * P],
                                      probs[:, j % PB, b * P:(b + 1) * P], ident[:])
                mm.then_inc(turned, 1)

            def values(j):
                job = jobs[j]
                run = j // RUN
                pe.wait_ge(copied, j + 1)
                if run >= 2 and j % RUN == 0:
                    pe.wait_ge(stored_low if in_pairs else stored, run - 1)
                nb = len(job.values)
                for b, v in enumerate(job.values):
                    mm = pe.matmul(psum[job.row:job.row + 64, OUT + run % 2, job.col:job.col + P], v,
                                   probs_t[:, j % TB, b * P:(b + 1) * P], start=(b == 0), stop=(b == nb - 1))
                mm.then_inc(valued, 1)

            for j in range(n + VALUES):
                if j < n:
                    scores(j)
                if 0 <= j - TURN < n:
                    turn(j - TURN)
                if j >= VALUES:
                    values(j - VALUES)

        @block.vector
        def _(dve):
            own = Chain(dve, dve_own)

            def largest(j):
                job = jobs[j]
                w = job.width
                dve.wait_ge(scored, j + 1)
                if job.dense:
                    if j >= PB:
                        dve.wait_ge(turned, j - PB + 1)
                    dve.scalar_tensor_tensor(out=probs[:, j % PB, 0:w], in0=psum[:, j % SB, 0:w], scalar=job.scale,
                                             in1=job.mask, op0=ALU.mult, op1=ALU.add).then_inc(found, 1)
                else:
                    dve.tensor_reduce(stats[:, 4, j:j + 1], psum[:, j % SB, 0:w], AX_X, ALU.max).then_inc(found, 1)

            def shift(j):
                job = jobs[j]
                dve.wait_ge(found, j + 1)
                if job.dense:
                    dve.tensor_reduce(stats[:, 0, j:j + 1], probs[:, j % PB, 0:job.width], AX_X, ALU.max,
                                      negate=True).then_inc(shifted, 1)
                elif job.sink is None:
                    dve.tensor_scalar(stats[:, 0, j:j + 1], stats[:, 4, j:j + 1], -job.scale, None,
                                      ALU.mult).then_inc(shifted, 1)
                else:
                    dve.scalar_tensor_tensor(out=stats[:, 0, j:j + 1], in0=stats[:, 4, j:j + 1], scalar=-job.scale,
                                             in1=job.sink, op0=ALU.mult, op1=ALU.min).then_inc(shifted, 1)

            def invert(j):
                dve.wait_ge(powered, j + 1)
                total = stats[:, 1, j:j + 1]
                if jobs[j].sink is not None:
                    own(dve.tensor_scalar(stats[:, 2, j:j + 1], total, stats[:, 3, j:j + 1], None, ALU.add))
                    total = stats[:, 2, j:j + 1]
                dve.reciprocal(stats[:, 4, j:j + 1], total).then_inc(inverted, 1)

            def store_low(run):
                dve.wait_ge(stored, run + 1)
                high, _, low = stores[run]
                dve.tensor_tensor(low, psum[:, OUT + run % 2, :], high.bitcast(F32), ALU.subtract).then_inc(stored_low, 1)

            count, step, needed = besides or (0, None, 0)
            n_besides = 0

            def beside(j):
                nonlocal n_besides
                if n_besides < count and n_besides * (needed - 1) < count * (j + 1):
                    if n_besides:
                        dve.wait_ge(besides_done, n_besides)
                    step(dve, n_besides).then_inc(besides_done, 1)
                    n_besides += 1

            done = 0
            for j in range(n + 2):
                if count and j == needed:
                    assert n_besides == count
                    dve.wait_ge(besides_done, count)
                if j < n:
                    largest(j)
                if j >= 2:
                    invert(j - 2)
                beside(j)
                if j < n:
                    shift(j)
                beside(j)
                beside(j)
                if in_pairs and j > RUN * (done + 1) + VALUES + 1:
                    store_low(done)
                    done += 1
            while in_pairs and done < n // RUN:
                store_low(done)
                done += 1

        @block.gpsimd
        def _(pool):
            for j, job in enumerate(jobs):
                pool.wait_ge(inverted, j + 1)
                p = probs[:, j % PB, 0:job.width]
                pool.tensor_scalar(p, p, stats[:, 4, j:j + 1], None, ALU.mult).then_inc(normed, 1)

        @block.scalar
        def _(act):
            own = Chain(act, act_own)

            def power(j):
                job = jobs[j]
                act.wait_ge(shifted, j + 1)
                if job.sink is not None:
                    own(act.activation(stats[:, 3, j:j + 1], job.sink, ACT.Exp, bias=stats[:, 0, j:j + 1], scale=-1.0))
                p = probs[:, j % PB, 0:job.width]
                if job.dense:
                    source, scale = p, 1.0
                else:
                    source, scale = psum[:, j % SB, 0:job.width], job.scale
                    if j >= PB:
                        act.wait_ge(turned, j - PB + 1)
                act.activation(p, source, ACT.Exp, bias=stats[:, 0, j:j + 1], scale=scale,
                               accum_out=stats[:, 1, j:j + 1]).then_inc(powered, 1)

            def copy(j):
                act.wait_ge(turned, j + 1)
                if j >= TB:
                    act.wait_ge(valued, j - TB + 1)
                w = jobs[j].width
                act.activation(probs_t[:, j % TB, 0:w], psum[:, SB + j % TB, 0:w], ACT.Copy).then_inc(copied, 1)

            def store(run):
                act.wait_ge(valued, RUN * (run + 1))
                out, bank_view, _ = stores[run]
                act.activation(out, bank_view(psum[:, OUT + run % 2, :]), ACT.Copy).then_inc(stored, 1)

            done = 0
            for j in range(n + TURN):
                if j >= TURN:
                    copy(j - TURN)
                if j < n:
                    power(j)
                if j > RUN * (done + 1) + VALUES:
                    store(done)
                    done += 1
            while done < n // RUN:
                store(done)
                done += 1


ATTENTION_SEMS = "scored found shifted powered normed turned copied valued stored stored_low dve_own act_own inverted besides_done"



def product_by_tokens(pe, psum, bank, weights, lhs, n_items, chunks, written=None):
    k = 0
    for i in range(n_items):
        w = weights.take(pe)
        for kk in range(w[0].shape[1]):
            if written is not None:
                pe.wait_ge(written, k + 1)
            for t in range(T):
                tile = slice(t * P, (t + 1) * P)
                mm = product(pe, psum[:, bank + t, 0:w[0].shape[2]], [lhs[:, k, j, tile] for j in (0, 1)],
                             [w[j][:, kk, :] for j in (0, 1)], start=(k == 0), stop=(k == chunks - 1))
            k += 1
        weights.used(mm)
    assert k == chunks


def product_by_channels(pe, psum, banks, weights, pair, chunks):
    k = 0
    for i in range(2):
        w = weights.take(pe)
        n = w[0].shape[1]
        for h, bank in enumerate(banks):
            for kk in range(n):
                mm = product(pe, psum[:, bank, :], [w[j][:, kk, h * P:(h + 1) * P] for j in (0, 1)],
                             [pair[:, k + kk, j, :] for j in (0, 1)], start=(k + kk == 0),
                             stop=(k + kk == chunks - 1))
        k += n
        weights.used(mm)
    assert k == chunks


def rows(w, k0, kk, c0, c1):
    return w[k0 * P:(k0 + kk) * P, c0:c1].rearrange("(k p) c -> p k c", p=P)


def for_tokens(w, chunks, c0, c1, k0=0):
    per = max(kk for kk in range(1, chunks + 1) if chunks % kk == 0 and kk * (c1 - c0) <= SLOT)
    return [rows(w, k0 + k, per, c0, c1) for k in range(0, chunks, per)]


def for_channels(w, chunks, c0, c1):
    return [rows(w, k, chunks // 2, c, c + 256) for c in range(c0, c1, 256) for k in (0, chunks // 2)]


def output_products(nc, psum, x, weights, lhs, chunks, per_half, gate=None):
    start = weights.taken
    end = start + 2 * per_half
    with stage(nc, "summed gated") as (summed, gated), nc.Block() as block:
        @block.sync
        def _(sp):
            weights.send(sp, end)

        @block.tensor
        def _(pe):
            for c in range(2):
                product_by_tokens(pe, psum, 4 * c, weights, lhs, per_half, chunks)

        @block.scalar
        def _(act):
            for i in range(start, end):
                weights.high(act, i)

        @block.vector
        def _(dve):
            for c in range(2):
                for i in range(per_half):
                    weights.low(dve, start + c * per_half + i)
                dve.wait_ge(weights.items_done, start + (c + 1) * per_half)
                for t in range(T):
                    cols = slice(c * 512, (c + 1) * 512)
                    prod = psum[:, 4 * c + t, :]
                    if gate is not None:
                        if 4 * c + t >= 2:
                            dve.wait_ge(summed, 4 * c + t - 1)
                        dve.tensor_tensor(gate[1][:, t % 2, :], prod, gate[0][:, cols], ALU.mult).then_inc(gated, 1)
                        dve.wait_ge(gated, 4 * c + t + 1)
                        prod = gate[1][:, t % 2, :]
                    dve.tensor_tensor(x[:, t, cols], prod, x[:, t, cols], ALU.add).then_inc(summed, 1)


def layers(nc, psum, x, weights, consts, norm1, w_in, mla_q_norm, mla_kv_norm, mla_w_uq, mla_w_ukv,
           swa_sinks, fox_b_f, w_out, norm2, w_up, w_down):
    ident, ones, causal, window, onehot, gate_forms = consts
    F = w_up.shape[2]
    KH = F // P // 2
    chunks = [(0, 512), (512, 1024), (1024, 1536), (1536, COL["dq"]), (COL["dv"], IN_WIDTH)]

    rope_table = nc.inline_tensor(rope_tables(), name="rope_table")
    with nc.Fori(0, DEPTH) as l, ExitStack() as lay:
        def sb(name, shape, ctx=lay, dtype=F32):
            return ctx.enter_context(nc.sbuf_tensor(name, shape, dtype))

        def one(a):
            return a[bass.ds(l, 1)].rearrange("o a b -> (o a) b")

        win, wuq, wukv, wout, wup, wdown = (one(a) for a in (w_in, mla_w_uq, mla_w_ukv, w_out, w_up, w_down))
        items, ends = [], []
        for c0, c1 in chunks:
            items += for_tokens(win, KD, c0, c1)
            ends.append(len(items))
        items += for_channels(win, KD, COL["dq"], COL["dv"])
        ends.append(len(items))
        items += for_tokens(wuq, 2, 0, 384) + for_tokens(wukv, 1, 0, 512)
        out_items = for_tokens(wout, KD, 0, 512) + for_tokens(wout, KD, 512, D)
        items += out_items
        for half in range(2):
            items += for_channels(wup, KD, half * KH * P, (half + 1) * KH * P)
            down_items = [i for c in (0, 512) for i in for_tokens(wdown, KH, c, c + 512, k0=half * KH)]
            items += down_items
        weights.restart(items)

        gains = sb("gains", [P, 32])
        sinks = sb("sinks", [P, 4])
        rope = sb("rope", [P, 2, T, 32])
        forget_bias = sb("forget_bias", [P, 1])
        small = sb("small", [P, 32])
        with ExitStack() as ctx:
            vec_rows = sb("vec_rows", [32, P], ctx)
            with stage(nc, "vectors_landed cleared vectors_turned vectors_stored") as (
                    vectors_landed, cleared, vectors_turned, vectors_stored), nc.Block() as block:
                @block.sync
                def _(sp):
                    sp.wait_ge(cleared, 1)
                    for r, v in ((0, norm1), (8, norm2), (16, mla_q_norm), (18, mla_kv_norm)):
                        n = v.shape[1] // P
                        sp.dma_start(vec_rows[r:r + n, :],
                                     v[bass.ds(l, 1), :].rearrange("o (r c) -> (o r) c", c=P)).then_inc(vectors_landed, 16)
                    sp.dma_start(sinks[:], swa_sinks[bass.ds(l, 1), :].to_broadcast([P, 4])).then_inc(vectors_landed, 16)
                    for h in range(4):
                        sp.dma_start(forget_bias[32 * h:32 * h + 32, :],
                                     fox_b_f[bass.ds(l, 1), h:h + 1].to_broadcast([32, 1])).then_inc(vectors_landed, 16)
                    sp.dma_start(rope[:], rope_table[:]).then_inc(vectors_landed, 16)
                    weights.send(sp, 0)
                    sp.wait_ge(vectors_landed, 160)

                @block.vector
                def _(dve):
                    dve.memset(vec_rows[:], 0.0).then_inc(cleared, 1)
                    dve.wait_ge(vectors_turned, 1)
                    dve.tensor_copy(gains[:], psum[:, 0, 0:32]).then_inc(vectors_stored, 1)
                    dve.wait_ge(vectors_landed, 160)
                    dve.tensor_scalar(sinks[:], sinks[:], -1.0, None, ALU.mult).then_inc(vectors_stored, 1)

                @block.tensor
                def _(pe):
                    pe.wait_ge(vectors_landed, 160)
                    pe.transpose(psum[:, 0, 0:32], vec_rows[:], ident[0:32, 0:32]).then_inc(vectors_turned, 1)

        with ExitStack() as mix:
            values = sb("values", [P, T, VALUES_W], mix)
            gates = sb("gates", [P, 2, S], mix)
            turned = sb("turned_qk", [P, N_TURNED, S], mix)
            with ExitStack() as ctx:
                proj = sb("proj", [P, T, PROJ_W], ctx)
                with ExitStack() as c2:
                    turned_x = sb("turned_x", [P, KD, 2, S], c2, F32R)
                    rows_x = proj[:].rearrange("p t c -> p (t c)")[:, 0:T * D].rearrange("p (t c) -> p t c", t=T)
                    norm_and_turn(nc, psum, x, rows_x, gains[:, 0:8], turned_x, ident, small)
                    in_projection(nc, psum, weights, turned_x, dict(proj=proj, values=values), turned, chunks, ends,
                                  rope, sb("sines", [P, 896], c2))
                qa = sb("qa", [P, T, 4 * MLA_DIM], ctx)
                ka = sb("ka", [P, T, 4 * MLA_DIM], ctx)
                with ExitStack() as c2:
                    latents(nc, psum, weights, proj, qa, ka, values, gates, gains, forget_bias, gate_forms, small, ident,
                            rope, sb("latent", [P, T, 384], c2), sb("latent_t", [P, 3, 2, S], c2, F32R),
                            sb("gate_work", [P, 3, S], c2))
                turn_heads(nc, psum, proj, qa, ka, turned, ident)
            chosen = sb("chosen", [P, T, S], mix)
            with ExitStack() as ctx:
                score_keys(nc, psum, values, turned, chosen, causal, sb("relu", [P, 3, S], ctx))
            mixed = sb("mixed", [P, KD, 2, S], mix, F32R)
            with ExitStack() as ctx:
                jobs = layer_jobs(turned, values, gates, chosen, causal, window, sinks)
                stores = [(mixed[:, c, 0, :], lambda bank: bank, mixed[:, c, 1, :])
                          for g in JOB_ORDER for c in (2 * "abcd".index(g), 2 * "abcd".index(g) + 1)]
                with stage(nc, ATTENTION_SEMS) as sems:
                    attention(nc, psum, jobs, stores, ident, sb("probs", [P, 6, S], ctx),
                              sb("probs_t", [P, 3, S], ctx), sb("stats", [P, 5, len(jobs)], ctx), sems,
                              besides=(*select_keys(chosen, sb("best", [P, 8], ctx)), 3 * len(jobs) // 4))
            output_products(nc, psum, x, weights, mixed, KD, len(out_items) // 2)

        with ExitStack() as ctx:
            turned_x = sb("turned_x_mlp", [P, KD, 2, S], ctx, F32R)
            with ExitStack() as c2:
                norm_and_turn(nc, psum, x, sb("rows_mlp", [P, T, D], c2), gains[:, 8:16], turned_x, ident, small)
            hidden = sb("hidden", [P, KH, 2, S], ctx, F32R)
            relu = sb("relu_mlp", [P, 3, S], ctx)
            square = sb("square_mlp", [P, 3, S], ctx)
            for half in range(2):
                half_mlp(nc, psum, x, weights, turned_x, hidden, KH, relu, square, len(down_items) // 2)
        clear(nc, weights.sems())


def half_mlp(nc, psum, x, weights, turned_x, hidden, n, relu, square, per_half):
    B = 3
    start = weights.taken
    down = start + n
    end = down + 2 * per_half
    with stage(nc, "rectified squared high low summed") as (rectified, squared, high, low, summed), nc.Block() as block:
        @block.sync
        def _(sp):
            weights.send(sp, end)

        @block.tensor
        def _(pe):
            for f in range(0, n, 2):
                if f >= 8:
                    pe.wait_ge(rectified, f - 6)
                product_by_channels(pe, psum, (f % 8, f % 8 + 1), weights, turned_x, KD)
            for c in range(2):
                pe.wait_ge(rectified, n - 4 + 4 * c)
                product_by_tokens(pe, psum, 4 * c, weights, hidden, per_half, n, low)

        @block.scalar
        def _(act):
            def round_square(f):
                act.wait_ge(squared, f + 1)
                act.activation(hidden[:, f, 0, :], square[:, f % B, :], ACT.Copy).then_inc(high, 1)

            for f in range(0, n, 2):
                weights.high(act, start + f)
                weights.high(act, start + f + 1)
                act.wait_ge(weights.items_done, start + f + 2)
                for g in (f, f + 1):
                    if g >= B:
                        act.wait_ge(squared, g - B + 1)
                    act.activation(relu[:, g % B, :], psum[:, g % 8, :], ACT.Relu).then_inc(rectified, 1)
                    if g >= 1:
                        round_square(g - 1)
            round_square(n - 1)
            for i in range(down, end):
                weights.high(act, i)

        @block.vector
        def _(dve):
            def rest(f):
                dve.wait_ge(high, f + 1)
                dve.tensor_tensor(hidden[:, f, 1, :], square[:, f % B, :], hidden[:, f, 0, :].bitcast(F32),
                                  ALU.subtract).then_inc(low, 1)

            for f in range(n):
                weights.low(dve, start + f)
                dve.wait_ge(rectified, f + 1)
                if f >= B:
                    dve.wait_ge(low, f - B + 1)
                dve.tensor_tensor(square[:, f % B, :], relu[:, f % B, :], relu[:, f % B, :], ALU.mult).then_inc(squared, 1)
                if f >= 1:
                    rest(f - 1)
            rest(n - 1)
            for c in range(2):
                for i in range(per_half):
                    weights.low(dve, down + c * per_half + i)
                dve.wait_ge(weights.items_done, down + (c + 1) * per_half)
                for t in range(T):
                    cols = slice(c * 512, (c + 1) * 512)
                    dve.tensor_tensor(x[:, t, cols], psum[:, 4 * c + t, :], x[:, t, cols], ALU.add).then_inc(summed, 1)


def rotate(dve, own, heads, tables, sines):
    n, half = heads.shape[1], heads.shape[3]
    cos, sin = (spread(spread(tables[:, i, 0:32:32 // half], 1, 2), 1, n) for i in range(2))
    sine = sines[:, 0:n * 2 * half].rearrange("p (h a f) -> p h a f", h=n, a=2)
    own(dve.tensor_tensor(sine, heads, sin, ALU.mult))
    own(dve.tensor_tensor(heads, heads, cos, ALU.mult))
    dve.tensor_tensor(heads[:, :, 0, :], heads[:, :, 0, :], sine[:, :, 1, :], ALU.subtract).then_inc(own.sem, 1)
    own.n += 1
    own(dve.tensor_tensor(heads[:, :, 1, :], heads[:, :, 1, :], sine[:, :, 0, :], ALU.add))


def in_projection(nc, psum, weights, turned_x, buffers, turned, chunks, ends, rope, sines):
    groups = len(ends)

    def copies(g, b):
        bank = 4 * (g % 2) + b
        if g == groups - 1:
            return [(turned[:, DQ + b, :], psum[:, bank, :])]
        c0, c1 = chunks[g]
        found = []
        for p0, p1, name, at in PIECES:
            a, e = max(p0, c0), min(p1, c1)
            if a < e:
                found.append((buffers[name][:, b, at + a - p0:at + e - p0], psum[:, bank, a - c0:e - c0]))
        return found

    def copied(g):
        return sum(2 * len(copies(i, 0)) for i in range(g + 1))

    after_2 = [(tok("bq"), 14, 32)]
    after_3 = [(tok("kr"), 1, 16), (tok("qi"), 9, 16)]
    rotations = {3: [(t, after_2) for t in range(T)], 4: [(t, after_3) for t in range(T)]}

    with stage(nc, "stored_act stored_dve dve_own") as (stored_act, stored_dve, dve_own), nc.Block() as block:
        @block.sync
        def _(sp):
            weights.send(sp, ends[-1])

        @block.tensor
        def _(pe):
            for g in range(groups):
                if g >= 2:
                    pe.wait_ge(stored_act, copied(g - 2))
                    pe.wait_ge(stored_dve, copied(g - 2))
                bank = 4 * (g % 2)
                if g < groups - 1:
                    product_by_tokens(pe, psum, bank, weights, turned_x, ends[g] - (ends[g - 1] if g else 0), KD)
                else:
                    product_by_channels(pe, psum, (bank, bank + 1), weights, turned_x, KD)
                    product_by_channels(pe, psum, (bank + 2, bank + 3), weights, turned_x, KD)

        @block.scalar
        def _(act):
            done = 0
            for g in range(groups):
                for i in range(done, ends[g]):
                    weights.high(act, i)
                done = ends[g]
                act.wait_ge(weights.items_done, ends[g])
                for b in (0, 1):
                    for out, bank in copies(g, b):
                        act.activation(out, bank, ACT.Copy).then_inc(stored_act, 1)

        @block.vector
        def _(dve):
            own = Chain(dve, dve_own)
            done = 0
            todo = []
            for g in range(groups):
                if g in rotations:
                    dve.wait_ge(stored_act, copied(g - 1))
                    dve.wait_ge(stored_dve, copied(g - 1))
                    todo += rotations[g]
                for i in range(done, ends[g]):
                    weights.low(dve, i)
                    if todo:
                        t, parts = todo.pop(0)
                        for at, n, half in parts:
                            rotate(dve, own, buffers["proj"][:, t, at:at + 2 * n * half].rearrange(
                                "p (h a f) -> p h a f", h=n, a=2), rope[:, :, t, :], sines)
                if g == groups - 1:
                    assert not todo
                done = ends[g]
                dve.wait_ge(weights.items_done, ends[g])
                for b in (2, 3):
                    for out, bank in copies(g, b):
                        dve.tensor_copy(out, bank).then_inc(stored_dve, 1)


def latents(nc, psum, weights, proj, qa, ka, values, gates, gains, forget_bias, gate_forms, small, ident, rope,
            latent, latent_t, gate_work):
    QW, KW = SPLITS["cq"], SPLITS["ckv"]
    ss, ms, root, rstd = (small[:, 8 * i:8 * i + 8] for i in range(4))
    at_uq = weights.taken
    at_ukv = at_uq + 1
    v_mla = values[:, :, V_MLA:V_MLA + 256]
    f0 = tok("f")
    spread_f = gate_work[:, 2, :].rearrange("p (t c) -> p t c", t=T)

    def by_head(ap):
        return ap.rearrange("p (h c) -> p h c", h=4)

    def q_copies(t):
        return [(qa[:, t, :], psum[:, 4 + t, 0:384])]

    def kv_copies(t):
        bank = by_head(psum[:, t, :])
        return [(by_head(ka[:, t, :])[:, :, 0:MLA_NOPE], bank[:, :, 0:MLA_NOPE]), (by_head(v_mla[:, t, :]), bank[:, :, 64:128])]

    with stage(nc, "squared mean_ready root_ready dve_own scaled turned gates_turned high low "
                   "stored_act stored_dve gate_abs gate_exp gate_arg gate_log repeated") as (
            squared, mean_ready, root_ready, dve_own, scaled, turned, gates_turned, high, low,
            stored_act, stored_dve, gate_abs, gate_exp, gate_arg, gate_log, repeated), nc.Block() as block:
        @block.sync
        def _(sp):
            weights.send(sp, at_ukv + 1)

        @block.scalar
        def _(act):
            for t in range(T):
                act.activation(latent[:, t, 0:QW], proj[:, t, 0:QW], ACT.Square,
                               accum_out=ss[:, t:t + 1]).then_inc(squared, 1)
                act.activation(latent[:, t, QW:QW + KW], proj[:, t, QW:QW + KW], ACT.Square,
                               accum_out=ss[:, 4 + t:5 + t]).then_inc(squared, 1)
            act.wait_ge(mean_ready, 2)
            act.activation(root, ms, ACT.Sqrt).then_inc(root_ready, 1)
            for k in range(3):
                act.wait_ge(turned, k + 1)
                act.activation(latent_t[:, k, 0, :], psum[:, k, :], ACT.Copy,
                               scale=gains[:, 16 + k:17 + k]).then_inc(high, 1)
            act.wait_ge(gate_abs, 1)
            act.activation(gate_work[:, 1, :], gate_work[:, 1, :], ACT.Exp, scale=-1.0).then_inc(gate_exp, 1)
            act.wait_ge(gate_arg, 1)
            act.activation(gate_work[:, 1, :], gate_work[:, 1, :], ACT.Ln).then_inc(gate_log, 1)
            for at, copies in ((at_uq, q_copies), (at_ukv, kv_copies)):
                weights.high(act, at)
                act.wait_ge(weights.items_done, at + 1)
                for t in (0, 1):
                    for out, bank in copies(t):
                        act.activation(out, bank, ACT.Copy).then_inc(stored_act, 1)

        @block.vector
        def _(dve):
            own = Chain(dve, dve_own)
            dve.wait_ge(squared, 2 * T)
            dve.tensor_scalar(ms[:, 0:4], ss[:, 0:4], 1.0 / QW, EPS, ALU.mult, ALU.add).then_inc(mean_ready, 1)
            dve.tensor_scalar(ms[:, 4:8], ss[:, 4:8], 1.0 / KW, EPS, ALU.mult, ALU.add).then_inc(mean_ready, 1)
            dve.wait_ge(root_ready, 1)
            own(dve.reciprocal(rstd, root))
            for t in range(T):
                dve.tensor_scalar(latent[:, t, 0:QW], proj[:, t, 0:QW], rstd[:, t:t + 1], None,
                                  ALU.mult).then_inc(scaled, 1)
                dve.tensor_scalar(latent[:, t, QW:QW + KW], proj[:, t, QW:QW + KW], rstd[:, 4 + t:5 + t], None,
                                  ALU.mult).then_inc(scaled, 1)
            for k in range(3):
                dve.wait_ge(high, k + 1)
                dve.scalar_tensor_tensor(out=latent_t[:, k, 1, :], in0=psum[:, k, :], scalar=gains[:, 16 + k:17 + k],
                                         in1=latent_t[:, k, 0, :].bitcast(F32), op0=ALU.mult,
                                         op1=ALU.subtract).then_inc(low, 1)
            dve.wait_ge(gates_turned, 1)
            own(dve.tensor_scalar(gate_work[:, 0, :], psum[:, 3, :], forget_bias[:, 0:1], None, ALU.add))
            dve.scalar_tensor_tensor(out=gate_work[:, 1, :], in0=gate_work[:, 0, :], scalar=-1.0,
                                     in1=gate_work[:, 0, :], op0=ALU.mult, op1=ALU.max).then_inc(gate_abs, 1)
            own(dve.memset(gate_work[:, 2, :], 1.0))
            dve.wait_ge(gate_exp, 1)
            dve.tensor_scalar(gate_work[:, 1, :], gate_work[:, 1, :], 1.0, None, ALU.add).then_inc(gate_arg, 1)
            dve.wait_ge(gate_log, 1)
            own(dve.scalar_tensor_tensor(out=gate_work[:, 0, :], in0=gate_work[:, 0, :], scalar=0.0,
                                         in1=gate_work[:, 1, :], op0=ALU.min, op1=ALU.subtract))
            own(dve.tensor_tensor_scan(gate_work[:, 1, :], gate_work[:, 2, :], gate_work[:, 0, :], 0.0,
                                       ALU.mult, ALU.add))
            for i in range(2):
                own(dve.tensor_scalar(gates[:, i, :], gate_work[:, 1, :], gate_forms[:, 2 * i:2 * i + 1],
                                      gate_forms[:, 2 * i + 1:2 * i + 2], ALU.mult, ALU.add))
            for at, copies in ((at_uq, q_copies), (at_ukv, kv_copies)):
                weights.low(dve, at)
                dve.wait_ge(weights.items_done, at + 1)
                for t in (2, 3):
                    for out, bank in copies(t):
                        dve.tensor_copy(out, bank).then_inc(stored_dve, 1)
            dve.wait_ge(stored_act, 2)
            dve.wait_ge(stored_dve, 2)
            for t in range(T):
                rotate(dve, own, by_head(qa[:, t, :])[:, :, MLA_NOPE:MLA_DIM].rearrange("p h (a f) -> p h a f", a=2),
                       rope[:, :, t, :], gate_work[:, 2, :])

        @block.gpsimd
        def _(pool):
            def heads(ap, n):
                return ap.rearrange("p t (h c) -> p t h c", h=n)

            pool.tensor_copy(spread_f.rearrange("p t (h c) -> p t h c", h=4),
                             spread(values[:, :, f0:f0 + 4], 3, 32)).then_inc(repeated, 1)
            pool.tensor_copy(heads(ka[:], 4)[:, :, :, MLA_NOPE:MLA_DIM],
                             spread(proj[:, :, tok("kr"):tok("kr") + 32], 2, 4)).then_inc(repeated, 1)
            pool.wait_ge(scaled, 2 * T)
            for v in range(2):
                c = tok("bk") + 64 * v
                pool.tensor_copy(heads(proj[:, :, P * v:P * (v + 1)], 2), spread(proj[:, :, c:c + 64], 2, 2)
                                 ).then_inc(repeated, 1)
            pool.tensor_copy(heads(proj[:, :, 2 * P:3 * P], 4),
                             spread(proj[:, :, tok("ki"):tok("ki") + 32], 2, 4)).then_inc(repeated, 1)

        @block.tensor
        def _(pe):
            pe.wait_ge(repeated, 1)
            for t in range(T):
                mm = pe.transpose(psum[:, 3, t * P:(t + 1) * P], spread_f[:, t, :], ident[:])
            mm.then_inc(gates_turned, 1)
            pe.wait_ge(scaled, 2 * T)
            for k in range(3):
                for t in range(T):
                    mm = pe.transpose(psum[:, k, t * P:(t + 1) * P], latent[:, t, k * P:(k + 1) * P], ident[:])
                mm.then_inc(turned, 1)
            pe.wait_ge(low, 2)
            product_by_tokens(pe, psum, 4, weights, latent_t[:, 0:2], 1, 2)
            pe.wait_ge(low, 3)
            pe.wait_ge(dve_own, 2)
            product_by_tokens(pe, psum, 0, weights, latent_t[:, 2:3], 1, 1)


def turn_heads(nc, psum, proj, qa, ka, turned, ident):
    groups = [(QA, 4, MLA_DIM), (KA, 4, MLA_DIM), (BQ, 4, P), (CQ, 4, P), (QI, 3, P)]

    def source(c, t):
        if c < KA:
            return qa[:, t, (c - QA) * MLA_DIM:(c - QA + 1) * MLA_DIM]
        if c < BQ:
            return ka[:, t, (c - KA) * MLA_DIM:(c - KA + 1) * MLA_DIM]
        for first, at in ((KI, 2 * P), (QI, tok("qi")), (CQ, tok("cq_")), (BK, 0), (BQ, tok("bq"))):
            if c >= first:
                return proj[:, t, at + (c - first) * P:at + (c - first + 1) * P]

    todo = [(g, t) for g in groups for t in range(T)]
    with stage(nc, "turned_banks stored_act stored_dve") as (turned_banks, stored_act, stored_dve), nc.Block() as block:
        @block.tensor
        def _(pe):
            for i, ((first, n, width), t) in enumerate(todo):
                if i >= 8:
                    pe.wait_ge((stored_act, stored_dve)[i % 2], (i - 8) // 2 + 1)
                for c in range(n):
                    mm = pe.transpose(psum[0:width, i % 8, c * P:(c + 1) * P], source(first + c, t), ident[:])
                mm.then_inc(turned_banks, 1)

        def copies(eng, half, copy, stored):
            for i, ((first, n, width), t) in enumerate(todo):
                if i % 2 == half:
                    eng.wait_ge(turned_banks, i + 1)
                    copy(turned[0:width, first:first + n, t * P:(t + 1) * P],
                         psum[0:width, i % 8, 0:n * P].rearrange("p (c q) -> p c q", c=n)).then_inc(stored, 1)

        @block.scalar
        def _(act):
            copies(act, 0, lambda out, bank: act.activation(out, bank, ACT.Copy), stored_act)

        @block.vector
        def _(dve):
            copies(dve, 1, lambda out, bank: dve.tensor_copy(out, bank), stored_dve)


TOP_K = 128
JOB_ORDER = "abdc"


def score_keys(nc, psum, values, turned, score, causal, relu):
    HEADS, DIM, B = 8, 32, 3
    assert TOP_K == P
    w0 = tok("w")
    todo = [(t, h) for t in range(1, T) for h in range(HEADS)]
    with stage(nc, "scored rectified weighed") as (scored, rectified, weighed), nc.Block() as block:
        @block.tensor
        def _(pe):
            for j, (t, h) in enumerate(todo):
                if j >= 8:
                    pe.wait_ge(rectified, j - 7)
                r = DIM * (h % 4)
                pe.matmul(psum[:, j % 8, 0:(t + 1) * P], turned[r:r + DIM, QI + h // 4, t * P:(t + 1) * P],
                          turned[r:r + DIM, KI, 0:(t + 1) * P], start=True, stop=True).then_inc(scored, 1)

        @block.scalar
        def _(act):
            for j, (t, h) in enumerate(todo):
                act.wait_ge(scored, j + 1)
                if j >= B:
                    act.wait_ge(weighed, j - B + 1)
                act.activation(relu[:, j % B, 0:(t + 1) * P], psum[:, j % 8, 0:(t + 1) * P],
                               ACT.Relu).then_inc(rectified, 1)

        @block.vector
        def _(dve):
            for j, (t, h) in enumerate(todo):
                w = (t + 1) * P
                dve.wait_ge(rectified, j + 1)
                before = causal[:, S - w:S] if h == 0 else score[:, t, 0:w]
                dve.scalar_tensor_tensor(out=score[:, t, 0:w], in0=relu[:, j % B, 0:w],
                                         scalar=values[:, t, w0 + h:w0 + h + 1], in1=before, op0=ALU.mult,
                                         op1=ALU.add).then_inc(weighed, 1)
                dve.wait_ge(weighed, j + 1)


def select_keys(chosen, best):
    per_tile = 2 * TOP_K // 8 + 1

    def step(dve, i):
        t, i = 1 + i // per_tile, i % per_tile
        s = chosen[:, t, 0:(t + 1) * P]
        if i == per_tile - 1:
            return dve.tensor_scalar(s, s, TAKEN / 2, MASKED, ALU.is_gt, ALU.mult)
        if i % 2 == 0:
            return dve.max(best[:], s)
        return dve.match_replace(s, best[:], s, TAKEN)
    return (T - 1) * per_tile, step


def layer_jobs(turned, values, gates, chosen, causal, window, sinks):
    jobs = []
    for group in JOB_ORDER:
        for h in range(4):
            r = 64 * (h % 2)
            for t in range(T):
                w = (t + 1) * P
                q, k0, blocks = slice(t * P, w), 0, list(range(t + 1))
                mask = causal[:, S - P:S]
                sink = None
                dense = False
                scale = 64 ** -0.5
                if group == "a":
                    scale = 96 ** -0.5
                    scores = [(turned[0:MLA_DIM, QA + h, q], turned[0:MLA_DIM, KA + h, 0:w])]
                    v0 = V_MLA + 64 * h
                    v = [values[:, b, v0:v0 + 64] for b in blocks]
                elif group == "b":
                    blocks = list(range(max(t - 1, 0), t + 1))
                    k0 = blocks[0] * P
                    mask = window[:, 2 * P - len(blocks) * P:2 * P]
                    sink = sinks[:, h:h + 1]
                    scores = [(turned[r:r + 64, BQ + h // 2, q], turned[r:r + 64, BK + h // 2, k0:w])]
                    v0 = tok("bv") + 64 * (h // 2)
                    v = [values[:, b, v0:v0 + 64] for b in blocks]
                elif group == "c":
                    if t:
                        mask = chosen[:, t, 0:w]
                        dense = True
                    scores = [(turned[r:r + 64, CQ + h // 2, q], turned[r:r + 64, CK + h // 2, 0:w])]
                    v0 = tok("cv") + 64 * h
                    v = [values[:, b, v0:v0 + 64] for b in blocks]
                else:
                    scores = [(turned[r:r + 64, DQ + h // 2, q], turned[r:r + 64, DK + h // 2, 0:w]),
                              (gates[32 * h:32 * h + 2, 0, q], gates[32 * h:32 * h + 2, 1, 0:w])]
                    v0 = tok("dv") + 64 * h
                    v = [values[:, b, v0:v0 + 64] for b in blocks]
                jobs.append(Job(scores, w - k0, mask, scale, v, r, t * P, sink, dense))
    return jobs



SPLITS_2 = dict(qa=1024, ka=1024, va=1024, za=1024, beta=8, a=8, qb=768, kb=768, vb=768, zb=768, ga=1024, gb=1024)
COL_2 = {}
_n = 0
for _k, _w in SPLITS_2.items():
    COL_2[_k] = _n
    _n += _w
H = 8
CONV = 4
CH = 64
N_CH = S // CH
LEVELS = 6
GROUPS = 3
DILATION = (1, 4, 16)


def norm_rows(nc, x, gain_row, work, small):
    gain, scaled_x = work[:, 0, :], work[:, 1:3, :]
    ss, ms, root, rstd = (small[:, 4 * i:4 * i + 4] for i in range(4))
    with stage(nc, "gain_landed squared mean_ready root_ready dve_own") as (
            gain_landed, squared, mean_ready, root_ready, dve_own), nc.Block() as block:
        @block.sync
        def _(sp):
            sp.dma_start(gain, gain_row.to_broadcast([P, D])).then_inc(gain_landed, 16)

        @block.scalar
        def _(act):
            for t in range(T):
                if t >= 2:
                    act.wait_ge(squared, t - 1)
                act.activation(scaled_x[:, t % 2, :], x[:, t, :], ACT.Square,
                               accum_out=ss[:, t:t + 1]).then_inc(squared, 1)
            act.wait_ge(mean_ready, 1)
            act.activation(root, ms, ACT.Sqrt).then_inc(root_ready, 1)

        @block.vector
        def _(dve):
            own = Chain(dve, dve_own)
            dve.wait_ge(squared, T)
            dve.tensor_scalar(ms, ss, 1.0 / D, EPS, ALU.mult, ALU.add).then_inc(mean_ready, 1)
            dve.wait_ge(root_ready, 1)
            own(dve.reciprocal(rstd, root))
            dve.wait_ge(gain_landed, 16)
            for t in range(T):
                own(dve.scalar_tensor_tensor(out=x[:, t, :], in0=x[:, t, :], scalar=rstd[:, t:t + 1], in1=gain,
                                             op0=ALU.mult, op1=ALU.mult))


def second_constants(nc, decay_mask, level_masks, pick, window_incl, residues):
    with stage(nc, "filled masked") as (filled, masked), nc.Block() as block:
        @block.vector
        def _(dve):
            own = Chain(dve, filled)
            own(dve.memset(decay_mask[:], 0.0))
            own(dve.memset(level_masks[:], 0.0))
            for i in range(LEVELS):
                s = 1 << i
                own(dve.memset(level_masks[:, i, :].rearrange("p (j a w) -> p j a w", a=2, w=s)[:, :, 1, :], 1.0))
            own(dve.memset(window_incl[:], 0.0))
            own(dve.memset(residues[:], 0.0))
            own(dve.memset(pick[:], 0.0))
            own(dve.memset(pick[:, 15:16], 1.0))

        @block.gpsimd
        def _(pool):
            pool.wait_ge(filled, 6 + LEVELS)
            own = Chain(pool, masked)

            def keep(view, pattern, base, channel, fill):
                own(pool.affine_select(out=view, in_=view, compare_op=ALU.is_ge, fill=fill, base=base,
                                       pattern=pattern, channel_multiplier=channel))
            keep(decay_mask[:], [[1, P]], 0, -1, MASKED)
            keep(decay_mask[:].rearrange("p (j w) -> p j w", w=CH), [[-CH, 2], [0, CH]], 0, 1, MASKED)
            for i in range(LEVELS):
                s = 1 << i
                half = level_masks[:, i, :].rearrange("p (j a w) -> p j a w", a=2, w=s)[:, :, 1, :]
                keep(half, [[-2 * s, P // (2 * s)], [0, s]], 0, 1, 0.0)
                keep(half, [[2 * s, P // (2 * s)], [0, s]], s - 1, -1, 0.0)
            keep(window_incl[:], [[1, 2 * P]], 0, -1, MASKED)
            keep(window_incl[:], [[-1, 2 * P]], P, 1, MASKED)
            keep(residues[:], [[-1, P]], 0, 1, MASKED)
            keep(residues[:].rearrange("p (j w) -> p j w", w=32), [[32, 4], [0, 32]], 31, -1, MASKED)


def modulation(nc, psum, weights, a, ident, ones, work, cols, conv_cols, modulated, gate_row, head_vecs, n_ada):
    vec_rows, conv_rows, silu_c, silu_pair, gate_bias, mod_rows = work
    n_cols = 41
    with stage(nc, "landed conv_landed bias_landed head_landed cleared turned dve_own silu_ready high low "
                   "rows_ready columns_ready") as (
            landed, conv_landed, bias_landed, head_landed, cleared, turned, dve_own, silu_ready,
            high, low, rows_ready, columns_ready), nc.Block() as block:
        @block.sync
        def _(sp):
            sp.wait_ge(cleared, 1)
            for r, name in ((0, "norm_w_2"), (8, "c_2"), (16, "ada_b_2"), (40, "dn_norm_w_2")):
                n = a[name].shape[1] // P
                sp.dma_start(vec_rows[r:r + n, :],
                             a[name].rearrange("o (r c) -> (o r) c", c=P)).then_inc(landed, 16)
            sp.dma_start(conv_rows[:], a["conv_w_2"].rearrange("o j (r c) -> (o j r) c", c=P)).then_inc(conv_landed, 16)
            weights.send(sp, n_ada)
            sp.dma_start(gate_bias[:], a["ada_b_2"][:, 2 * D:3 * D].to_broadcast([P, D])).then_inc(bias_landed, 16)
            for i, name in enumerate(("a_log_2", "dt_bias_2")):
                sp.dma_start(head_vecs[:, i:i + 1], a[name].rearrange("o (h u) -> (o h) u", u=1)).then_inc(head_landed, 16)
            sp.wait_ge(head_landed, 32)

        @block.tensor
        def _(pe):
            pe.wait_ge(landed, 64)
            pe.wait_ge(conv_landed, 16)
            pe.transpose(psum[:, 7, 0:64], vec_rows[:], ident[0:64, 0:64])
            pe.transpose(psum[:, 7, 64:160], conv_rows[:], ident[0:96, 0:96]).then_inc(turned, 1)
            pe.wait_ge(low, KD)
            for p in range(3 * D // 256):
                for i in range(2):
                    w = weights.take(pe)
                    for kk in range(KD // 2):
                        k = i * (KD // 2) + kk
                        mm = product(pe, psum[:, p // 2, 256 * (p % 2):256 * (p % 2 + 1)],
                                     [silu_pair[:, k, j, :] for j in (0, 1)], [w[j][:, kk, :] for j in (0, 1)],
                                     start=(k == 0), stop=(k == KD - 1))
                    weights.used(mm)
            pe.wait_ge(rows_ready, 4)
            for c in range(2 * KD):
                mm = pe.matmul(psum[:, 6, c:c + 1], mod_rows[:, c * P:(c + 1) * P], ident[:, 0:1], start=True, stop=True)
            mm.then_inc(columns_ready, 1)

        @block.scalar
        def _(act):
            act.wait_ge(dve_own, 2)
            act.activation(silu_c[:], cols[:, 8:16], ACT.Silu).then_inc(silu_ready, 1)
            act.wait_ge(silu_ready, 1)
            for k in range(KD):
                act.activation(silu_pair[:, k, 0, :], ones[:], ACT.Copy, scale=silu_c[:, k:k + 1]).then_inc(high, 1)
            for i in range(n_ada):
                weights.high(act, i)
            for b in range(4):
                act.wait_ge(weights.items_done, 4 * (b + 1))
                act.activation(mod_rows[:, 512 * b:512 * (b + 1)], psum[:, b, :], ACT.Copy).then_inc(rows_ready, 1)

        @block.vector
        def _(dve):
            own = Chain(dve, dve_own)
            dve.memset(vec_rows[:], 0.0).then_inc(cleared, 1)
            dve.wait_ge(turned, 1)
            own(dve.tensor_copy(cols[:], psum[:, 7, 0:64]))
            own(dve.tensor_copy(conv_cols[:], psum[:, 7, 64:160]))
            dve.wait_ge(silu_ready, 1)
            for k in range(KD):
                dve.wait_ge(high, k + 1)
                dve.scalar_tensor_tensor(out=silu_pair[:, k, 1, :], in0=ones[:], scalar=silu_c[:, k:k + 1],
                                         in1=silu_pair[:, k, 0, :].bitcast(F32), op0=ALU.mult,
                                         op1=ALU.subtract).then_inc(low, 1)
            own(dve.tensor_scalar(cols[:, 48:56], cols[:, 24:32], 1.0, None, ALU.add))
            for i in range(n_ada):
                weights.low(dve, i)
            dve.wait_ge(columns_ready, 1)
            own(dve.tensor_tensor(modulated[:, 8:16], psum[:, 6, 0:8], cols[:, 16:24], ALU.add))
            own(dve.tensor_tensor(modulated[:, 0:8], psum[:, 6, 8:16], cols[:, 48:56], ALU.add))
            own(dve.tensor_tensor(modulated[:, 0:8], modulated[:, 0:8], cols[:, 0:8], ALU.mult))
            dve.wait_ge(bias_landed, 16)
            for i in range(2):
                own(dve.tensor_tensor(gate_row[:, 512 * i:512 * (i + 1)], psum[:, 4 + i, :],
                                      gate_bias[:, 512 * i:512 * (i + 1)], ALU.add))


def conv_projection(nc, psum, weights, turned_x, qkv, rows, conv_cols, pick, head_vecs, work, end):
    before, squares, soft = work
    NB, SQ, BETA, DECAY = 4, 7, 5, 6
    NQ = 4
    CHUNKS = 3 * H
    with stage(nc, "copied convolved activated squared summed dve_own rows_exp rows_log "
                   "a_ready beta_ready zeroed") as (
            copied, convolved, activated, squared, summed, dve_own, rows_exp, rows_log,
            a_ready, beta_ready, zeroed), nc.Block() as block:
        @block.sync
        def _(sp):
            weights.send(sp, end)

        @block.tensor
        def _(pe):
            w = weights.take(pe)
            for bank, c in ((BETA, 0), (DECAY, H)):
                for k in range(KD):
                    mm = product(pe, psum[0:H, bank, :], [w[j][:, k, c:c + H] for j in (0, 1)],
                                 [turned_x[:, k, j, :] for j in (0, 1)], start=(k == 0), stop=(k == KD - 1))
            weights.used(mm)

            def sum_squares(c):
                pe.wait_ge(squared, c + 1)
                pe.matmul(psum[0:16, SQ, :], pick[:, 15 - c:31 - c], squares[:, c % NQ, :], start=(c == 0),
                          stop=(c == 2 * H - 1)).then_inc(summed, 1)

            for c in range(0, CHUNKS, 2):
                if c >= NB:
                    pe.wait_ge(copied, c - NB + 2)
                product_by_channels(pe, psum, (c % NB, c % NB + 1), weights, turned_x, KD)
                if 4 <= c < 2 * H + 4:
                    sum_squares(c - 4)
                    sum_squares(c - 3)

        start = end - CHUNKS

        @block.scalar
        def _(act):
            weights.high(act, start - 1)
            act.wait_ge(zeroed, 1)

            def silu(c):
                act.wait_ge(convolved, c + 1)
                act.activation(qkv[:, c, :], before[:, c % 3, 3:3 + S], ACT.Silu).then_inc(activated, 1)

            for c in range(CHUNKS + 1):
                if c < CHUNKS:
                    weights.high(act, start + c + 1)
                    if c % 2 == 0:
                        act.wait_ge(weights.items_done, start + c + 2)
                    if c >= 3:
                        act.wait_ge(activated, c - 2)
                    act.activation(before[:, c % 3, 3:3 + S], psum[:, c % NB, :], ACT.Copy).then_inc(copied, 1)
                if c >= 1:
                    silu(c - 1)
            act.wait_ge(a_ready, 1)
            act.activation(soft[:, 1, :], soft[:, 1, :], ACT.Exp, scale=-1.0).then_inc(rows_exp, 1)
            act.activation(head_vecs[:, 2:3], head_vecs[:, 0:1], ACT.Exp).then_inc(rows_exp, 1)
            act.wait_ge(a_ready, 2)
            act.activation(soft[:, 1, :], soft[:, 1, :], ACT.Ln).then_inc(rows_log, 1)
            act.wait_ge(weights.items_done, start)
            act.activation(rows[:, 0, :], psum[0:H, BETA, :], ACT.Sigmoid).then_inc(beta_ready, 1)

        def square(dve, c):
            dve.wait_ge(activated, c + 1)
            if c >= NQ:
                dve.wait_ge(summed, c - NQ + 1)
            dve.tensor_tensor(squares[:, c % NQ, :], qkv[:, c, :], qkv[:, c, :], ALU.mult).then_inc(squared, 1)

        @block.vector
        def _(dve):
            own = Chain(dve, dve_own)
            dve.memset(before[:, :, 0:3], 0.0).then_inc(zeroed, 1)
            weights.low(dve, start - 1)
            for c in range(CHUNKS):
                weights.low(dve, start + c + 1)
                dve.wait_ge(copied, c + 1)
                b = before[:, c % 3, :]
                acc = squares[:, NQ + c % 2, :]
                own(dve.tensor_scalar(acc, b[:, 0:S], conv_cols[:, c:c + 1], None, ALU.mult))
                for j in (1, 2):
                    own(dve.scalar_tensor_tensor(out=acc, in0=b[:, j:j + S], scalar=conv_cols[:, 24 * j + c:24 * j + c + 1],
                                                 in1=acc, op0=ALU.mult, op1=ALU.add))
                dve.scalar_tensor_tensor(out=b[:, 3:3 + S], in0=b[:, 3:3 + S],
                                         scalar=conv_cols[:, 72 + c:73 + c], in1=acc, op0=ALU.mult,
                                         op1=ALU.add).then_inc(convolved, 1)
                if c >= 1 and c - 1 < 2 * H:
                    square(dve, c - 1)
            own(dve.tensor_scalar(soft[:, 0, :], psum[0:H, DECAY, :], head_vecs[:, 1:2], None, ALU.add))
            dve.scalar_tensor_tensor(out=soft[:, 1, :], in0=soft[:, 0, :], scalar=-1.0, in1=soft[:, 0, :],
                                     op0=ALU.mult, op1=ALU.max).then_inc(a_ready, 1)
            dve.wait_ge(rows_exp, 2)
            dve.tensor_scalar(soft[:, 1, :], soft[:, 1, :], 1.0, None, ALU.add).then_inc(a_ready, 1)
            own(dve.tensor_scalar(head_vecs[:, 3:4], head_vecs[:, 2:3], -1.0, None, ALU.mult))
            dve.wait_ge(rows_log, 1)
            own(dve.scalar_tensor_tensor(out=soft[:, 0, :], in0=soft[:, 0, :], scalar=0.0, in1=soft[:, 1, :],
                                         op0=ALU.max, op1=ALU.add))
            own(dve.tensor_scalar(rows[:, 1, :], soft[:, 0, :], head_vecs[:, 3:4], None, ALU.mult))



def normalize_and_spread(nc, psum, qkv, rows, ident, onehot, k_tok, v_tok, tok_cols, last_decay, work,
                         row_stats):
    SQ = 7
    norms, = row_stats
    exps, lasts, restart = work
    with stage(nc, "dve_own q_done root_ready spread_done scaled k_turned stored_act stored_dve rows_exp lasts_ready "
                   "rows_turned") as (
            dve_own, q_done, root_ready, spread_done, scaled, k_turned, stored_act, stored_dve, rows_exp, lasts_ready,
            rows_turned), nc.Block() as block:
        @block.scalar
        def _(act):
            act.wait_ge(q_done, 1)
            act.activation(norms[:, 0, :], norms[:, 0, :], ACT.Sqrt).then_inc(root_ready, 1)
            act.wait_ge(lasts_ready, 1)
            act.activation(exps[:, 0, :], rows[:, 1, :], ACT.Exp).then_inc(rows_exp, 1)
            act.activation(exps[:, 1, :], exps[:, 1, :], ACT.Exp).then_inc(rows_exp, 1)
            act.activation(lasts[:], lasts[:], ACT.Exp).then_inc(rows_exp, 1)
            for i in range(16):
                act.wait_ge(k_turned, i + 1)
                if i % 2 == 0:
                    h = i % H
                    out = (k_tok if i < H else v_tok)[:, :, h * P:(h + 1) * P]
                    act.activation(out, psum[:, i % 4, :].rearrange("p (t c) -> p t c", t=T), ACT.Copy
                                   ).then_inc(stored_act, 1)

        @block.vector
        def _(dve):
            own = Chain(dve, dve_own)
            dve.tensor_scalar(norms[:, 0, :], psum[0:16, SQ, :], EPS, None, ALU.add).then_inc(q_done, 1)
            own(dve.memset(restart[:], 1.0))
            own(dve.memset(restart[:].rearrange("p (n c) -> p n c", c=CH)[:, :, 0:1], 0.0))
            own(dve.tensor_tensor_scan(exps[:, 0, :], restart[:], rows[:, 1, :], 0.0, ALU.mult, ALU.add))
            own(dve.tensor_copy(rows[:, 1, :], exps[:, 0, :]))
            by_chunk = rows[:, 1, :].rearrange("p (n c) -> p n c", c=CH)
            own(dve.tensor_copy(lasts[:].unsqueeze(2), by_chunk[:, :, CH - 1:CH]))
            dve.tensor_tensor(exps[:, 1, :].rearrange("p (n c) -> p n c", c=CH),
                              spread(lasts[:], 2, CH), by_chunk, ALU.subtract).then_inc(lasts_ready, 1)
            dve.wait_ge(root_ready, 1)
            own(dve.reciprocal(norms[:, 1, :], norms[:, 0, :]))
            for c in range(2 * H):
                dve.wait_ge(spread_done, c + 1)
                if c < H:
                    dve.scalar_tensor_tensor(out=qkv[:, c, :], in0=qkv[:, c, :], scalar=float(P) ** -0.5,
                                             in1=psum[:, 4 + c % 3, :], op0=ALU.mult, op1=ALU.mult).then_inc(scaled, 1)
                else:
                    dve.tensor_tensor(qkv[:, c, :], qkv[:, c, :], psum[:, 4 + c % 3, :], ALU.mult).then_inc(scaled, 1)
            for i in range(16):
                dve.wait_ge(k_turned, i + 1)
                if i % 2 == 1:
                    h = i % H
                    out = (k_tok if i < H else v_tok)[:, :, h * P:(h + 1) * P]
                    dve.tensor_copy(out, psum[:, i % 4, :].rearrange("p (t c) -> p t c", t=T)).then_inc(stored_dve, 1)
            dve.wait_ge(rows_turned, 1)
            own(dve.tensor_copy(tok_cols[:].rearrange("p a t h -> p (a t h)"), psum[:, 4, 0:4 * T * H]))
            own(dve.tensor_tensor(tok_cols[:, 2], tok_cols[:, 2], tok_cols[:, 0], ALU.mult))
            own(dve.tensor_copy(last_decay[:].rearrange("p h n -> p (h n)"), psum[:, 5, 0:H * N_CH]))

        @block.tensor
        def _(pe):
            pe.wait_ge(dve_own, 6)
            for c in range(2 * H):
                if c >= 3:
                    pe.wait_ge(scaled, c - 2)
                pe.matmul(psum[:, 4 + c % 3, :], onehot[0:16, c, :], norms[:, 1, :], start=True,
                          stop=True).then_inc(spread_done, 1)
            for i in range(16):
                if i < H:
                    pe.wait_ge(scaled, H + i + 1)
                if i >= 4:
                    if i % 2 == 0:
                        pe.wait_ge(stored_act, (i - 4) // 2 + 1)
                    else:
                        pe.wait_ge(stored_dve, (i - 4) // 2 + 1)
                for t in range(T):
                    mm = pe.transpose(psum[:, i % 4, t * P:(t + 1) * P], qkv[:, H + i, t * P:(t + 1) * P], ident[:])
                mm.then_inc(k_turned, 1)
            pe.wait_ge(scaled, 2 * H)
            pe.wait_ge(rows_exp, 3)
            for i, src in enumerate((rows[:, 0, :], rows[:, 1, :], exps[:, 0, :], exps[:, 1, :])):
                for t in range(T):
                    o = (i * T + t) * H
                    pe.transpose(psum[:, 4, o:o + H], src[:, t * P:(t + 1) * P], ident[0:H, 0:H])
            for h in range(H):
                mm = pe.matmul(psum[:, 5, h * N_CH:(h + 1) * N_CH], onehot[0:H, h, :], lasts[:], start=True, stop=True)
            mm.then_inc(rows_turned, 1)


def delta_prepare(nc, psum, q_t, k_t, attn_t, k_tok, v_tok, rows, tok_cols, decay_mask, level_masks, ident, onehot,
                  sbx):
    G, HG = 2, 4
    dec, lt, x_m, x_t, y = (sbx(n, [P, G, HG * P]) for n in ("decays", "lower_t", "inverse", "inverse_t", "y"))
    eg = y
    lms = sbx("level_lower", [P, G, 2, HG * P])
    heads = lambda ap: ap.rearrange("p (h c) -> p h c", h=HG)
    ML = LEVELS - 1
    order = [(t, g) for t in range(T) for g in range(G)]
    with stage(nc, "formed argued decayed exp_ready attn_ready lower_ready started level_ready flipped inverse_ready y_done y_copied "
                   "z_done refined v_ready k_ready solved stored dve_own pool_own q_decayed") as (
            formed, argued, decayed, exp_ready, attn_ready, lower_ready, started, level_ready, flipped, inverse_ready,
            y_done, y_copied, z_done, refined, v_ready, k_ready, solved, stored, dve_own, pool_own,
            q_decayed), nc.Block() as block:
        @block.tensor
        def _(pe):
            for t in range(T):
                tile = slice(t * P, (t + 1) * P)
                for g in range(G):
                    i = t * G + g
                    if t:
                        pe.wait_ge(stored, i - 1)
                    b = 4 * g
                    for hh in range(HG):
                        h = HG * g + hh
                        c = slice(hh * P, (hh + 1) * P)
                        pe.matmul(psum[:, b, c], onehot[0:H, h, :], rows[:, 1, tile], start=True, stop=True)
                        pe.matmul(psum[:, b + 1, c], onehot[0:H, h, :], rows[:, 0, tile], start=True, stop=True)
                        pe.matmul(psum[:, b + 2, c], k_t[:, h, tile], k_t[:, h, tile], start=True, stop=True)
                        mm = pe.matmul(psum[:, b + 3, c], k_t[:, h, tile], q_t[:, h, tile], start=True, stop=True)
                    mm.then_inc(formed, 1)
                for g in range(G):
                    pe.wait_ge(started, t * G + g + 1)
                    pe.wait_ge(exp_ready, t * G + g + 1)
                    for hh in range(HG):
                        c = slice(hh * P, (hh + 1) * P)
                        mm = pe.transpose(psum[:, 4 * g, c], x_t[:, g, c], ident[:])
                    mm.then_inc(flipped, 1)
                for lv in range(ML):
                    for g in range(G):
                        i = (t * ML + lv) * G + g
                        pe.wait_ge(level_ready, i + 1)
                        if lv == 0:
                            pe.wait_ge(inverse_ready, t * G + g + 1)
                        else:
                            pe.wait_ge(refined, i - G + 1)
                        for hh in range(HG):
                            c = slice(hh * P, (hh + 1) * P)
                            mm = pe.matmul(psum[:, 4 * g + 1, c], lms[:, g, lv % 2, c], x_m[:, g, c], start=True, stop=True)
                        mm.then_inc(y_done, 1)
                    for g in range(G):
                        i = (t * ML + lv) * G + g
                        pe.wait_ge(y_copied, i + 1)
                        for hh in range(HG):
                            c = slice(hh * P, (hh + 1) * P)
                            mm = pe.matmul(psum[:, 4 * g + 2, c], y[:, g, c], x_t[:, g, c], start=True, stop=True)
                            if lv < ML - 1:
                                mm = pe.matmul(psum[:, 4 * g + 3, c], x_t[:, g, c], y[:, g, c], start=True, stop=True)
                        mm.then_inc(z_done, 1)
                for g in range(G):
                    i = t * G + g
                    pe.wait_ge(refined, (t * ML + ML - 1) * G + g + 1)
                    pe.wait_ge(v_ready, i + 1)
                    pe.wait_ge(k_ready, i + 1)
                    for hh in range(HG):
                        c = slice(hh * P, (hh + 1) * P)
                        pe.matmul(psum[:, 4 * g, c], x_t[:, g, c], dec[:, g, c], start=True, stop=True)
                        mm = pe.matmul(psum[:, 4 * g + 1, c], lt[:, g, c], x_t[:, g, c], start=True, stop=True)
                    mm.then_inc(solved, 1)

        @block.scalar
        def _(act):
            for t in range(T):
                tile = slice(t * P, (t + 1) * P)
                for g in range(G):
                    i = t * G + g
                    act.wait_ge(argued, i + 1)
                    act.activation(dec[:, g, :], dec[:, g, :], ACT.Exp).then_inc(decayed, 1)
                    act.activation(eg[:, g, :], psum[:, 4 * g, :], ACT.Exp).then_inc(exp_ready, 1)
                for g in range(G):
                    act.wait_ge(flipped, t * G + g + 1)
                    act.activation(x_m[:, g, :], psum[:, 4 * g, :], ACT.Copy).then_inc(inverse_ready, 1)
                for lv in range(ML):
                    for g in range(G):
                        i = (t * ML + lv) * G + g
                        act.wait_ge(y_done, i + 1)
                        if lv == 0:
                            act.wait_ge(q_decayed, t * G + g + 1)
                        act.activation(y[:, g, :], psum[:, 4 * g + 1, :], ACT.Copy).then_inc(y_copied, 1)
                for g in range(G):
                    i = t * G + g
                    act.wait_ge(solved, i + 1)
                    act.activation(v_tok[:, t, HG * g * P:HG * (g + 1) * P], psum[:, 4 * g, :], ACT.Copy)
                    act.activation(k_t[:, HG * g:HG * (g + 1), tile], heads(psum[:, 4 * g + 1, :]),
                                   ACT.Copy).then_inc(stored, 1)

        @block.vector
        def _(dve):
            own = Chain(dve, dve_own)
            for t in range(T):
                for g in range(G):
                    i = t * G + g
                    dve.wait_ge(formed, i + 1)
                    if t:
                        dve.wait_ge(solved, i - 1)
                    cols = tok_cols[:, 1, t, HG * g:HG * (g + 1)]
                    own(dve.tensor_tensor(heads(dec[:, g, :]), heads(psum[:, 4 * g, :]), spread(cols, 2, P), ALU.subtract))
                    dve.tensor_tensor(heads(dec[:, g, :]), heads(dec[:, g, :]), spread(decay_mask[:], 1, HG),
                                      ALU.add).then_inc(argued, 1)
                for g in range(G):
                    i = t * G + g
                    dve.wait_ge(decayed, i + 1)
                    dve.tensor_tensor(attn_t[:, t, HG * g * P:HG * (g + 1) * P], psum[:, 4 * g + 3, :],
                                      dec[:, g, :], ALU.mult).then_inc(attn_ready, 1)
                    own(dve.tensor_tensor(lt[:, g, :], psum[:, 4 * g + 2, :], dec[:, g, :], ALU.mult))
                    own(dve.tensor_tensor(lt[:, g, :], lt[:, g, :], psum[:, 4 * g + 1, :], ALU.mult))
                    dve.sem_inc(lower_ready, 1)
                    own(dve.tensor_tensor(heads(x_t[:, g, :]), heads(lt[:, g, :]), spread(level_masks[:, 0, :], 1, HG), ALU.mult))
                    dve.tensor_tensor(heads(x_t[:, g, :]), spread(ident[:], 1, HG), heads(x_t[:, g, :]),
                                      ALU.subtract).then_inc(started, 1)
                for lv in range(ML):
                    for g in range(G):
                        i = (t * ML + lv) * G + g
                        dve.wait_ge(z_done, i + 1)
                        if lv < ML - 1:
                            own(dve.tensor_tensor(x_m[:, g, :], x_m[:, g, :], psum[:, 4 * g + 3, :], ALU.subtract))
                        dve.tensor_tensor(x_t[:, g, :], x_t[:, g, :], psum[:, 4 * g + 2, :], ALU.subtract).then_inc(refined, 1)

        @block.gpsimd
        def _(pool):
            own = Chain(pool, pool_own)
            for t in range(T):
                tile = slice(t * P, (t + 1) * P)
                for lv in range(ML):
                    for g in range(G):
                        i = (t * ML + lv) * G + g
                        if lv == 0:
                            pool.wait_ge(lower_ready, t * G + g + 1)
                        if i - 2 * G >= 0:
                            pool.wait_ge(y_done, i - 2 * G + 1)
                        pool.tensor_tensor(heads(lms[:, g, lv % 2, :]), heads(lt[:, g, :]),
                                           spread(level_masks[:, lv + 1, :], 1, HG), ALU.mult).then_inc(level_ready, 1)
                    if lv == 0:
                        for g in range(G):
                            i = t * G + g
                            hs = slice(HG * g, HG * (g + 1))
                            pool.wait_ge(exp_ready, i + 1)
                            pool.tensor_tensor(q_t[:, hs, tile], q_t[:, hs, tile], heads(eg[:, g, :]), ALU.mult).then_inc(q_decayed, 1)
                            pool.wait_ge(attn_ready, i + 1)
                            pool.tensor_tensor(heads(dec[:, g, :]), heads(v_tok[:, t, HG * g * P:HG * (g + 1) * P]),
                                               spread(tok_cols[:, 0, t, hs], 2, P), ALU.mult).then_inc(v_ready, 1)
                for g in range(G):
                    i = t * G + g
                    hs = slice(HG * g, HG * (g + 1))
                    kk = heads(k_tok[:, t, HG * g * P:HG * (g + 1) * P])
                    pool.wait_ge(level_ready, (t * ML + ML - 1) * G + g + 1)
                    pool.wait_ge(started, i + 1)
                    pool.tensor_tensor(heads(lt[:, g, :]), kk, spread(tok_cols[:, 2, t, hs], 2, P), ALU.mult).then_inc(k_ready, 1)
                    pool.wait_ge(k_ready, i + 1)
                    own(pool.tensor_tensor(kk, kk, spread(tok_cols[:, 3, t, hs], 2, P), ALU.mult))


def delta_scan(nc, psum, q_t, w_t, attn_t, k_tok, u, last_decay, state):
    G, HG = 2, 4
    with stage(nc, "read_state v_ready products o_stored state_ready") as (
            read_state, v_ready, products, o_stored, state_ready), nc.Block() as block:
        def place(n):
            return n // 2, CH * (n % 2)

        def done(n, g):
            return G * n + g + 1

        @block.tensor
        def _(pe):
            for n in range(N_CH):
                t, b = place(n)
                chunk = slice(t * P + b, t * P + b + CH)
                rows = slice(b, b + CH)
                for g in range(G):
                    if n:
                        pe.wait_ge(state_ready, HG * done(n - 1, g))
                        for h in range(HG * g, HG * (g + 1)):
                            c = slice((h % HG) * P, (h % HG + 1) * P)
                            mm = pe.matmul(psum[rows, g, c], w_t[:, h, chunk], state[:, h, :], start=True, stop=True)
                        mm.then_inc(read_state, 1)
                for g in range(G):
                    if n:
                        pe.wait_ge(o_stored, done(n - 1, g))
                        pe.wait_ge(v_ready, done(n - 1, g))
                    for h in range(HG * g, HG * (g + 1)):
                        c = slice((h % HG) * P, (h % HG + 1) * P)
                        hc = slice(h * P, (h + 1) * P)
                        if n:
                            pe.matmul(psum[rows, 2 + g, c], q_t[:, h, chunk], state[:, h, :], start=True, stop=False)
                        mm = pe.matmul(psum[rows, 2 + g, c], attn_t[rows, t, h * P + b:h * P + b + CH], u[rows, t, hc],
                                       start=(n == 0), stop=True)
                        if n < N_CH - 1:
                            mm = pe.matmul(psum[:, 4 + g, c], k_tok[rows, t, hc], u[rows, t, hc], start=True, stop=True)
                    mm.then_inc(products, 1)

        @block.vector
        def _(dve):
            for n in range(N_CH):
                t, b = place(n)
                for g in range(G):
                    if n:
                        c = slice(512 * g, 512 * (g + 1))
                        dve.wait_ge(read_state, done(n - 1, g))
                        dve.tensor_tensor(u[b:b + CH, t, c], u[b:b + CH, t, c], psum[b:b + CH, g, :],
                                          ALU.subtract).then_inc(v_ready, 1)
                if n == N_CH - 1:
                    break
                for g in range(G):
                    dve.wait_ge(products, done(n, g))
                    for h in range(HG * g, HG * (g + 1)):
                        kv = psum[:, 4 + g, (h % HG) * P:(h % HG + 1) * P]
                        if n:
                            dve.scalar_tensor_tensor(out=state[:, h, :], in0=state[:, h, :],
                                                     scalar=last_decay[:, h, n:n + 1], in1=kv, op0=ALU.mult,
                                                     op1=ALU.add).then_inc(state_ready, 1)
                        else:
                            dve.tensor_copy(state[:, h, :], kv).then_inc(state_ready, 1)

        @block.scalar
        def _(act):
            for n in range(N_CH):
                t, b = place(n)
                for g in range(G):
                    act.wait_ge(products, done(n, g))
                    act.activation(attn_t[b:b + CH, t, 512 * g:512 * (g + 1)], psum[b:b + CH, 2 + g, :],
                                   ACT.Copy).then_inc(o_stored, 1)


def channel_products(nc, psum, weights, pair, chunks, epilogues, also=None, names=""):
    n = len(epilogues)
    start = weights.taken
    end = start + n
    act_before = [sum(1 for e in epilogues[:c] if e[0] == "act") for c in range(n + 1)]
    dve_before = [c - act_before[c] for c in range(n + 1)]
    with stage(nc, "stored_act stored_dve dve_own " + names) as sems, nc.Block() as block:
        stored_act, stored_dve, dve_own = sems[0:3]

        @block.sync
        def _(sp):
            weights.send(sp, end)

        @block.tensor
        def _(pe):
            for c in range(0, n, 2):
                if c >= 8:
                    if act_before[c - 6]:
                        pe.wait_ge(stored_act, act_before[c - 6])
                    if dve_before[c - 6]:
                        pe.wait_ge(stored_dve, dve_before[c - 6])
                product_by_channels(pe, psum, (c % 8, c % 8 + 1), weights, pair, chunks)

        @block.scalar
        def _(act):
            for c, e in enumerate(epilogues):
                weights.high(act, start + c)
                if also and c < len(also[0]):
                    also[0][c](act, sems[3:])
                weights.high(act, start + c + 1)
                if e[0] == "act":
                    act.wait_ge(weights.items_done, start + 2 * (c // 2) + 2)
                    act.activation(e[2], e[3](psum[:, c % 8, :]), e[1]).then_inc(stored_act, 1)

        @block.vector
        def _(dve):
            own = Chain(dve, dve_own)
            for c, e in enumerate(epilogues):
                weights.low(dve, start + c)
                if also and c < len(also[1]):
                    also[1][c](dve, sems[3:])
                weights.low(dve, start + c + 1)
                if e[0] == "dve":
                    dve.wait_ge(weights.items_done, start + 2 * (c // 2) + 2)
                    for s in e[1][:-1]:
                        own(s(dve, psum[:, c % 8, :]))
                    e[1][-1](dve, psum[:, c % 8, :]).then_inc(stored_dve, 1)


def same(bank):
    return bank


def permuted(view, group):
    if group == 0:
        return view
    return view.rearrange("p (s r) -> p r s", r=DILATION[group])


def in_order(view, group):
    if group == 0:
        return view
    return view.rearrange("p (r s) -> p r s", r=DILATION[group])


def second_part(nc, psum, x, weights, consts, a):
    ident, ones, causal, window, onehot, gate_forms = consts

    with ExitStack() as all2:
        def sb(name, shape, ctx=all2, dtype=F32):
            return ctx.enter_context(nc.sbuf_tensor(name, shape, dtype))

        one = lambda name: a[name].rearrange("o r c -> (o r) c")
        ada, win, wa, wb, wout = (one(n) for n in ("ada_w_2", "w_in_2", "w_proj_a_2", "w_proj_b_2", "w_out_2"))
        KB = wb.shape[0] // P

        def project(*names):
            return [i for n in names for i in for_channels(win, KD, COL_2[n], COL_2[n] + SPLITS_2[n])]

        items = for_channels(ada, KD, 0, 3 * D)
        n_ada = len(items)
        items.append(rows(win, 0, KD, COL_2["beta"], COL_2["beta"] + 16))
        items += project("qa", "ka", "va")
        n_conv = len(items)
        items += project("za", "ga") + for_channels(wa, KD, 0, D)
        items += project("qb", "kb", "vb", "zb", "gb") + for_channels(wb, KB, 0, D)
        out_items = for_tokens(wout, KD, 0, 512) + for_tokens(wout, KD, 512, D)
        weights.restart(items + out_items)

        small = sb("small_2", [P, 32])
        cols = sb("cols_2", [P, 64])
        conv_cols = sb("conv_cols", [P, CONV * 3 * H])
        modulated = sb("modulated", [P, 16])
        gate_row = sb("gate_row", [P, D])
        head_vecs = sb("head_vecs", [H, 4])
        window_incl = sb("window_incl", [P, 2 * P])
        residues = sb("residues", [P, P])
        with ExitStack() as ctx:
            norm_rows(nc, x, a["final_norm"].rearrange("(o d) -> o d", o=1), sb("norm_work", [P, 3, D], ctx), small)
            work = (sb("vec_rows_2", [64, P], ctx), sb("conv_rows", [96, P], ctx), sb("silu_c", [P, KD], ctx),
                    sb("silu_pair", [P, KD, 2, P], ctx, F32R), sb("gate_bias", [P, D], ctx),
                    sb("mod_rows", [P, 2 * D], ctx))
            modulation(nc, psum, weights, a, ident, ones, work, cols, conv_cols, modulated, gate_row, head_vecs, n_ada)

        qkv = sb("qkv", [P, 3 * H, S])
        part = [qkv[:, H * i:H * (i + 1), :] for i in range(3)]
        token_major = [p.rearrange("p k s -> p (k s)").rearrange("p (t c) -> p t c", t=T) for p in part]
        attn_t = token_major[2]
        with ExitStack() as delta:
            decay_mask = sb("decay_mask", [P, P], delta)
            level_masks = sb("level_masks", [P, LEVELS, P], delta)
            pick = sb("pick", [P, 31], delta)
            second_constants(nc, decay_mask, level_masks, pick, window_incl, residues)
            heads_rows = sb("heads_rows", [H, 2, S], delta)
            tok_cols = sb("tok_cols", [P, 4, T, H], delta)
            last_decay = sb("last_decay", [P, H, N_CH], delta)
            with ExitStack() as ctx:
                turned_x = sb("turned_x2", [P, KD, 2, S], ctx, F32R)
                squares = sb("squares", [P, 6, S], ctx)
                norm_and_turn(nc, psum, x, token_major[2], modulated[:, 0:8], turned_x, ident, small,
                              bias=modulated[:, 8:16], work=squares)
                conv_projection(nc, psum, weights, turned_x, qkv, heads_rows, conv_cols, pick, head_vecs,
                                (sb("before", [P, 3, S + 3], ctx), squares, sb("soft", [H, 2, S], ctx)), n_conv)
            k_tok = sb("k_tok", [P, T, D], delta)
            v_tok = sb("v_tok", [P, T, D], delta)
            with ExitStack() as ctx:
                normalize_and_spread(nc, psum, qkv, heads_rows, ident, onehot, k_tok, v_tok, tok_cols,
                                     last_decay, (sb("exps", [H, 2, S], ctx), sb("lasts", [H, N_CH], ctx),
                                                  sb("restart", [H, S], ctx)),
                                     (sb("norms", [16, 2, S], ctx),))
            with ExitStack() as ctx:
                delta_prepare(nc, psum, part[0], part[1], attn_t, k_tok, v_tok, heads_rows, tok_cols, decay_mask,
                              level_masks, ident, onehot, lambda n, s: sb(n, s, ctx))
            with ExitStack() as ctx:
                delta_scan(nc, psum, part[0], part[1], attn_t, k_tok, v_tok, last_decay,
                           sb("state", [P, H, P], ctx))

        turned_x = sb("turned_x3", [P, KD, 2, S], dtype=F32R)
        norm_and_turn(nc, psum, x, token_major[1], modulated[:, 0:8], turned_x, ident, small,
                      bias=modulated[:, 8:16], work=qkv)
        merged = part[2]
        with ExitStack() as ctx:
            o_stats = sb("o_stats", [P, 4, T * H], ctx)
            y_a = part[0]
            junk = token_major[1]

            def square_o(t):
                def step(act, sems):
                    for h in range(H):
                        i = t * H + h
                        act.activation(junk[:, t, h * P:(h + 1) * P], attn_t[:, t, h * P:(h + 1) * P], ACT.Square,
                                       accum_out=o_stats[:, 0, i:i + 1]).then_inc(sems[0], 1)
                return step

            def root_o(act, sems):
                act.wait_ge(sems[1], 1)
                act.activation(o_stats[:, 2, :], o_stats[:, 1, :], ACT.Sqrt).then_inc(sems[2], 1)

            def mean_o(dve, sems):
                dve.wait_ge(sems[0], T * H)
                dve.tensor_scalar(o_stats[:, 1, :], o_stats[:, 0, :], 1.0 / P, EPS, ALU.mult, ALU.add).then_inc(sems[1], 1)

            def norm_o(dve, sems):
                own = Chain(dve, sems[3])
                dve.wait_ge(sems[2], 1)
                own(dve.reciprocal(o_stats[:, 3, :], o_stats[:, 2, :]))
                for t in range(T):
                    o = attn_t[:, t, :].rearrange("p (h c) -> p h c", h=H)
                    own(dve.tensor_tensor(o, o, spread(o_stats[:, 3, t * H:(t + 1) * H], 2, P), ALU.mult))

            nothing = lambda eng, sems: None
            channel_products(nc, psum, weights, turned_x, KD, [("act", ACT.Silu, y_a[:, c, :], same) for c in range(H)],
                             also=([square_o(t) for t in range(T)] + [root_o], [nothing] * T + [mean_o, norm_o]),
                             names="o_squared o_mean o_root o_own")
            y_pair = sb("y_a_pair", [P, KD, 2, S], ctx, F32R)
            with stage(nc, "turned gated high low") as (turned, gated, high, low), nc.Block() as block:
                @block.tensor
                def _(pe):
                    for h in range(H):
                        for t in range(T):
                            mm = pe.transpose(psum[:, h, t * P:(t + 1) * P], attn_t[:, t, h * P:(h + 1) * P], ident[:])
                        mm.then_inc(turned, 1)

                @block.scalar
                def _(act):
                    for h in range(H):
                        act.wait_ge(gated, h + 1)
                        act.activation(y_pair[:, h, 0, :], y_a[:, h, :], ACT.Copy).then_inc(high, 1)

                @block.vector
                def _(dve):
                    def rest(h):
                        dve.wait_ge(high, h + 1)
                        dve.tensor_tensor(y_pair[:, h, 1, :], y_a[:, h, :], y_pair[:, h, 0, :].bitcast(F32),
                                          ALU.subtract).then_inc(low, 1)

                    for h in range(H):
                        dve.wait_ge(turned, h + 1)
                        dve.scalar_tensor_tensor(out=y_a[:, h, :], in0=psum[:, h, :], scalar=cols[:, 40:41],
                                                 in1=y_a[:, h, :], op0=ALU.mult, op1=ALU.mult).then_inc(gated, 1)
                        if h >= 1:
                            rest(h - 1)
                    rest(H - 1)
            gate_a = part[1]
            channel_products(nc, psum, weights, turned_x, KD,
                             [("act", ACT.Sigmoid, gate_a[:, c, :], same) for c in range(KD)])

            def times(c):
                return lambda dve, bank: dve.tensor_tensor(merged[:, c, :], bank, gate_a[:, c, :], ALU.mult)

            channel_products(nc, psum, weights, y_pair, KD, [("dve", [times(c)]) for c in range(KD)])
        with ExitStack() as ctx:
            dilated(nc, psum, weights, turned_x, qkv, merged, KB, window_incl, causal, residues, ident, onehot, sb, ctx)
        split_operand(nc, lambda k: merged[:, k, :], turned_x, KD)
        output_products(nc, psum, x, weights, turned_x, KD, len(out_items) // 2, gate=(gate_row, qkv[:, 0:2, :]))
        with ExitStack() as ctx:
            norm_rows(nc, x, a["final_norm_w_2"].rearrange("(o d) -> o d", o=1), sb("norm_work_2", [P, 3, D], ctx), small)


def dilated(nc, psum, weights, turned_x, free_chunks, merged, KB, window_incl, causal, residues, ident, onehot, sb,
            ctx):
    C = KB
    q, k = (free_chunks[:, C * i:C * (i + 1), :] for i in range(2))
    v_t = sb("v_turned", [P, C, S], ctx)
    v = sb("v_rows", [P, T, C * P], ctx)
    eps = []
    for name, dst in (("q", q), ("k", k), ("v", v_t)):
        for c in range(C):
            g = c // 2
            eps.append(("act", ACT.Copy, in_order(dst[:, c, :], g), lambda bank, g=g: permuted(bank, g)))
    channel_products(nc, psum, weights, turned_x, KD, eps)
    with stage(nc, "turned stored") as (turned, stored), nc.Block() as block:
        @block.tensor
        def _(pe):
            for c in range(C):
                for b in range(T):
                    mm = pe.transpose(psum[:, c, b * P:(b + 1) * P], v_t[:, c, b * P:(b + 1) * P], ident[:])
                mm.then_inc(turned, 1)

        @block.scalar
        def _(act):
            for c in range(C):
                act.wait_ge(turned, c + 1)
                act.activation(v[:, :, c * P:(c + 1) * P], psum[:, c, :].rearrange("p (t c) -> p t c", t=T),
                               ACT.Copy).then_inc(stored, 1)

    y = v_t
    jobs = []
    for g in range(GROUPS):
        for i in range(4):
            c = 2 * g + i // 2
            r = 64 * (i % 2)
            for b in range(T):
                blocks = [b] if g else list(range(max(b - 1, 0), b + 1))
                w = len(blocks) * P
                keys = slice(blocks[0] * P, (b + 1) * P)
                mask = (window_incl[:, 2 * P - w:2 * P], causal[:, S - P:S], residues[:])[g]
                jobs.append(Job([(q[r:r + 64, c, b * P:(b + 1) * P], k[r:r + 64, c, keys])], w, mask, 64 ** -0.5,
                                [v[:, kb, c * P + r:c * P + r + 64] for kb in blocks], r, b * P))
    stores = [(permuted(y[:, c, :], c // 2), lambda bank, g=c // 2: in_order(bank, g), None)
              for c in range(C)]
    stats = sb("stats_2", [P, 5, len(jobs)], ctx)
    with ExitStack() as c2:
        with stage(nc, ATTENTION_SEMS) as sems:
            attention(nc, psum, jobs, stores, ident, sb("probs2", [P, 6, 2 * P], c2),
                      sb("probs_t2", [P, 3, 2 * P], c2), stats, sems)
    z = free_chunks[:, 0:C, :]
    gate_b = free_chunks[:, C:C + KD, :]
    channel_products(nc, psum, weights, turned_x, KD,
                     [("act", ACT.Silu, z[:, c, :], same) for c in range(C)]
                     + [("act", ACT.Sigmoid, gate_b[:, c, :], same) for c in range(KD)])
    with ExitStack() as c2:
        lse = sb("lse", [4, GROUPS, S], c2)
        top = sb("top", [4, 2, S], c2)
        pair = sb("pair", [4, 2, P], c2)
        with stage(nc, "logged lse_ready turned dve_own powered spread_done weighed") as (
                logged, lse_ready, turned, dve_own, powered, spread_done, weighed), nc.Block() as block:
            @block.scalar
            def _(act):
                act.activation(stats[:, 2, :], stats[:, 1, :], ACT.Ln).then_inc(logged, 1)
                act.wait_ge(dve_own, 3 + GROUPS + 2 + GROUPS)
                act.activation(lse[:], lse[:], ACT.Exp).then_inc(powered, 1)

            @block.vector
            def _(dve):
                own = Chain(dve, dve_own)
                dve.wait_ge(logged, 1)
                own(dve.tensor_tensor(stats[:, 3, :], stats[:, 2, :], stats[:, 0, :], ALU.subtract))
                for j in range(2):
                    own(dve.tensor_copy(pair[:, j, :].rearrange("p (a c) -> p a c", a=2),
                                        onehot[0:4, 2 * j:2 * j + 2, 0:64]))
                dve.wait_ge(turned, 1)
                for g in range(GROUPS):
                    own(dve.tensor_copy(lse[:, g, :], psum[0:4, g, :]))
                own(dve.tensor_tensor(top[:, 0, :], lse[:, 0, :], lse[:, 1, :], ALU.max))
                own(dve.tensor_tensor(top[:, 0, :], top[:, 0, :], lse[:, 2, :], ALU.max))
                for g in range(GROUPS):
                    own(dve.tensor_tensor(lse[:, g, :], lse[:, g, :], top[:, 0, :], ALU.subtract))
                dve.wait_ge(powered, 1)
                own(dve.tensor_tensor(top[:, 0, :], lse[:, 0, :], lse[:, 1, :], ALU.add))
                own(dve.tensor_tensor(top[:, 0, :], top[:, 0, :], lse[:, 2, :], ALU.add))
                own(dve.reciprocal(top[:, 1, :], top[:, 0, :]))
                for g in range(GROUPS):
                    own(dve.tensor_tensor(lse[:, g, :], lse[:, g, :], top[:, 1, :], ALU.mult))
                for c in range(C):
                    dve.wait_ge(spread_done, c + 1)
                    own(dve.tensor_tensor(y[:, c, :], y[:, c, :], psum[:, c, :], ALU.mult))
                    dve.tensor_tensor(y[:, c, :], y[:, c, :], z[:, c, :], ALU.mult).then_inc(weighed, 1)

            @block.tensor
            def _(pe):
                pe.wait_ge(dve_own, 1)
                for g in range(GROUPS):
                    for b in range(T):
                        src = stats[:, 3, 16 * g + b:16 * g + b + 13:4]
                        out = permuted(psum[0:4, g, :], g)
                        if g == 0:
                            out = out[:, b * P:(b + 1) * P]
                        elif g == 1:
                            out = out[:, b, :]
                        else:
                            out = out[:, 4 * b:4 * b + 4, :]
                        mm = pe.transpose(out, src, ident[:])
                mm.then_inc(turned, 1)
                pe.wait_ge(dve_own, 3 + GROUPS + 2 + GROUPS + 3 + GROUPS)
                for c in range(C):
                    pe.matmul(psum[:, c, :], pair[:, c % 2, :], lse[:, c // 2, :], start=True, stop=True).then_inc(spread_done, 1)

    split_operand(nc, lambda c: y[:, c, :], turned_x, C)

    def steps(c):
        return [lambda dve, bank: dve.tensor_tensor(gate_b[:, c, :], bank, gate_b[:, c, :], ALU.mult),
                lambda dve, bank: dve.tensor_tensor(merged[:, c, :], merged[:, c, :], gate_b[:, c, :], ALU.add)]

    channel_products(nc, psum, weights, turned_x[:, 0:C], KB, [("dve", steps(c)) for c in range(KD)])


def program(nc, a, out, first_only=False):
    with ExitStack() as ctx:
        def sb(name, shape):
            return ctx.enter_context(nc.sbuf_tensor(name, shape, F32))

        psum = ctx.enter_context(nc.psum_tensor("psum", [P, 8, 512], F32))
        x = sb("x_stream", [P, T, D])
        weights = WeightRing(nc, ctx)
        consts = constants(nc, sb, psum)
        with stage(nc, "x_landed other") as (x_landed, other), nc.Block() as block:
            @block.sync
            def _(sp):
                sp.dma_start(x[:], a["x"][0].rearrange("(t p) d -> p t d", p=P)).then_inc(x_landed, 16)
                sp.wait_ge(x_landed, 16)
        names = ("norm1 w_in mla_q_norm mla_kv_norm mla_w_uq mla_w_ukv swa_sinks fox_b_f w_out norm2 w_up "
                 "w_down").split()
        layers(nc, psum, x, weights, consts, *[a[n] for n in names])
        if not first_only:
            second_part(nc, psum, x, weights, consts, a)
        with stage(nc, "out_landed other") as (out_landed, other), nc.Block() as block:
            @block.sync
            def _(sp):
                sp.dma_start(out[0].rearrange("(t p) d -> p t d", p=P), x[:]).then_inc(out_landed, 16)
                sp.wait_ge(out_landed, 16)


_INS = ["x", "norm1", "w_in", "mla_q_norm", "mla_kv_norm", "mla_w_uq", "mla_w_ukv", "swa_sinks", "fox_b_f", "w_out",
        "norm2", "w_up", "w_down", "final_norm", "c_2", "norm_w_2", "ada_w_2", "ada_b_2", "w_in_2", "conv_w_2",
        "a_log_2", "dt_bias_2", "dn_norm_w_2", "w_proj_a_2", "w_proj_b_2", "w_out_2", "final_norm_w_2"]


def kernel(**inputs):
    import numpy as _np
    import concourse.bacc as _bacc
    from concourse import mybir as _mybir
    from concourse.bass_utils import run_bass_kernel_spmd as _run

    nc = _bacc.Bacc("TRN2", target_bir_lowering=False, num_devices=1)
    arrays, args = {}, {}
    for name in _INS:
        a = _np.ascontiguousarray(inputs[name])
        arrays[f"in_{name}_dram"] = a
        args[name] = nc.dram_tensor(f"in_{name}_dram", a.shape, _mybir.dt.from_np(a.dtype), kind="ExternalInput").ap()
    out = nc.dram_tensor("out_0_dram", (1, S, D), _mybir.dt.float32, kind="ExternalOutput").ap()
    program(nc, args, out)
    r = _run(nc, [arrays], core_ids=[0])
    return r.results[0]["out_0_dram"]
```
